# Optimizing a Trainium2 kernel written in Bass

```python
import jax, jax.numpy as jnp
from jax import lax
import numpy as np

D_MODEL = 1024
BATCH = 1
SEQ = 1024
DEPTH = 2

CONV_CH = 512
CONV_W = 3
MLA_HEADS = 8
QK_NOPE = 64
QK_ROPE = 32
V_DIM = 64
Q_RANK = 384
KV_RANK = 256
ROPE_THETA = 10000.0
ATTN_BLOCK = 128
EVEN_SPLITS = (CONV_CH, 2 * CONV_CH, 3 * CONV_CH, 3 * CONV_CH + Q_RANK, 3 * CONV_CH + Q_RANK + KV_RANK)
EVEN_IN = 3 * CONV_CH + Q_RANK + KV_RANK + QK_ROPE
EVEN_MIX = CONV_CH + MLA_HEADS * V_DIM
SG_WIDTH = 1024
SG_GROUPS = 8
SG_CHUNK = 128
N_GROUPS = 4
EXP_PER_GROUP = 8
N_EXPERTS = N_GROUPS * EXP_PER_GROUP
TOP_K = 2
D_EXPERT = 512
MOE_BLOCK = 128
PLE_DIM = 256
N_EVEN = (DEPTH + 1) // 2
N_ODD = DEPTH // 2
NORM_EPS = 1e-6
NEG_INF = -1e30

kernel_name = "hybrid_conv_mla_sgmlp_hmoe"

def rms_norm(x, g):
    x32 = x.astype(jnp.float32)
    y = x32 * lax.rsqrt(jnp.mean(x32 * x32, axis=-1, keepdims=True) + NORM_EPS)
    return y.astype(x.dtype) * g

def rope_angles(positions):
    inv_freq = 1.0 / (ROPE_THETA ** (jnp.arange(0, QK_ROPE, 2, dtype=jnp.float32) / QK_ROPE))
    ang = positions.astype(jnp.float32)[..., None] * inv_freq
    return jnp.cos(ang)[:, :, None, :], jnp.sin(ang)[:, :, None, :]

def apply_rope(x, cos, sin):
    half = x.shape[-1] // 2
    x1, x2 = x[..., :half], x[..., half:]
    c, s = cos.astype(x.dtype), sin.astype(x.dtype)
    return jnp.concatenate([x1 * c - x2 * s, x2 * c + x1 * s], axis=-1)

def causal_block_attention(q, k, v):
    B_, S_, H, Dqk = q.shape
    nb = S_ // ATTN_BLOCK
    scale = 1.0 / float(np.sqrt(Dqk))
    qb = q.reshape(B_, nb, ATTN_BLOCK, H, Dqk).transpose(1, 0, 2, 3, 4)
    key_idx = jnp.arange(S_)

    def attend(args):
        q_blk, blk = args
        s = jnp.einsum('bqhd,bkhd->bhqk', q_blk, k).astype(jnp.float32) * scale
        q_idx = blk * ATTN_BLOCK + jnp.arange(ATTN_BLOCK)
        s = jnp.where(key_idx[None, :] <= q_idx[:, None], s, NEG_INF)
        pr = jax.nn.softmax(s, axis=-1).astype(v.dtype)
        return jnp.einsum('bhqk,bkhd->bqhd', pr, v)

    o = lax.map(attend, (qb, jnp.arange(nb)))
    return o.transpose(1, 0, 2, 3, 4).reshape(B_, S_, H * v.shape[-1])

def conv_mla_mixer(hn, positions, w_in, conv_w, q_norm, w_q_up, kv_norm, w_kv_up, w_out):
    B_, S_, _ = hn.shape
    proj = hn @ w_in
    xc, gb, gc, c_q, c_kv, k_pe = jnp.split(proj, EVEN_SPLITS, axis=-1)
    z = gc * xc
    z = lax.conv_general_dilated(z, conv_w[:, None, :], window_strides=(1,),
                                 padding=[(CONV_W - 1, 0)],
                                 dimension_numbers=('NWC', 'WIO', 'NWC'),
                                 feature_group_count=CONV_CH)
    y_a = gb * z
    q = (rms_norm(c_q, q_norm) @ w_q_up).reshape(B_, S_, MLA_HEADS, QK_NOPE + QK_ROPE)
    kv = (rms_norm(c_kv, kv_norm) @ w_kv_up).reshape(B_, S_, MLA_HEADS, QK_NOPE + V_DIM)
    k_nope, v = kv[..., :QK_NOPE], kv[..., QK_NOPE:]
    cos, sin = rope_angles(positions)
    q_pe = apply_rope(q[..., QK_NOPE:], cos, sin)
    k_pe = apply_rope(k_pe[:, :, None, :], cos, sin)
    q = jnp.concatenate([q[..., :QK_NOPE], q_pe], axis=-1)
    k = jnp.concatenate([k_nope, jnp.broadcast_to(k_pe, (B_, S_, MLA_HEADS, QK_ROPE))], axis=-1)
    y_b = causal_block_attention(q, k, v)
    return jnp.concatenate([y_a, y_b], axis=-1) @ w_out

def spatial_gating_mixer(hn, w_in, v_norm, w_s, b_s, w_out):
    B_, S_, _ = hn.shape
    z = jax.nn.gelu(hn @ w_in)
    u, v = z[..., :SG_WIDTH], z[..., SG_WIDTH:]
    v = rms_norm(v, v_norm).reshape(B_, S_ // SG_CHUNK, SG_CHUNK, SG_GROUPS, SG_WIDTH // SG_GROUPS)
    w = jnp.tril(w_s)
    s = jnp.einsum('gts,bcsgd->bctgd', w, v) + b_s.T[:, :, None]
    return (u * s.reshape(B_, S_, SG_WIDTH)) @ w_out

def hierarchical_moe(h, w_rg, w_re, w_gate, w_up, w_down):
    B_, S_, D = h.shape
    T = B_ * S_
    xt = h.reshape(T, D)
    g_logits = (xt @ w_rg).astype(jnp.float32)
    g_prob = jax.nn.softmax(g_logits, axis=-1)
    g_idx = jnp.argmax(g_logits, axis=-1)
    g_w = jnp.take_along_axis(g_prob, g_idx[:, None], axis=-1)
    e_logits = (xt @ w_re).astype(jnp.float32).reshape(T, N_GROUPS, EXP_PER_GROUP)
    e_logits = jnp.take_along_axis(e_logits, g_idx[:, None, None], axis=1)[:, 0]
    top_p, top_i = lax.top_k(jax.nn.softmax(e_logits, axis=-1), TOP_K)
    top_p = top_p / jnp.sum(top_p, axis=-1, keepdims=True)
    weights = (g_w * top_p).reshape(-1)
    expert = (g_idx[:, None] * EXP_PER_GROUP + top_i).reshape(-1)
    tok = jnp.repeat(jnp.arange(T, dtype=jnp.int32), TOP_K)
    A = T * TOP_K
    order = jnp.argsort(expert)
    se = expert[order]
    counts = jnp.bincount(expert, length=N_EXPERTS)
    starts = jnp.cumsum(counts) - counts
    padded = ((counts + MOE_BLOCK - 1) // MOE_BLOCK) * MOE_BLOCK
    pend = jnp.cumsum(padded)
    pstarts = pend - padded
    dest = pstarts[se] + (jnp.arange(A) - starts[se])
    P = A + N_EXPERTS * MOE_BLOCK
    nblk = P // MOE_BLOCK
    buf_tok = jnp.full((P,), T, dtype=jnp.int32).at[dest].set(tok[order])
    buf_w = jnp.zeros((P,), dtype=jnp.float32).at[dest].set(weights[order])
    blk_e = jnp.minimum(jnp.searchsorted(pend, jnp.arange(nblk) * MOE_BLOCK, side='right'),
                        N_EXPERTS - 1)
    xpad = jnp.concatenate([xt, jnp.zeros((1, D), xt.dtype)], axis=0)
    xb = xpad[buf_tok].reshape(nblk, MOE_BLOCK, D)

    def expert_block(args):
        x_blk, e = args
        return (jax.nn.silu(x_blk @ w_gate[e]) * (x_blk @ w_up[e])) @ w_down[e]

    yb = lax.map(expert_block, (xb, blk_e)).reshape(P, D)
    yb = yb * buf_w[:, None].astype(yb.dtype)
    out = jax.ops.segment_sum(yb, buf_tok, num_segments=T + 1)[:T]
    return out.reshape(B_, S_, D)

def per_layer_embedding(h, p_i, g_norm, w_gate, w_proj):
    gate = jax.nn.sigmoid(rms_norm(h, g_norm) @ w_gate)
    return gate * (p_i @ w_proj)

def setup_inputs(seed: int = 0) -> dict:
    key = jax.random.key(seed)
    ks = jax.random.split(key, 32)
    f32 = jnp.float32

    def nrm(k, shape, fan_in):
        return jax.random.normal(k, shape, f32) * (fan_in ** -0.5)

    def gain(k, shape):
        return 1.0 + 0.02 * jax.random.normal(k, shape, f32)

    x = jax.random.normal(ks[0], (BATCH, SEQ, D_MODEL), f32)
    p = jax.random.normal(ks[1], (DEPTH, BATCH, SEQ, PLE_DIM), f32)
    positions = (jnp.arange(SEQ, dtype=jnp.int32)[None, :]
                 + jax.random.randint(ks[2], (BATCH, 1), 0, 1024, dtype=jnp.int32))
    return {
        'x': x,
        'p': p,
        'positions': positions,
        'norm_mix': gain(ks[3], (DEPTH, D_MODEL)),
        'norm_ffn': gain(ks[4], (DEPTH, D_MODEL)),
        'w_in_e': nrm(ks[5], (N_EVEN, D_MODEL, EVEN_IN), D_MODEL),
        'conv_w': nrm(ks[6], (N_EVEN, CONV_W, CONV_CH), CONV_W),
        'q_norm': gain(ks[7], (N_EVEN, Q_RANK)),
        'w_q_up': nrm(ks[8], (N_EVEN, Q_RANK, MLA_HEADS * (QK_NOPE + QK_ROPE)), Q_RANK),
        'kv_norm': gain(ks[9], (N_EVEN, KV_RANK)),
        'w_kv_up': nrm(ks[10], (N_EVEN, KV_RANK, MLA_HEADS * (QK_NOPE + V_DIM)), KV_RANK),
        'w_out_e': nrm(ks[11], (N_EVEN, EVEN_MIX, D_MODEL), EVEN_MIX),
        'w_in_o': nrm(ks[12], (N_ODD, D_MODEL, 2 * SG_WIDTH), D_MODEL),
        'v_norm': gain(ks[13], (N_ODD, SG_WIDTH)),
        'w_s': nrm(ks[14], (N_ODD, SG_GROUPS, SG_CHUNK, SG_CHUNK), SG_CHUNK),
        'b_s': 1.0 + 0.02 * jax.random.normal(ks[15], (N_ODD, SG_GROUPS, SG_CHUNK), f32),
        'w_out_o': nrm(ks[16], (N_ODD, SG_WIDTH, D_MODEL), SG_WIDTH),
        'w_router_group': nrm(ks[17], (DEPTH, D_MODEL, N_GROUPS), D_MODEL),
        'w_router_expert': nrm(ks[18], (DEPTH, D_MODEL, N_EXPERTS), D_MODEL),
        'w_gate': nrm(ks[19], (DEPTH, N_EXPERTS, D_MODEL, D_EXPERT), D_MODEL),
        'w_up': nrm(ks[20], (DEPTH, N_EXPERTS, D_MODEL, D_EXPERT), D_MODEL),
        'w_down': nrm(ks[21], (DEPTH, N_EXPERTS, D_EXPERT, D_MODEL), D_EXPERT),
        'norm_ple': gain(ks[22], (DEPTH, D_MODEL)),
        'w_ple_gate': nrm(ks[23], (DEPTH, D_MODEL, D_MODEL), D_MODEL),
        'w_ple_proj': nrm(ks[24], (DEPTH, PLE_DIM, D_MODEL), PLE_DIM),
        'final_norm': gain(ks[25], (D_MODEL,)),
    }

def reference(x, p, positions, norm_mix, norm_ffn, w_in_e, conv_w, q_norm, w_q_up, kv_norm,
              w_kv_up, w_out_e, w_in_o, v_norm, w_s, b_s, w_out_o, w_router_group,
              w_router_expert, w_gate, w_up, w_down, norm_ple, w_ple_gate, w_ple_proj,
              final_norm):
    h = x
    for i in range(DEPTH):
        hn = rms_norm(h, norm_mix[i])
        j = i // 2
        if i % 2 == 0:
            mix = conv_mla_mixer(hn, positions, w_in_e[j], conv_w[j], q_norm[j], w_q_up[j],
                                 kv_norm[j], w_kv_up[j], w_out_e[j])
        else:
            mix = spatial_gating_mixer(hn, w_in_o[j], v_norm[j], w_s[j], b_s[j], w_out_o[j])
        h = h + mix
        h = h + hierarchical_moe(rms_norm(h, norm_ffn[i]), w_router_group[i], w_router_expert[i],
                                 w_gate[i], w_up[i], w_down[i])
        h = h + per_layer_embedding(h, p[i], norm_ple[i], w_ple_gate[i], w_ple_proj[i])
    return rms_norm(h, final_norm)


_drawn_inputs = setup_inputs


def setup_inputs(seed=0):
    import zlib

    import numpy as np

    out = dict(_drawn_inputs(seed))
    spreads = {}
    factors = {'q_norm': 8.0,
     'kv_norm': 6.414,
     'v_norm': 35.781,
     'b_s': 25.74,
     'norm_ple': 61.344,
     'final_norm': 7.839,
     'norm_ffn': 6.494}
    for name, (base, spread) in spreads.items():
        noise = np.random.default_rng([zlib.crc32(name.encode()), seed]).standard_normal(out[name].shape)
        drawn = base * np.exp(spread * noise) if base else spread * noise
        out[name] = __import__('jax').numpy.asarray(drawn.astype(out[name].dtype))
    for name, factor in factors.items():
        out[name] = (out[name] * factor).astype(out[name].dtype)
    return out
```

```python
from contextlib import ExitStack

import numpy as np

import concourse.bass as bass
from concourse import mybir

F32 = mybir.dt.float32
F32R = mybir.dt.float32r
I32 = mybir.dt.int32
ALU = mybir.AluOpType
ACT = mybir.ActivationFunctionType
AXX = mybir.AxisListType.X

P = 128
D = 1024
T = 1024
NT = T // P
KD = D // P
DEPTH = 2
EPS = 1e-6
NEG = -1e30
CONV = 512
QR, KVR = 384, 256
H, NOPE, ROPE, VD = 8, 64, 32, 64
DQK = NOPE + ROPE
E, NG, EG, F = 32, 4, 8, 512
SG, SGG = 1024, 8
UNIT = 2048
RING = 6
SPLIT = 4
OVB = 2 * T // P - 1
NB = E + OVB
SCALE = float(DQK) ** -0.5
TWO_PI_HI, TWO_PI_LO = 6.28125, 0.0019353071795864769
PI = 3.141592653589793

C_QN, C_KVN, C_VN, C_CONV, C_ROPE = 0, 3, 5, 13, 25
N_COLS = C_ROPE + 2


class Tally:

    def __init__(self, sem):
        self.sem, self.base, self.k = sem, 0, 0

    def inc(self, ins, n=1):
        ins.then_inc(self.sem, n)
        self.k += n
        return self.value()

    def value(self):
        return self.base + self.k

    def link(self, eng, ins):
        eng.wait_ge(self.sem, self.inc(ins))

    def enter(self, i, per):
        self._start, self._per = self.value(), per
        self.base, self.k = i * per + self._start, 0

    def leave(self, turns):
        assert self.k == self._per, (self.k, self._per)
        self.base, self.k = self._start + turns * self._per, 0


class Count:

    def __init__(self, sem, base):
        self.sem, self.base = sem, base

    def __call__(self, n):
        return self.sem, n + self.base


def program(nc, A, out):
    with ExitStack() as ctx:
        names = {}

        def sem(name):
            assert name not in names, name
            names[name] = ctx.enter_context(nc.semaphore(name))
            return names[name]

        counts = {}

        def count(name, total):
            c, at = counts.get(name) or (sem(name), 0)
            counts[name] = c, at + total
            return Count(c, at)

        top = [(nc.sbuf_base + 63) // 64 * 64]

        def keep(name, shape, dt=F32):
            t = nc.alloc_sbuf_tensor_at(name, shape, dt, offset=top[0])
            top[0] += (int(np.prod(shape[1:])) * 4 + 31) // 32 * 32
            return t

        h = keep("h", [P, NT, D])
        ring = keep("ring", [P, RING, UNIT])
        ident = keep("ident", [P, P])
        ones = keep("ones", [P, P])
        before = keep("before", [P, P])
        causal = keep("causal", [P, P])
        cols = keep("cols", [P, N_COLS])
        wr = keep("wr", [P, KD, NG + E])
        ss = keep("ss", [P, NT])
        rstd = keep("rstd", [P, NT])
        eps_c = keep("eps_c", [P, 1])
        idx_tab = keep("idx_tab", [P, NB], I32)
        ov_e = keep("ov_e", [P, OVB + 1], I32)
        dest_i = keep("dest_i", [P, 2 * NT], I32)
        w_tok = keep("w_tok", [P, 2 * NT])
        fence = keep("fence", [P, 10])
        ARENA = top[0]

        class Arena:
            def __init__(self, tag):
                self.tag, self.at = tag, ARENA

            def __call__(self, name, shape, dt=F32):
                t = nc.alloc_sbuf_tensor_at(f"{self.tag}_{name}", shape, dt, offset=self.at)
                self.at += (int(np.prod(shape[1:])) * 4 + 31) // 32 * 32
                assert self.at <= nc.sbuf_usable_end if hasattr(nc, "sbuf_usable_end") else True
                return t

        banks = ctx.enter_context(nc.psum_tensor("banks", [P, 8 * 512], F32))

        def bank(b, n=1):
            return banks[:, b * 512:(b + n) * 512]

        xn_dram = nc.dram_tensor("xn_dram", (T, D), F32, kind="Internal").ap()
        y_dram = nc.dram_tensor("y_dram", (NB * P, D), F32, kind="Internal").ap()

        act_chain = Tally(sem("act_chain"))
        dve_chain = Tally(sem("dve_chain"))
        pool_chain = Tally(sem("pool_chain"))
        s_const = sem("s_const")
        s_load = sem("s_load")
        ring_full = [sem(f"ring_full{i}") for i in range(RING)]
        unit_pe = sem("unit_pe")
        unit_dve = sem("unit_dve")

        class Stream:

            def __init__(self):
                self.owner = []
                self.n_pe = self.n_dve = 0

            def dense(self, n):
                first = len(self.owner)
                for _ in range(n):
                    self.n_pe += 1
                    self.owner.append((unit_pe, self.n_pe))
                return first

            def expert(self, n):
                first = len(self.owner)
                for _ in range(n):
                    self.n_dve += 1
                    self.owner.append((unit_dve, self.n_dve))
                return first

            def wait_free(self, sp, u):
                if u >= RING:
                    sp.wait_ge(*self.owner[u - RING])

        stream = Stream()

        def full(eng, u):
            eng.wait_ge(ring_full[u % RING], 16 * (u // RING + 1))

        def load_unit(sp, u, src, n, parts=P):
            stream.wait_free(sp, u)
            sp.dma_start(ring[:, u % RING, 0:n], src).then_inc(ring_full[u % RING], 16)

        class NormTranspose:

            def __init__(self, tag, gain_row, xt, xn, gbc, h_ready, store=None):
                self.gain_row, self.xt, self.xn, self.gbc = gain_row, xt, xn, gbc
                self.h_ready, self.store = h_ready, store
                self.nbuf = xn.shape[1]
                self.s_g = count("norm_gain", 16)
                self.s_ss = count("norm_squares", NT)
                self.s_rms = count("norm_rms", 2)
                self.s_xn = count("norm_xn", NT)
                self.s_tr = count("norm_tr", 2 * NT)
                self.s_evA = count("norm_evA", NT)
                self.s_evD = count("norm_evD", NT)
                self.s_st = [count(f"norm_store{i}", 16 * NT // self.nbuf) for i in range(self.nbuf)] \
                    if store is not None else None
                self.done = [self.s_evA(NT), self.s_evD(NT)]

            def sp(self, sp):
                for s, v in self.h_ready:
                    sp.wait_ge(s, v)
                sp.dma_start(self.gbc[:], self.gain_row.partition_broadcast(P)).then_inc(self.s_g.sem, 16)

            def sp_store(self, sp):
                for t in range(NT):
                    sp.wait_ge(*self.s_xn(t + 1))
                    sp.dma_start(self.store[t * P:(t + 1) * P, :], self.xn[:, t % self.nbuf, :])\
                      .then_inc(self.s_st[t % self.nbuf].sem, 16)

            def act(self, act):
                for s, v in self.h_ready:
                    act.wait_ge(s, v)
                for t in range(NT):
                    act.activation(self.xt[:, t, :], h[:, t, :], ACT.Square,
                                   accum_out=ss[:, t:t + 1]).then_inc(self.s_ss.sem, 1)
                act.wait_ge(*self.s_rms(1))
                act.activation(rstd[:], rstd[:], ACT.Sqrt).then_inc(self.s_rms.sem, 1)
                for t in range(NT):
                    act.wait_ge(*self.s_tr(2 * t + 1))
                    act.activation(self.xt[:, 0:4, t * P:(t + 1) * P],
                                   bank(2 * (t % 2)).rearrange("p (k c) -> p k c", c=P),
                                   ACT.Copy).then_inc(self.s_evA.sem, 1)

            def dve(self, dve):
                dve.wait_ge(*self.s_ss(NT))
                dve.tensor_scalar(rstd[:], ss[:], 1.0 / D, EPS, ALU.mult, ALU.add).then_inc(self.s_rms.sem, 1)
                dve.wait_ge(*self.s_rms(2))
                dve_chain.link(dve, dve.reciprocal(rstd[:], rstd[:]))
                dve.wait_ge(*self.s_g(16))

                def scale(t):
                    b = t % self.nbuf
                    if t >= self.nbuf:
                        dve.wait_ge(*self.s_tr(2 * (t - self.nbuf + 1)))
                        if self.s_st:
                            dve.wait_ge(*self.s_st[b](16 * (t // self.nbuf)))
                    dve.scalar_tensor_tensor(self.xn[:, b, :], h[:, t, :], rstd[:, t:t + 1], self.gbc[:],
                                             ALU.mult, ALU.mult).then_inc(self.s_xn.sem, 1)

                scale(0)
                scale(1)
                for t in range(NT):
                    dve.wait_ge(*self.s_tr(2 * t + 2))
                    dve.tensor_copy(self.xt[:, 4:8, t * P:(t + 1) * P],
                                    bank(2 * (t % 2) + 1).rearrange("p (k c) -> p k c", c=P))\
                       .then_inc(self.s_evD.sem, 1)
                    if t + 2 < NT:
                        scale(t + 2)

            def pe(self, pe):
                for t in range(NT):
                    pe.wait_ge(*self.s_xn(t + 1))
                    for half in range(2):
                        if t >= 2:
                            pe.wait_ge(*(self.s_evA, self.s_evD)[half](t - 1))
                        for k in range(4):
                            ins = pe.transpose(bank(2 * (t % 2) + half)[:, k * P:(k + 1) * P],
                                               self.xn[:, t % self.nbuf, (4 * half + k) * P:(4 * half + k + 1) * P],
                                               ident[:])
                        ins.then_inc(self.s_tr.sem, 1)

        class TokenMajor:

            def __init__(self, tag, xt, panels, kd, width, first_bank=4, nbanks=4):
                self.xt, self.panels, self.kd, self.width = xt, panels, kd, width
                self.units = [stream.dense(2) for _ in panels]
                self.b0, self.nb = first_bank, nbanks
                self.n = len(panels) * NT
                self.s_mm = count("out_mm", self.n)
                self.s_take = count("out_take", self.n)

            def sp(self, sp):
                for u, src in zip(self.units, self.panels):
                    for half in range(2):
                        load_unit(sp, u + half, src[:, half * UNIT:(half + 1) * UNIT], UNIT)

            def pe(self, pe, ready):
                for s, v in ready:
                    pe.wait_ge(s, v)
                for c, u in enumerate(self.units):
                    for t in range(NT):
                        g = c * NT + t
                        if g >= self.nb:
                            pe.wait_ge(*self.s_take(g - self.nb + 1))
                        for k in range(self.kd):
                            if t == 0 and k % 4 == 0:
                                full(pe, u + k // 4)
                            w = ring[:, (u + k // 4) % RING, (k % 4) * 512:(k % 4 + 1) * 512]
                            ins = pe.matmul(bank(self.b0 + g % self.nb), self.xt[:, k, t * P:(t + 1) * P], w,
                                            start=(k == 0), stop=(k == self.kd - 1))
                        ins.then_inc(self.s_mm.sem, 1)

            def bank_of(self, g):
                return bank(self.b0 + g % self.nb)

        def setup_sp(sp):
            sp.dma_start(h[:], A["x"].rearrange("(t p) d -> p t d", p=P)).then_inc(s_load, 16)
            sp.dma_start(cols[:], A["cols"]).then_inc(s_load, 16)

        def setup_pool(pool):
            pool.memset(ident[:], 0.0).then_inc(pool_chain.sem, 1)
            pool.memset(ones[:], 1.0).then_inc(pool_chain.sem, 1)
            pool.memset(before[:], 1.0).then_inc(pool_chain.sem, 1)
            pool.memset(causal[:], 0.0).then_inc(pool_chain.sem, 1)
            pool.memset(fence[:], 0.0).then_inc(pool_chain.sem, 1)
            pool.memset(eps_c[:], EPS).then_inc(pool_chain.sem, 1)
            pool_chain.k += 6
            pool.wait_ge(pool_chain.sem, 6)
            pool.affine_select(out=ident[:], in_=ident[:], compare_op=ALU.not_equal, fill=1.0, base=0,
                               pattern=[[-1, P]], channel_multiplier=1).then_inc(s_const, 1)
            pool.affine_select(out=before[:], in_=before[:], compare_op=ALU.is_gt, fill=0.0, base=0,
                               pattern=[[1, P]], channel_multiplier=-1).then_inc(s_const, 1)
            pool.affine_select(out=causal[:], in_=causal[:], compare_op=ALU.is_ge, fill=NEG, base=0,
                               pattern=[[-1, P]], channel_multiplier=1).then_inc(s_const, 1)

        CONSTS = [(s_const, 3)]
        LOADS = [(s_load, 32)]

        a0 = Arena("mix0")
        xt0 = a0("xt", [P, KD, T])
        yt0 = a0("yt", [P, KD, T])
        cq = a0("cq", [P, 3, T])
        ckv = a0("ckv", [P, 2, T])
        trig = a0("trig", [P, 2, T])
        qk = a0("qk", [P, 4, T])
        rt = a0("rt", [P, 2, T])
        wh = a0("wh", [P, 2, 3 * DQK + 2 * NOPE])
        lrow = a0("lrow", [P, 3 * NT])
        gbc0 = rt[:, 0, :]
        ytok = xt0[:, 0:4, :].rearrange("p a b -> p (a b)").rearrange("p (t c) -> p t c", c=H * VD)
        pt = xt0[:, 4:6, :]
        vals = [z[:, 6:8, :].rearrange("p a b -> p (a b)").rearrange("p (t c) -> p t c", c=H * VD)
                for z in (xt0, yt0)]
        prob = yt0[:, 4:6, :]
        posi = yt0[:, 0, :].bitcast(I32)
        ZB, AB, GB = yt0[:, 4, :], yt0[:, 5, :], yt0[:, 6, :]
        REG = slice(64, 96)

        norm0 = NormTranspose("n0", A["norm_mix"][0:1, :], xt0, qk, gbc0, [])
        norm0.h_ready = LOADS

        IN_W = [3 * P, KVR + ROPE] + [3 * P] * 4
        in_units = [stream.dense(2) for _ in IN_W]
        wv_unit = stream.dense(1)
        s_in = sem("s_in")
        s_in_a = sem("s_in_a")
        s_in_d = sem("s_in_d")
        s_trig = sem("s_trig")
        s_zero = sem("s_zero")
        s_pos = sem("s_pos")
        s_sq = sem("s_sq")
        s_latn = sem("s_latn")
        s_wh = [sem("s_wh0"), sem("s_wh1")]
        s_v = sem("s_v")
        s_va, s_vd = sem("s_va"), sem("s_vd")
        s_proj = sem("s_proj")
        s_qkv = sem("s_qkv")
        s_rope = sem("s_rope")
        s_sc = sem("s_sc")
        s_max = sem("s_max")
        s_exp = sem("s_exp")
        s_ptr = sem("s_ptr")
        s_pta = sem("s_pta")
        s_ptd = sem("s_ptd")
        s_pv = sem("s_pv")
        s_o = sem("s_o")
        s_yt = sem("s_yt")
        s_yte = sem("s_yte")

        def in_sp(sp):
            sp.dma_start(posi[REG, :], A["positions"].partition_broadcast(32)).then_inc(s_pos, 16)
            for n, (u, w) in enumerate(zip(in_units, IN_W)):
                src = A["w_in_kv"] if n == 1 else A["w_in_e"][4 if n == 0 else n - 2]
                for half in range(2):
                    load_unit(sp, u + half, src[:, half * 4 * w:(half + 1) * 4 * w], 4 * w)
                if n == 1:
                    for b in range(2):
                        sp.dma_start(wh[:, b, :], A["w_heads"][b]).then_inc(s_wh[b], 16)
            load_unit(sp, wv_unit, A["w_v"], 2 * H * VD)

        GROUPS = []
        for n in range(6):
            GROUPS += [("in", n, b, hf) for b in range(3) for hf in range(2)]
            if n == 2:
                GROUPS += [("sq", m, hf) for m in range(2) for hf in range(2)]
            if n == 3:
                GROUPS += [("head", m, hf) for m in range(2) for hf in range(2)]

        def place(*group):
            return GROUPS.index(group)

        reader, a_read, d_read = {}, 0, 0
        for g, group in enumerate(GROUPS):
            if group[0] == "in" and group[1] >= 2 and group[2] < 2:
                d_read += 1
                reader[g] = (s_in_d, d_read)
            else:
                a_read += 1
                reader[g] = (s_in_a, a_read)

        LAT = [(cq, 3, QR, C_QN, [qk[:, 0, :], qk[:, 1, :], qk[:, 2, :]]),
               (ckv, 2, KVR, C_KVN, [qk[:, 3, :], yt0[:, 7, :]])]
        WQ = 3 * DQK

        def head_product(pe, dst, m, hf, b):
            rank, nk, first, step, w = ((cq, 3, 0, DQK, DQK), (ckv, 2, WQ, NOPE, NOPE))[m]
            for k in range(nk):
                ins = pe.matmul(dst[0:w, :], wh[:, b, first + k * step:first + k * step + w],
                                rank[:, k, hf * 512:(hf + 1) * 512], start=(k == 0), stop=(k == nk - 1))
            return ins

        def head_copy(act, src, m, hf, b):
            sl = slice(hf * 512, (hf + 1) * 512)
            if m == 0:
                return act.activation(qk[0:DQK, b, sl], src[0:DQK, :], ACT.Copy, scale=SCALE)
            return act.activation(qk[0:NOPE, 2 + b, sl], src[0:NOPE, :], ACT.Copy)

        def in_pe(pe):
            for s, v in norm0.done:
                pe.wait_ge(s, v)
            for g, group in enumerate(GROUPS):
                if g >= 8:
                    pe.wait_ge(*reader[g - 8])
                if group[0] == "in":
                    n, b, hf = group[1:]
                    u, w = in_units[n], IN_W[n]
                    m = ROPE if (n, b) == (1, 2) else P
                    po = 64 if m == ROPE else 0
                    for k in range(KD):
                        if b == 0 and hf == 0 and k % 4 == 0:
                            full(pe, u + k // 4)
                        lhs = ring[:, (u + k // 4) % RING, (k % 4) * w + b * P:(k % 4) * w + b * P + m]
                        ins = pe.matmul(bank(g % 8)[po:po + m, :], lhs, xt0[:, k, hf * 512:(hf + 1) * 512],
                                        start=(k == 0), stop=(k == KD - 1))
                elif group[0] == "sq":
                    m, hf = group[1:]
                    pe.wait_ge(s_sq, 5)
                    squares = LAT[m][4]
                    for k, src in enumerate(squares):
                        ins = pe.matmul(bank(g % 8), ones[:], src[:, hf * 512:(hf + 1) * 512],
                                        start=(k == 0), stop=(k == len(squares) - 1))
                else:
                    m, hf = group[1:]
                    pe.wait_ge(s_latn, 5)
                    pe.wait_ge(s_wh[0], 16)
                    ins = head_product(pe, bank(g % 8), m, hf, 0)
                ins.then_inc(s_in, 1)
                if group[0] == "in" and group[2:] == (2, 1):
                    pe.wait_ge(s_in, g + 1)
                    pe.nop().then_inc(unit_pe, 2)

        def zero_pool(pool):
            pool.memset(yt0[:, 3, :], 0.0).then_inc(s_const, 1)

        def zero_sp(sp):
            sp.wait_ge(s_const, 4)
            for b in range(OVB):
                sp.dma_start(y_dram[(E + b) * P:(E + b + 1) * P, :], yt0[:, 3, :]).then_inc(s_zero, 16)

        def in_act(act):
            for g, group in enumerate(GROUPS):
                if g in reader and reader[g][0] is s_in_d:
                    continue
                hf = group[-1]
                sl = slice(hf * 512, (hf + 1) * 512)
                src = bank(g % 8)
                if group[0] == "in":
                    n, b = group[1:3]
                    act.wait_ge(s_in, g + 1)
                    if n == 0:
                        dst = cq[:, b, sl]
                    elif n == 1:
                        dst, src = (ckv[:, b, sl], src) if b < 2 else (rt[REG, 0, sl], src[REG, :])
                    else:
                        if n > 2 and hf == 0:
                            act.wait_ge(s_in_d, 4 * (n - 2) - 2)
                        dst = GB[:, sl]
                    ins = act.activation(dst, src, ACT.Copy)
                elif group[0] == "sq":
                    m = group[1]
                    act.wait_ge(s_in, place("sq", m, 1) + 1)
                    ins = act.activation(qk[:, m, sl], src, ACT.Sqrt, scale=1.0 / LAT[m][2], bias=eps_c[:])
                else:
                    act.wait_ge(s_in, g + 1)
                    ins = head_copy(act, src, group[1], hf, 0)
                ins.then_inc(s_in_a, 1)
                if group == ("in", 0, 2, 1):
                    trig_act(act)
                if group == ("in", 1, 2, 1):
                    act.wait_ge(*reader[g])
                    for c, nk, _, _, squares in LAT:
                        for k in range(nk):
                            act.activation(squares[k], c[:, k, :], ACT.Square).then_inc(s_sq, 1)

        def conv_dve(dve, n):
            wc = C_CONV + 3 * n
            dve.wait_ge(*reader[place("in", 2 + n, 2, 1)])
            for hf in range(2):
                sl = slice(hf * 512, (hf + 1) * 512)
                dve.tensor_tensor(ZB[:, sl], bank(place("in", 2 + n, 0, hf) % 8), GB[:, sl],
                                  ALU.mult).then_inc(s_in_d, 1)
            dve.wait_ge(s_in_d, 4 * n + 2)
            L = dve_chain.link
            L(dve, dve.tensor_scalar(AB[:, :], ZB[:, :], cols[:, wc + 2:wc + 3], None, ALU.mult))
            L(dve, dve.scalar_tensor_tensor(AB[:, 1:T], ZB[:, 0:T - 1], cols[:, wc + 1:wc + 2],
                                            AB[:, 1:T], ALU.mult, ALU.add))
            L(dve, dve.scalar_tensor_tensor(AB[:, 2:T], ZB[:, 0:T - 2], cols[:, wc:wc + 1],
                                            AB[:, 2:T], ALU.mult, ALU.add))
            if n == 3:
                dve.wait_ge(s_zero, 16 * OVB)
            for hf in range(2):
                sl = slice(hf * 512, (hf + 1) * 512)
                dve.tensor_tensor(yt0[:, n, sl], bank(place("in", 2 + n, 1, hf) % 8), AB[:, sl],
                                  ALU.mult).then_inc(s_in_d, 1)

        def trig_dve(dve):
            ang, k_i, kf, w1 = rt[REG, 1, :], yt0[REG, 1, :].bitcast(I32), trig[REG, 1, :], trig[REG, 0, :]
            L = dve_chain.link
            dve.wait_ge(s_pos, 16)
            L(dve, dve.tensor_copy(w1, posi[REG, :]))
            L(dve, dve.tensor_scalar(ang, w1, cols[REG, C_ROPE:C_ROPE + 1], None, ALU.mult))
            L(dve, dve.tensor_scalar(w1, ang, 1.0 / (2 * PI), None, ALU.mult))
            L(dve, dve.tensor_copy(k_i, w1))
            L(dve, dve.tensor_copy(kf, k_i))
            L(dve, dve.scalar_tensor_tensor(ang, kf, -TWO_PI_HI, ang, ALU.mult, ALU.add))
            L(dve, dve.scalar_tensor_tensor(ang, kf, -TWO_PI_LO, ang, ALU.mult, ALU.add))

            def wrap(x, tmp):
                L(dve, dve.tensor_scalar(tmp, x, PI, -2 * PI, ALU.is_gt, ALU.mult))
                L(dve, dve.tensor_tensor(x, x, tmp, ALU.add))
                L(dve, dve.tensor_scalar(tmp, x, -PI, 2 * PI, ALU.is_lt, ALU.mult))
                L(dve, dve.tensor_tensor(x, x, tmp, ALU.add))

            wrap(ang, kf)
            L(dve, dve.tensor_scalar(w1, ang, PI / 2, None, ALU.add))
            wrap(w1, kf)
            L(dve, dve.tensor_scalar(w1, w1, 3.1415925, -3.1415925, ALU.min, ALU.max))
            dve.tensor_scalar(ang, ang, 3.1415925, -3.1415925, ALU.min, ALU.max).then_inc(s_trig, 1)

        def trig_act(act):
            act.wait_ge(s_trig, 1)
            act.activation(trig[REG, 0, :], trig[REG, 0, :], ACT.Sin).then_inc(s_trig, 1)
            act.activation(trig[REG, 1, :], rt[REG, 1, :], ACT.Sin).then_inc(s_trig, 1)

        def latent_dve(dve):
            for m, (c, nk, _, col, _) in enumerate(LAT):
                dve.wait_ge(*reader[place("sq", m, 1)])
                dve_chain.link(dve, dve.reciprocal(qk[:, m, :], qk[:, m, :]))
                for k in range(nk):
                    dve.scalar_tensor_tensor(c[:, k, :], c[:, k, :], cols[:, col + k:col + k + 1],
                                             qk[:, m, :], ALU.mult, ALU.mult).then_inc(s_latn, 1)
            L = dve_chain.link
            dve.wait_ge(s_trig, 3)
            L(dve, dve.tensor_scalar(trig[REG, 1, :], trig[REG, 1, :], cols[REG, C_ROPE + 1:C_ROPE + 2], None,
                                     ALU.mult))
            L(dve, dve.stream_shuffle(rt[REG, 1, :], rt[REG, 0, :], [(j + 16) % 32 for j in range(32)]))
            L(dve, dve.tensor_tensor(rt[REG, 1, :], rt[REG, 1, :], trig[REG, 1, :], ALU.mult))
            L(dve, dve.tensor_tensor(rt[REG, 0, :], rt[REG, 0, :], trig[REG, 0, :], ALU.mult))
            dve.tensor_tensor(qk[REG, 2, :], rt[REG, 0, :], rt[REG, 1, :], ALU.add).then_inc(s_rope, 1)
            dve.tensor_tensor(qk[REG, 3, :], rt[REG, 0, :], rt[REG, 1, :], ALU.add).then_inc(s_rope, 1)
            dve.wait_ge(s_rope, 2)

        def rope_step(dve, b, n):
            if n == 0:
                ins = dve.tensor_tensor(rt[REG, 0, :], qk[REG, b, :], trig[REG, 0, :], ALU.mult)
            elif n == 1:
                ins = dve.stream_shuffle(rt[REG, 1, :], qk[REG, b, :], [(j + 16) % 32 for j in range(32)])
            elif n == 2:
                ins = dve.tensor_tensor(rt[REG, 1, :], rt[REG, 1, :], trig[REG, 1, :], ALU.mult)
            else:
                dve.tensor_tensor(qk[REG, b, :], rt[REG, 0, :], rt[REG, 1, :], ALU.add).then_inc(s_rope, 1)
                return
            dve_chain.link(dve, ins)

        def in_dve(dve):
            trig_dve(dve)
            conv_dve(dve, 0)
            latent_dve(dve)
            conv_dve(dve, 1)
            dve.wait_ge(*reader[place("head", 0, 1)])
            for n in range(4):
                rope_step(dve, 0, n)
            conv_dve(dve, 2)
            conv_dve(dve, 3)

        def values_pe(pe):
            full(pe, wv_unit)
            for t in range(NT):
                if t < 4:
                    for g in range(len(GROUPS) - 8, len(GROUPS)):
                        if g % 8 == t:
                            pe.wait_ge(*reader[g])
                else:
                    pe.wait_ge((s_va, s_vd)[t % 2], (t - 4) // 2 + 1)
                for k in range(2):
                    ins = pe.matmul(bank(t % 4), ckv[:, k, t * P:(t + 1) * P],
                                    ring[:, wv_unit % RING, k * 512:(k + 1) * 512], start=(k == 0), stop=(k == 1))
                ins.then_inc(s_v, 1)
            for g in range(len(GROUPS) - 8, len(GROUPS)):
                pe.wait_ge(*reader[g])
            pe.wait_ge(s_v, NT)
            pe.nop().then_inc(unit_pe, 1)

        def values_out(eng, write, parity, s_done):
            eng.wait_ge(s_in_d, d_read)
            for t in range(parity, NT, 2):
                eng.wait_ge(s_v, t + 1)
                write(vals[t // 4][:, t % 4, :], bank(t % 4)).then_inc(s_done, 1)

        FILL = (1, 1, 1, 3)
        TURNS = H // 2
        STEPS = 2 * NT

        def ahead(eng, *sems):
            for s in sems:
                eng.nop().then_inc(s, 1)

        PT_GROUPS = []
        for n in range(STEPS):
            for j0 in range(0, n % NT + 1, 4):
                PT_GROUPS.append((n, j0, min(4, n % NT + 1 - j0), len(PT_GROUPS)))
        GT = len(PT_GROUPS)

        def groups_through(n):
            return sum(1 for x in PT_GROUPS if x[0] <= n)

        def turns(eng, turn):
            with eng.Fori(0, TURNS - 1) as i:
                turn(i, False)
            turn(TURNS - 1, True)

        def att_sp(sp):
            sp.wait_ge(s_in, place("head", 1, 1) + 1)
            sp.dma_start(wh[:, 0, :], A["w_heads"][2]).then_inc(s_wh[0], 16)
            with sp.Fori(0, TURNS - 2) as i:
                for u in range(2):
                    sp.wait_ge(s_proj, 8 * i + (4 * u + 4))
                    sp.dma_start(wh[:, 1 - u, :], A["w_heads"][bass.ds(2 * i + (u + 3), 1)]
                                 .rearrange("a p c -> (a p) c")).then_inc(s_wh[1 - u], 16)
            sp.wait_ge(s_proj, 8 * (TURNS - 2) + 4)
            sp.dma_start(wh[:, 1, :], A["w_heads"][H - 1]).then_inc(s_wh[1], 16)

        def att_pe(pe):
            ahead(pe, s_ptr, s_pv)

            def scores(i, n, last=False):
                u, b = n // NT % 2, n % NT
                if b in (4, 5) and not (last and u == 1):
                    pe.wait_ge(s_qkv, 8 * i + (4 * u + b))
                if n >= 1:
                    pe.wait_ge(s_exp, STEPS * i + (n - 1 + 1))
                if b == 0 and n > 0:
                    pe.wait_ge(s_qkv, 8 * i + (4 * (n // NT) + 1))
                    pe.wait_ge(s_rope, 2 * i + (n // NT + 3))
                for c in range(0, (b + 1) * P, 512):
                    w = min(512, (b + 1) * P - c)
                    dst = bank(2 * (n % 2), 2)[:, c:c + w]
                    last = c + w == (b + 1) * P
                    ins = pe.matmul(dst, qk[0:DQK, u, b * P:(b + 1) * P], qk[0:DQK, 2 + u, c:c + w],
                                    start=True, stop=not last)
                pe.matmul(dst[:, w - P:w], ident[:], causal[:], start=False, stop=True).then_inc(s_sc, 1)

            def turn(i, last):
                for n in range(STEPS):
                    u, b = n // NT, n % NT
                    if not (last and n + 1 == STEPS):
                        scores(i, n + 1, last)
                    if b < 4 and not (last and u == 1):
                        if b == 0:
                            pe.wait_ge(s_wh[1 - u], 16 * i + 16 * (1 + u))
                        pe.wait_ge(s_qkv, 8 * i + (4 * u + b + 1))
                        head_product(pe, bank(FILL[b]), b // 2, b % 2, 1 - u).then_inc(s_proj, 1)
                    pe.wait_ge(s_exp, STEPS * i + (n + 2))
                    for nn, j0, cnt, g in PT_GROUPS:
                        if nn == n:
                            pe.wait_ge((s_pta, s_ptd)[g % 2], GT // 2 * i + (g // 2 + 1))
                            for j in range(j0, j0 + cnt):
                                ins = pe.transpose(bank(4 + g % 2)[:, (j - j0) * P:(j - j0 + 1) * P],
                                                   prob[:, n % 2, j * P:(j + 1) * P], ident[:])
                            ins.then_inc(s_ptr, 1)
                    if n >= 1:
                        weigh(i, n - 1)
                weigh(i, STEPS - 1)

            def weigh(i, n):
                u, b = n // NT, n % NT
                for nn, _, _, g in PT_GROUPS:
                    if nn == n:
                        pe.wait_ge((s_pta, s_ptd)[g % 2], GT // 2 * i + (g // 2 + 2))
                pe.wait_ge(s_o, STEPS * i + max(n, 1))
                for j in range(b + 1):
                    ins = pe.matmul(bank(6 + n % 2)[:, 0:VD], pt[:, n % 2, j * P:(j + 1) * P],
                                    vals[j // 4][:, j % 4, bass.ds(2 * VD * i + VD * u, VD)],
                                    start=(j == 0), stop=(j == b))
                ins.then_inc(s_pv, 1)

            pe.wait_ge(*reader[place("head", 1, 1)])
            pe.wait_ge(s_rope, 3)
            pe.wait_ge(s_va, NT // 2)
            pe.wait_ge(s_vd, NT // 2)
            scores(0, 0)
            turns(pe, turn)

        def pt_out(eng, write, parity, s_done, i, n):
            for nn, j0, cnt, g in PT_GROUPS:
                if nn == n and g % 2 == parity:
                    eng.wait_ge(s_ptr, GT * i + (g + 2))
                    eng.wait_ge(s_pv, STEPS * i + (max(n - 1, 0) + 1))
                    write(pt[:, n % 2, j0 * P:(j0 + cnt) * P], bank(4 + g % 2)[:, 0:cnt * P]).then_inc(s_done, 1)

        def att_act(act):
            ahead(act, s_qkv, s_exp, s_pta)

            def exps(i, n):
                act.wait_ge(s_max, STEPS * i + (n + 1))
                if n >= 1:
                    act.wait_ge(s_ptr, GT * i + (groups_through(n - 2) + 1))
                u, b = n // NT % 2, n % NT
                w = (b + 1) * P
                act.activation(prob[:, n % 2, 0:w], bank(2 * (n % 2), 2)[:, 0:w], ACT.Exp,
                               bias=lrow[:, 2 * NT + b:2 * NT + b + 1],
                               accum_out=lrow[:, u * NT + b:u * NT + b + 1]).then_inc(s_exp, 1)

            def turn(i, last):
                for n in range(STEPS):
                    u, b = n // NT, n % NT
                    if not (last and n + 1 == STEPS):
                        exps(i, n + 1)
                    pt_out(act, lambda o, x: act.activation(o, x, ACT.Copy), 0, s_pta, i, n)
                    if b < 4 and not (last and u == 1):
                        act.wait_ge(s_proj, 8 * i + (4 * u + b + 1))
                        head_copy(act, bank(FILL[b]), b // 2, b % 2, 1 - u).then_inc(s_qkv, 1)

            exps(0, 0)
            turns(act, turn)

        def att_dve(dve):
            ahead(dve, s_ptd, s_o)
            L = dve_chain.link

            def row_max(i, n):
                b = n % NT
                dve.wait_ge(s_sc, STEPS * i + (n + 1))
                dve.tensor_reduce(lrow[:, 2 * NT + b:2 * NT + b + 1], bank(2 * (n % 2), 2)[:, 0:(b + 1) * P],
                                  axis=AXX, op=ALU.max, negate=True).then_inc(s_max, 1)

            def norm_out(i, n):
                u, b = n // NT, n % NT
                total = lrow[:, u * NT + b:u * NT + b + 1]
                L(dve, dve.reciprocal(total, total))
                dve.wait_ge(s_pv, STEPS * i + (n + 2))
                dve.tensor_scalar(ytok[:, b, bass.ds(2 * VD * i + VD * u, VD)], bank(6 + n % 2)[:, 0:VD],
                                  total, None, ALU.mult).then_inc(s_o, 1)

            def turn(i, last):
                for n in range(STEPS):
                    u, b = n // NT, n % NT
                    if not (last and n + 1 == STEPS):
                        row_max(i, n + 1)
                    pt_out(dve, dve.tensor_copy, 1, s_ptd, i, n)
                    if 3 <= b < 7 and not (last and u == 1):
                        if b == 3:
                            dve.wait_ge(s_qkv, 8 * i + (4 * u + 3))
                        rope_step(dve, 1 - u, b - 3)
                    if n >= 1:
                        norm_out(i, n - 1)
                norm_out(i, STEPS - 1)

            row_max(0, 0)
            with dve.Fori(0, TURNS - 1) as i:
                dve_chain.enter(i, 2 * 3 + STEPS)
                turn(i, False)
            dve_chain.leave(TURNS - 1)
            turn(TURNS - 1, True)

        def yt_pe(pe):
            pe.wait_ge(s_o, 1 + H * NT)
            for t in range(NT):
                if t >= 2:
                    pe.wait_ge(s_yte, t - 1)
                for k in range(4):
                    ins = pe.transpose(bank(t % 2)[:, k * P:(k + 1) * P], ytok[:, t, k * P:(k + 1) * P], ident[:])
                ins.then_inc(s_yt, 1)

        def yt_act(act):
            for t in range(NT):
                act.wait_ge(s_yt, t + 1)
                act.activation(yt0[:, 4:8, t * P:(t + 1) * P], bank(t % 2).rearrange("p (k c) -> p k c", c=P),
                               ACT.Copy).then_inc(s_yte, 1)

        class OutProj:

            def __init__(self, tag, xt, w, ready):
                self.g = TokenMajor(tag, xt, [w[c] for c in range(2)], KD, 512)
                self.ready = ready
                self.done = [self.g.s_take(self.g.n)]

            def sp(self, sp):
                self.g.sp(sp)

            def pe(self, pe):
                self.g.pe(pe, self.ready)
                pe.wait_ge(*self.g.s_mm(self.g.n))
                pe.nop().then_inc(unit_pe, 4)

            def dve(self, dve):
                for n in range(self.g.n):
                    c, t = divmod(n, NT)
                    dve.wait_ge(*self.g.s_mm(n + 1))
                    dve.tensor_tensor(h[:, t, c * 512:(c + 1) * 512], h[:, t, c * 512:(c + 1) * 512],
                                      self.g.bank_of(n), ALU.add).then_inc(self.g.s_take.sem, 1)

        out0 = OutProj("out0", yt0, A["w_out_e"], [(s_yte, NT)])

        class Moe:

            def __init__(self, l, h_ready):
                self.l = l
                tag = self.tag = f"m{l}_"
                a = Arena(tag)
                self.hi = a("hi", [P, SPLIT, UNIT], F32R)
                self.lo = a("lo", [P, SPLIT, UNIT], F32R)
                self.xg = a("xg", [P, 2, D])
                self.xh = a("xh", [P, 2, D], F32R)
                self.xl = a("xl", [P, 2, D], F32R)
                self.sg = a("sg", [P, F])
                self.hm = a("hm", [P, F])
                self.hh = a("hh", [P, F], F32R)
                self.hl = a("hl", [P, F], F32R)
                self.y = a("y", [P, 2, D])
                self.xf = a("xf", [P, D])
                self.hf = a("hf", [P, F])
                self.ovi = a("ovi", [P, 1], I32)
                b = Arena(tag + "r")
                self.xt = b("xt", [P, KD, T])
                self.xn = b("xn", [P, 4, D])
                self.gbc = b("gbc", [P, D])
                self.lg = b("lg", [P, NT, NG + E])
                self.oh = [b(f"oh{k}", [P, NT, E]) for k in range(2)]
                self.em = b("em", [P, NT, E])
                self.tmp = b("tmp", [P, NT, E])
                self.both = b("both", [P, NT, E])
                self.small = b("small", [P, 24, NT])
                self.row = b("row", [P, 8, E])
                self.iog = b("iog", [P, NG])
                self.ioe = b("ioe", [P, E])
                self.iox = b("iox", [P, E])
                self.iob = b("iob", [P, NB])
                self.ios = b("ios", [P, P])
                self.tok = b("tok", [P, NT])
                self.q_s = b("q_s", [P, 2 * NT, P])
                self.q_b = b("q_b", [P, 2 * NT, NB])
                self.ovc = b("ovc", [P, OVB, E])
                self.ovf = b("ovf", [P, OVB + 1])
                c = Arena(tag + "c")
                self.rows = c("rows", [P, 8, D])
                self.norm = NormTranspose(tag + "n", A["norm_ffn"][l:l + 1, :], self.xt, self.xn, self.gbc,
                                          h_ready, store=xn_dram)
                def S(n, total):
                    return count("moe_" + n, total)

                self.s_io, self.s_wr, self.s_lg = S("iota", 6), S("w_router", 16), S("logits", 1)
                self.s_exd, self.s_ex = S("exp_in", 2), S("exp", 2)
                self.s_A, self.s_rk, self.s_q = S("chosen", 1), S("ranks", 1), S("one_hots", 1)
                self.s_tab, self.s_rt = S("table", 1), S("routed", 1)
                self.s_gx = [S("gathered0", 8 * E), S("gathered1", 8 * E)]
                self.s_yst = [S("stored0", 8 * E), S("stored1", 8 * E)]
                self.s_xtr, self.s_xh, self.s_xl = S("x_transposed", E), S("x_hi", E), S("x_lo", E)
                self.s_hi, self.s_use = S("w_hi", 6 * E), S("w_used", 6 * E)
                self.s_sg, self.s_hm = S("silu", E), S("hidden", E)
                self.s_htr, self.s_hh, self.s_hl = S("h_transposed", E), S("h_hi", E), S("h_lo", E)
                self.s_ya, self.s_yd = S("y_act", E), S("y_dve", E)
                self.s_of, self.s_ow, self.s_oi, self.s_ox, self.s_op, self.s_oa, self.s_od, self.s_oy = (
                    Count(sem(f"beyond{l}_{n}"), 0)
                    for n in ("free", "weights", "index", "gathered", "pe", "act", "dve", "stored"))
                self.s_odone = S("beyond_done", 1)
                self.s_row = [S(f"row{i}", 32) for i in range(8)]
                self.s_comb = S("combined", 2 * NT)
                self.first = stream.expert(6 * E)
                self.done = [self.s_comb(2 * NT)]

            def iotas(self, pool):
                pool.wait_ge(*self.norm.s_xn(1))
                kw = dict(allow_small_or_imprecise_dtypes=True)
                for tile, pat, base, cm in ((self.iog, [[-1, NG]], NG, 0), (self.ioe, [[-1, E]], E, 0),
                                            (self.iox, [[1, E]], 0, 0), (self.iob, [[1, NB]], 0, 0),
                                            (self.ios, [[1, P]], 0, 0), (self.tok, [[P, NT]], 0, 1)):
                    pool.iota(tile[:], pattern=pat, base=base, channel_multiplier=cm, **kw).then_inc(self.s_io.sem, 1)

            def route_sp(self, sp):
                for s, v in self.norm.h_ready:
                    sp.wait_ge(s, v)
                sp.dma_start(wr[:], A["w_router"][self.l]).then_inc(self.s_wr.sem, 16)

            def route_pe(self, pe):
                for s, v in self.norm.done:
                    pe.wait_ge(s, v)
                pe.wait_ge(*self.s_wr(16))
                for t in range(NT):
                    for k in range(KD):
                        ins = pe.matmul(bank(4)[:, t * (NG + E):(t + 1) * (NG + E)],
                                        self.xt[:, k, t * P:(t + 1) * P], wr[:, k, :],
                                        start=(k == 0), stop=(k == KD - 1))
                ins.then_inc(self.s_lg.sem, 1)
                pe.wait_ge(*self.s_A(1))
                for t in range(NT):
                    for s in range(t + 1):
                        ins = pe.matmul(bank(5)[:, t * E:(t + 1) * E], before[:] if s == t else ones[:],
                                        self.both[:, s, :], start=(s == 0), stop=(s == t))
                for t in range(NT):
                    ins = pe.matmul(bank(6)[:, 0:E], ones[:], self.both[:, t, :], start=(t == 0),
                                    stop=(t == NT - 1))
                ins.then_inc(self.s_rk.sem, 1)
                pe.wait_ge(*self.s_q(1))
                for n in range(2 * NT):
                    ins = pe.matmul(bank(7)[:, 0:NB], self.q_s[:, n, :], self.q_b[:, n, :], start=(n == 0),
                                    stop=(n == 2 * NT - 1))
                ins.then_inc(self.s_tab.sem, 1)

            def route_act(self, act):
                act.wait_ge(*self.s_exd(1))
                act.activation(self.small[:, 4:8, :], self.small[:, 4:8, :], ACT.Exp).then_inc(self.s_ex.sem, 1)
                act.wait_ge(*self.s_exd(2))
                act.activation(self.small[:, 10, :], self.small[:, 10, :], ACT.Exp).then_inc(self.s_ex.sem, 1)

            def route_dve(self, dve):
                L = dve_chain.link
                sm, tmp, em = self.small, self.tmp, self.em
                dve.wait_ge(*self.s_io(6))
                dve.wait_ge(*self.s_lg(1))
                L(dve, dve.tensor_copy(self.lg[:].rearrange("p t c -> p (t c)"), bank(4)[:, 0:NT * (NG + E)]))
                gl = self.lg[:, :, 0:NG]
                el = self.lg[:, :, NG:NG + E]

                def bc(v, n):
                    return v.unsqueeze(2).to_broadcast([P, NT, n])

                def rowbc(v, n):
                    return v.unsqueeze(1).to_broadcast([P, NT, n])

                L(dve, dve.reduce_max(sm[:, 0, :], gl, AXX))
                g4 = self.tmp[:, :, 0:NG]
                L(dve, dve.tensor_tensor(g4, gl, bc(sm[:, 0, :], NG), ALU.is_ge))
                L(dve, dve.tensor_tensor(g4, g4, rowbc(self.iog[:], NG), ALU.mult))
                L(dve, dve.reduce_max(sm[:, 1, :], g4, AXX))
                goh = self.tmp[:, :, NG:2 * NG]
                L(dve, dve.tensor_tensor(goh, g4, bc(sm[:, 1, :], NG), ALU.is_equal))
                ge = sm[:, 4:8, :].rearrange("p g t -> p t g")
                dve.tensor_tensor(ge, gl, bc(sm[:, 0, :], NG), ALU.subtract).then_inc(self.s_exd.sem, 1)
                L(dve, dve.tensor_scalar(g4, goh, 1.0, -NEG, ALU.subtract, ALU.mult))
                for g in range(NG):
                    sl = slice(g * EG, (g + 1) * EG)
                    L(dve, dve.tensor_tensor(em[:, :, sl], el[:, :, sl], bc(goh[:, :, g], EG), ALU.mult))
                    L(dve, dve.tensor_tensor(em[:, :, sl], em[:, :, sl], bc(g4[:, :, g], EG), ALU.add))
                for k in range(2):
                    m = sm[:, 2 + k, :]
                    L(dve, dve.reduce_max(m, em[:], AXX))
                    L(dve, dve.tensor_tensor(tmp[:], em[:], bc(m, E), ALU.is_ge))
                    L(dve, dve.tensor_tensor(tmp[:], tmp[:], rowbc(self.ioe[:], E), ALU.mult))
                    L(dve, dve.reduce_max(sm[:, 9, :], tmp[:], AXX))
                    L(dve, dve.tensor_tensor(self.oh[k][:], tmp[:], bc(sm[:, 9, :], E), ALU.is_equal))
                    if k == 0:
                        L(dve, dve.scalar_tensor_tensor(em[:].rearrange("p t e -> p (t e)"),
                                                        self.oh[0][:].rearrange("p t e -> p (t e)"), 2 * NEG,
                                                        em[:].rearrange("p t e -> p (t e)"), ALU.mult, ALU.add))
                dve.tensor_tensor(self.both[:], self.oh[0][:], self.oh[1][:], ALU.add).then_inc(self.s_A.sem, 1)
                dve.tensor_tensor(sm[:, 10, :], sm[:, 3, :], sm[:, 2, :], ALU.subtract).then_inc(self.s_exd.sem, 1)
                dve.wait_ge(*self.s_ex(2))
                L(dve, dve.reduce_sum(sm[:, 11, :], ge, AXX))
                L(dve, dve.tensor_scalar(sm[:, 12, :], sm[:, 10, :], 1.0, None, ALU.add))
                L(dve, dve.tensor_tensor(sm[:, 11, :], sm[:, 11, :], sm[:, 12, :], ALU.mult))
                L(dve, dve.reciprocal(w_tok[:, 0:NT], sm[:, 11, :]))
                L(dve, dve.tensor_tensor(w_tok[:, NT:2 * NT], w_tok[:, 0:NT], sm[:, 10, :], ALU.mult))
                dve.wait_ge(*self.s_rk(1))
                r = self.row
                L(dve, dve.tensor_scalar(r[:, 1, :], bank(6)[:, 0:E], float(P), None, ALU.is_gt))
                for j in range(2, T // P):
                    L(dve, dve.scalar_tensor_tensor(r[:, 1, :], bank(6)[:, 0:E], float(P * j), r[:, 1, :],
                                                    ALU.is_gt, ALU.add))
                L(dve, dve.tensor_tensor_scan(r[:, 2, :], ones[:, 0:E], r[:, 1, :], 0.0, ALU.mult, ALU.add))
                L(dve, dve.tensor_tensor(r[:, 3, :], r[:, 2, :], r[:, 1, :], ALU.subtract))
                for k in range(2):
                    for n, src in enumerate((bank(5)[:, 0:NT * E].rearrange("p (t e) -> p t e", e=E),
                                             rowbc(self.iox[:], E), rowbc(r[:, 3, :], E))):
                        L(dve, dve.tensor_tensor(tmp[:], self.oh[k][:], src, ALU.mult))
                        L(dve, dve.reduce_sum(sm[:, 12 + 2 * n + k, :], tmp[:], AXX))
                rank, exp_, ovs = sm[:, 12:14, :], sm[:, 14:16, :], sm[:, 16:18, :]
                fl, bk, t2 = sm[:, 18:20, :], sm[:, 20:22, :], sm[:, 22:24, :]
                L(dve, dve.tensor_scalar(fl, rank, float(P), None, ALU.is_ge))
                for j in range(2, T // P):
                    L(dve, dve.scalar_tensor_tensor(fl, rank, float(P * j), fl, ALU.is_ge, ALU.add))
                L(dve, dve.tensor_tensor(t2, ovs, fl, ALU.add))
                L(dve, dve.scalar_tensor_tensor(t2, t2, float(E - 1), exp_, ALU.add, ALU.subtract))
                L(dve, dve.scalar_tensor_tensor(t2, fl, 1.0, t2, ALU.min, ALU.mult))
                L(dve, dve.tensor_tensor(bk, exp_, t2, ALU.add))
                L(dve, dve.scalar_tensor_tensor(rank, fl, -float(P), rank, ALU.mult, ALU.add))
                L(dve, dve.scalar_tensor_tensor(t2, bk, float(P), rank, ALU.mult, ALU.add))
                L(dve, dve.tensor_copy(dest_i[:].rearrange("p (k t) -> p k t", k=2), t2))
                for k in range(2):
                    for t in range(NT):
                        n = k * NT + t
                        dve.tensor_scalar(self.q_s[:, n, :], self.ios[:], sm[:, 12 + k, t:t + 1], None, ALU.is_equal)
                        ins = dve.tensor_scalar(self.q_b[:, n, :], self.iob[:], sm[:, 20 + k, t:t + 1],
                                                self.tok[:, t:t + 1], ALU.is_equal, ALU.mult)
                L(dve, ins)
                dve.engine_nop().then_inc(self.s_q.sem, 1)
                for b in range(OVB):
                    ins = dve.tensor_scalar(self.ovc[:, b, :], r[:, 2, :], float(b), None, ALU.is_le)
                L(dve, ins)
                L(dve, dve.reduce_sum(self.ovf[:, 0:OVB], self.ovc[:], AXX))
                L(dve, dve.tensor_scalar(self.ovf[:, 0:OVB], self.ovf[:, 0:OVB], float(E - 1), None, ALU.min))
                L(dve, dve.tensor_copy(self.ovf[:, OVB:OVB + 1], r[:, 2, E - 1:E]))
                L(dve, dve.tensor_copy(ov_e[:], self.ovf[:]))
                dve.wait_ge(*self.s_tab(1))
                dve.tensor_copy(idx_tab[:], bank(7)[:, 0:NB]).then_inc(self.s_rt.sem, 1)

            def unit(self, e, what, half):
                if what == "d":
                    e = e + 1
                    if isinstance(e, int) and e == E:
                        return 4 + 6 * (E - 1) + half
                if isinstance(e, int) and e == 0:
                    return {"g": 0, "u": 2}[what] + half
                return 4 + 6 * (e - 1) + {"g": 0, "d": 2, "u": 4}[what] + half

            def w_src(self, e, what, half):
                if what == "d":
                    w = A["w_down"][self.l].rearrange("e (p q) n -> e p (q n)", q=F // P)
                else:
                    w = A["w_gate" if what == "g" else "w_up"][self.l].rearrange("e (p k) n -> e p (k n)", k=KD)
                if isinstance(e, int):
                    return w[e, :, half * UNIT:(half + 1) * UNIT]
                return w[bass.ds(e, 1), :, half * UNIT:(half + 1) * UNIT].rearrange("a p c -> (a p) c")

            def rep(self, e, r):
                return e if isinstance(e, int) else r

            def load(self, sp, e, r, what, half):
                u, ur = self.unit(e, what, half), self.unit(r, what, half)
                g, gr = self.first + u, self.first + ur
                if isinstance(u, int):
                    stream.wait_free(sp, g)
                else:
                    sp.wait_ge(unit_dve, stream.owner[self.first][1] - 1 + u - RING + 1)
                sp.dma_start(ring[:, gr % RING, :], self.w_src(e, what, half)).then_inc(ring_full[gr % RING], 16)

            def full(self, eng, e, r, what, half):
                u, ur = self.unit(e, what, half), self.unit(r, what, half)
                g0, gr = self.first, self.first + self.unit(r, what, half)
                turns = gr // RING + 1
                if isinstance(e, int):
                    eng.wait_ge(ring_full[gr % RING], 16 * turns)
                else:
                    eng.wait_ge(ring_full[gr % RING], (e - r) * 16 + 16 * turns)

            def steps(self, e):
                if isinstance(e, int) and e == 0:
                    return [(e, "g"), (e, "u")]
                if isinstance(e, int) and e == E:
                    return [(e - 1, "d")]
                return [(e, "g"), (e - 1, "d"), (e, "u")]

            def sp(self, sp):
                self.over_loop(sp, lambda e, r: [self.load(sp, x, rx, w, hf)
                                                 for (x, w), (rx, _) in zip(self.steps(e), self.steps(r))
                                                 for hf in range(2)])

            def over_loop(self, eng, step):
                step(0, 0)
                step(1, 1)
                with eng.Fori(0, (E - 4) // 2) as i:
                    step(2 * i + 2, 2)
                    step(2 * i + 3, 3)
                step(E - 2, E - 2)
                step(E - 1, E - 1)
                step(E, E)

            def split(self, eng, e, r, what, half):
                u, ur = self.unit(e, what, half), self.unit(r, what, half)
                slot = ur % SPLIT
                src = ring[:, (self.first + ur) % RING, :]
                if eng is nc.scalar:
                    self.full(eng, e, r, what, half)
                    if not isinstance(u, int) or u >= SPLIT:
                        eng.wait_ge(*self.s_use(u - SPLIT + 1))
                    eng.activation(self.hi[:, slot, :], src, ACT.Copy).then_inc(self.s_hi.sem, 1)
                else:
                    eng.wait_ge(*self.s_hi(u + 1))
                    eng.tensor_tensor(self.lo[:, slot, :], src, self.hi[:, slot, :].bitcast(F32), ALU.subtract)\
                       .then_inc(unit_dve, 1)

            def unit_ready(self, pe, u):
                pe.wait_ge(unit_dve, stream.owner[self.first][1] + u)

            def x_transpose(self, pe, e, r):
                b = r % 2
                pe.wait_ge(*self.s_gx[b]((e // 2) * 16 + 16 if isinstance(e, int) else (e - r) * 8 + 16 * (r // 2 + 1)))
                if not isinstance(e, int) or e >= 1:
                    pe.wait_ge(*self.s_xl(e))
                for k in range(KD):
                    ins = pe.transpose(bank(0, 2)[:, k * P:(k + 1) * P], self.xg[:, b, k::KD], ident[:])
                ins.then_inc(self.s_xtr.sem, 1)

            def product(self, pe, out, xs, e, r, what, half, first, last):
                u, ur = self.unit(e, what, half), self.unit(r, what, half)
                self.unit_ready(pe, u)
                slot = ur % SPLIT
                n = UNIT // 512
                mats = []
                for q in range(n):
                    if what == "d":
                        row, col = q // 2, q % 2
                        k, o, st = 2 * half + row, out[:, col * 512:(col + 1) * 512], first and row == 0
                        en = last and row == 1
                    else:
                        k, o, st, en = 4 * half + q, out, first and q == 0, last and q == n - 1
                    mats.append((k, o, self.hi[:, slot, q * 512:(q + 1) * 512],
                                 self.lo[:, slot, q * 512:(q + 1) * 512], st, en))
                for k, o, wh_, wl_, st, en in mats:
                    xhk, xlk = xs(k)
                    pe.matmul(o, xhk, wh_, start=st, stop=False)
                    pe.matmul(o, xhk, wl_, start=False, stop=False)
                    ins = pe.matmul(o, xlk, wh_, start=False, stop=en)
                ins.then_inc(self.s_use.sem, 1)
                return ins

            def pe(self, pe):
                def xs(r):
                    return lambda k: (self.xh[:, r % 2, k * P:(k + 1) * P], self.xl[:, r % 2, k * P:(k + 1) * P])

                def hs(k):
                    return self.hh[:, k * P:(k + 1) * P], self.hl[:, k * P:(k + 1) * P]

                def step(e, r):
                    if r < E:
                        pe.wait_ge(*self.s_xl(e + 1))
                        if not isinstance(e, int) or e >= 1:
                            pe.wait_ge(*self.s_sg(e))
                        for half in range(2):
                            self.product(pe, bank(2), xs(r), e, r, "g", half, half == 0, half == 1)
                    if r >= 1:
                        pe.wait_ge(*self.s_hm(e))
                        for q in range(F // P):
                            ins = pe.transpose(bank(4)[:, q * P:(q + 1) * P], self.hm[:, q::F // P], ident[:])
                        ins.then_inc(self.s_htr.sem, 1)
                    if r + 1 < E:
                        self.x_transpose(pe, e + 1, r + 1)
                    if r >= 1:
                        pe.wait_ge(*self.s_hl(e))
                        if not isinstance(e, int) or e >= 2:
                            pe.wait_ge(*self.s_ya(e - 1))
                            pe.wait_ge(*self.s_yd(e - 1))
                        for half in range(2):
                            self.product(pe, bank(5, 2), hs, e - 1, r - 1, "d", half, half == 0, half == 1)
                    if r < E:
                        for half in range(2):
                            self.product(pe, bank(3), xs(r), e, r, "u", half, half == 0, half == 1)

                self.x_transpose(pe, 0, 0)
                self.over_loop(pe, step)

            def used(self, e, what):
                return self.unit(e, what, 1) + 1

            def act(self, act):
                def x_hi(e, r):
                    act.wait_ge(*self.s_xtr(e + 1))
                    if not isinstance(e, int) or e >= 2:
                        act.wait_ge(*self.s_use(self.used(e - 2, "u")))
                    act.activation(self.xh[:, r % 2, :], bank(0, 2), ACT.Copy).then_inc(self.s_xh.sem, 1)

                def step(e, r):
                    if r >= 1:
                        for half in range(2):
                            self.split(act, e - 1, r - 1, "d", half)
                    if r < E:
                        self.split(act, e, r, "u", 0)
                        act.wait_ge(*self.s_use(self.used(e, "g")))
                        if not isinstance(e, int) or e >= 1:
                            act.wait_ge(*self.s_hm(e))
                        act.activation(self.sg[:], bank(2), ACT.Silu).then_inc(self.s_sg.sem, 1)
                    if r >= 1:
                        act.wait_ge(*self.s_htr(e))
                        act.activation(self.hh[:], bank(4), ACT.Copy).then_inc(self.s_hh.sem, 1)
                    if r + 1 < E:
                        x_hi(e + 1, r + 1)
                    if r < E:
                        self.split(act, e, r, "u", 1)
                        if r + 1 < E:
                            for half in range(2):
                                self.split(act, e + 1, r + 1, "g", half)
                    if r >= 1:
                        act.wait_ge(*self.s_use(self.used(e - 1, "d")))
                        if not isinstance(e, int) or e >= 3:
                            act.wait_ge(*self.s_yst[(r - 1) % 2](self.stored(e - 3, r - 3)))
                        act.activation(self.y[:, (r - 1) % 2, 0:512], bank(5), ACT.Copy).then_inc(self.s_ya.sem, 1)

                act.wait_ge(*self.s_tab(1))
                for half in range(2):
                    self.split(act, 0, 0, "g", half)
                x_hi(0, 0)
                self.over_loop(act, step)

            def stored(self, e, r):
                if isinstance(e, int):
                    return 16 * (e // 2 + 1)
                return (e - r) * 8 + 16 * (r // 2 + 1)

            def dve(self, dve):
                def x_lo(e, r):
                    dve.wait_ge(*self.s_xh(e + 1))
                    dve.tensor_tensor(self.xl[:, r % 2, :], bank(0, 2), self.xh[:, r % 2, :].bitcast(F32),
                                      ALU.subtract).then_inc(self.s_xl.sem, 1)

                def step(e, r):
                    if r >= 1:
                        dve.wait_ge(*self.s_use(self.used(e - 1, "u")))
                        dve.wait_ge(*self.s_sg(e))
                        dve.tensor_tensor(self.hm[:], self.sg[:], bank(3), ALU.mult).then_inc(self.s_hm.sem, 1)
                        for half in range(2):
                            self.split(dve, e - 1, r - 1, "d", half)
                    if r < E:
                        self.split(dve, e, r, "u", 0)
                    if r >= 1:
                        dve.wait_ge(*self.s_hh(e))
                        dve.tensor_tensor(self.hl[:], bank(4), self.hh[:].bitcast(F32),
                                          ALU.subtract).then_inc(self.s_hl.sem, 1)
                    if r + 1 < E:
                        x_lo(e + 1, r + 1)
                    if r < E:
                        self.split(dve, e, r, "u", 1)
                        if r + 1 < E:
                            for half in range(2):
                                self.split(dve, e + 1, r + 1, "g", half)
                    if r >= 1:
                        dve.wait_ge(*self.s_use(self.used(e - 1, "d")))
                        if not isinstance(e, int) or e >= 3:
                            dve.wait_ge(*self.s_yst[(r - 1) % 2](self.stored(e - 3, r - 3)))
                        dve.tensor_copy(self.y[:, (r - 1) % 2, 512:1024], bank(6)).then_inc(self.s_yd.sem, 1)

                for half in range(2):
                    self.split(dve, 0, 0, "g", half)
                x_lo(0, 0)
                self.over_loop(dve, step)

            def pool(self, pool):
                def gather(e):
                    pool.indirect_dma_start(self.xg[:, e % 2, :], None, xn_dram,
                                            bass.IndirectOffsetOnAxis(ap=idx_tab[:, e:e + 1], axis=0))\
                        .then_inc(self.s_gx[e % 2].sem, 16)

                def store(e):
                    pool.wait_ge(*self.s_ya(e + 1))
                    pool.wait_ge(*self.s_yd(e + 1))
                    pool.dma_start(y_dram[e * P:(e + 1) * P, :], self.y[:, e % 2, :]).then_inc(self.s_yst[e % 2].sem, 16)

                pool.wait_ge(*self.s_rt(1))
                for n in range(4):
                    pool.wait_ge(*self.norm.s_st[n](16 * (NT // 4)))
                gather(0)
                gather(1)
                for e in range(E):
                    if e + 2 < E:
                        pool.wait_ge(*self.s_xtr(e + 1))
                        gather(e + 2)
                    if e >= 1:
                        store(e - 1)
                store(E - 1)
                for b in range(2):
                    pool.wait_ge(*self.s_yst[b](16 * (E // 2)))

            def number(self, eng):
                eng.wait_ge(*self.s_rt(1))
                return eng.value_load(ov_e[0:1, OVB:OVB + 1], min_val=0, max_val=OVB)

            def beyond_sp(self, sp):
                sp.wait_ge(unit_dve, stream.owner[self.first + 6 * E - 1][1])
                n = self.number(sp)
                with sp.If(n > 0):
                    with sp.Fori(0, n) as j:
                        sp.wait_ge(*self.s_of(j + 1))
                        e = sp.value_load(ov_e[0:1, bass.ds(j, 1)], min_val=0, max_val=E - 1)
                        for m, (w, q) in enumerate((("w_gate", KD), ("w_up", KD), ("w_down", F // P))):
                            src = A[w][self.l].rearrange("e (p q) n -> e p (q n)", q=q)[bass.ds(e, 1)]
                            sp.dma_start(ring[:, 2 * m:2 * m + 2, :].rearrange("p a c -> p (a c)"),
                                         src.rearrange("a p c -> (a p) c")).then_inc(self.s_ow.sem, 16)
                sp.wait_ge(*self.s_odone(1))

            def beyond_pool(self, pool):
                def step(n):
                    n += 5 * self.l
                    return pool.tensor_tensor(fence[:, n:n + 1], ones[:, 0:1], ones[:, 0:1], ALU.add)

                step(0).then_inc(self.s_of.sem, 1)
                n = self.number(pool)
                with pool.If(n > 0):
                    with pool.Fori(0, n) as j:
                        pool.wait_ge(*self.s_of(j + 1))
                        pool.tensor_copy(self.ovi[:], idx_tab[:, bass.ds(j + E, 1)]).then_inc(self.s_oi.sem, 1)
                        pool.wait_ge(*self.s_oi(2 * j + 1))
                        step(1).then_inc(self.s_oi.sem, 1)
                        pool.indirect_dma_start(self.xg[:, 0, :], None, xn_dram,
                                                bass.IndirectOffsetOnAxis(ap=self.ovi[:, 0:1], axis=0))\
                            .then_inc(self.s_ox.sem, 16)
                        pool.wait_ge(*self.s_oa(4 * j + 4))
                        pool.dma_start(y_dram[bass.ds(j * P + E * P, P), :], self.y[:, 0, :])\
                            .then_inc(self.s_oy.sem, 16)
                        pool.wait_ge(*self.s_oi(2 * j + 2))
                        pool.wait_ge(*self.s_oy(16 * j + 16))
                        step(2).then_inc(self.s_of.sem, 1)
                step(3).then_inc(self.s_odone.sem, 1)

            def beyond_pe(self, pe):
                n = self.number(pe)
                pe.wait_ge(*self.s_ya(E))
                pe.wait_ge(*self.s_yd(E))
                with pe.If(n > 0):
                    with pe.Fori(0, n) as j:
                        pe.wait_ge(*self.s_ox(16 * j + 16))
                        for k in range(KD):
                            ins = pe.transpose(bank(0, 2)[:, k * P:(k + 1) * P], self.xg[:, 0, k::KD], ident[:])
                        ins.then_inc(self.s_op.sem, 1)
                        pe.wait_ge(*self.s_oa(4 * j + 1))
                        pe.wait_ge(*self.s_ow(48 * j + 48))
                        for m in range(2):
                            for k in range(KD):
                                w = ring[:, 2 * m + k // 4, (k % 4) * 512:(k % 4 + 1) * 512]
                                ins = pe.matmul(bank(2 + m), self.xf[:, k * P:(k + 1) * P], w, start=(k == 0),
                                                stop=(k == KD - 1))
                        ins.then_inc(self.s_op.sem, 1)
                        pe.wait_ge(*self.s_od(j + 1))
                        for q in range(F // P):
                            ins = pe.transpose(bank(4)[:, q * P:(q + 1) * P], self.hm[:, q::F // P], ident[:])
                        ins.then_inc(self.s_op.sem, 1)
                        pe.wait_ge(*self.s_oa(4 * j + 3))
                        for c in range(2):
                            for q in range(F // P):
                                w = ring[:, 4 + q // 2, (q % 2) * D + c * 512:(q % 2) * D + (c + 1) * 512]
                                ins = pe.matmul(bank(5 + c), self.hf[:, q * P:(q + 1) * P], w, start=(q == 0),
                                                stop=(q == F // P - 1))
                        ins.then_inc(self.s_op.sem, 1)

            def beyond_act(self, act):
                n = self.number(act)
                with act.If(n > 0):
                    with act.Fori(0, n) as j:
                        act.wait_ge(*self.s_op(4 * j + 1))
                        act.activation(self.xf[:], bank(0, 2), ACT.Copy).then_inc(self.s_oa.sem, 1)
                        act.wait_ge(*self.s_op(4 * j + 2))
                        act.activation(self.sg[:], bank(2), ACT.Silu).then_inc(self.s_oa.sem, 1)
                        act.wait_ge(*self.s_op(4 * j + 3))
                        act.activation(self.hf[:], bank(4), ACT.Copy).then_inc(self.s_oa.sem, 1)
                        act.wait_ge(*self.s_op(4 * j + 4))
                        act.activation(self.y[:, 0, :], bank(5, 2), ACT.Copy).then_inc(self.s_oa.sem, 1)

            def beyond_dve(self, dve):
                n = self.number(dve)
                with dve.If(n > 0):
                    with dve.Fori(0, n) as j:
                        dve.wait_ge(*self.s_oa(4 * j + 2))
                        dve.tensor_tensor(self.hm[:], self.sg[:], bank(3), ALU.mult).then_inc(self.s_od.sem, 1)

            def combine_pool(self, pool):
                for n in range(2 * NT):
                    if n >= 8:
                        pool.wait_ge(*self.s_comb(n - 7))
                    t, k = n // 2, n % 2
                    pool.indirect_dma_start(self.rows[:, n % 8, :], None, y_dram,
                                            bass.IndirectOffsetOnAxis(ap=dest_i[:, k * NT + t:k * NT + t + 1], axis=0))\
                        .then_inc(self.s_row[n % 8].sem, 16)

            def combine_dve(self, dve):
                for n in range(2 * NT):
                    t, k = n // 2, n % 2
                    dve.wait_ge(*self.s_row[n % 8](16 * (n // 8 + 1)))
                    if k:
                        dve.wait_ge(*self.s_comb(n))
                    dve.scalar_tensor_tensor(h[:, t, :], self.rows[:, n % 8, :],
                                             w_tok[:, k * NT + t:k * NT + t + 1], h[:, t, :],
                                             ALU.mult, ALU.add).then_inc(self.s_comb.sem, 1)

        class Ple:

            def __init__(self, l, h_ready):
                a = Arena(f"p{l}")
                tag = f"p{l}_"
                self.l = l
                self.xt = a("xt", [P, KD, T])
                self.xn = a("xn", [P, 4, D])
                self.gbc = a("gbc", [P, D])
                self.pt = a("pt", [P, 2, T])
                self.sg = a("sg", [P, 4, 512])
                self.norm = NormTranspose(tag + "n", A["norm_ple"][l:l + 1, :], self.xt, self.xn, self.gbc, h_ready)
                self.s_p, self.s_g, self.s_pr, self.s_sg, self.s_mul, self.s_add = (
                    count("ple_" + n, t) for n, t in (("p", 16), ("gate", 2 * NT), ("proj", 2 * NT),
                                                      ("sigmoid", 2 * NT), ("mul", 2 * NT), ("add", 2 * NT)))
                self.units = [stream.dense(3) for _ in range(2)]
                self.done = [self.s_add(2 * NT)]

            def sp_pt(self, sp):
                sp.dma_start(self.pt[:], A["p_t"][self.l]).then_inc(self.s_p.sem, 16)

            def sp(self, sp):
                for c, u in enumerate(self.units):
                    for half in range(2):
                        load_unit(sp, u + half, A["w_ple_gate"][self.l, c][:, half * UNIT:(half + 1) * UNIT], UNIT)
                    load_unit(sp, u + 2, A["w_ple_proj"][self.l, c], 2 * 512)

            def pe(self, pe):
                for s, v in self.norm.done:
                    pe.wait_ge(s, v)
                pe.wait_ge(*self.s_p(16))
                for c, u in enumerate(self.units):
                    for t in range(NT):
                        g = c * NT + t
                        if g >= 2:
                            pe.wait_ge(*self.s_sg(g - 1))
                            pe.wait_ge(*self.s_mul(g - 1))
                        for k in range(KD):
                            if t == 0 and k % 4 == 0:
                                full(pe, u + k // 4)
                            ins = pe.matmul(bank(4 + g % 2), self.xt[:, k, t * P:(t + 1) * P],
                                            ring[:, (u + k // 4) % RING, (k % 4) * 512:(k % 4 + 1) * 512],
                                            start=(k == 0), stop=(k == KD - 1))
                        ins.then_inc(self.s_g.sem, 1)
                        if t == 0:
                            full(pe, u + 2)
                        for k in range(2):
                            ins = pe.matmul(bank(6 + g % 2), self.pt[:, k, t * P:(t + 1) * P],
                                            ring[:, (u + 2) % RING, k * 512:(k + 1) * 512],
                                            start=(k == 0), stop=(k == 1))
                        ins.then_inc(self.s_pr.sem, 1)
                    pe.wait_ge(*self.s_pr((c + 1) * NT))
                    pe.nop().then_inc(unit_pe, 3)

            def act(self, act):
                for g in range(2 * NT):
                    act.wait_ge(*self.s_g(g + 1))
                    if g >= 4:
                        act.wait_ge(*self.s_mul(g - 3))
                    act.activation(self.sg[:, g % 4, :], bank(4 + g % 2), ACT.Sigmoid).then_inc(self.s_sg.sem, 1)

            def dve(self, dve):
                for g in range(2 * NT):
                    c, t = divmod(g, NT)
                    hs = h[:, t, c * 512:(c + 1) * 512]
                    dve.wait_ge(*self.s_sg(g + 1))
                    dve.wait_ge(*self.s_pr(g + 1))
                    dve.tensor_tensor(self.sg[:, g % 4, :], self.sg[:, g % 4, :], bank(6 + g % 2), ALU.mult)\
                       .then_inc(self.s_mul.sem, 1)
                    dve.wait_ge(*self.s_mul(g + 1))
                    dve.tensor_tensor(hs, hs, self.sg[:, g % 4, :], ALU.add).then_inc(self.s_add.sem, 1)

        class SpatialGate:
            def __init__(self, h_ready):
                a = Arena("mix1")
                self.xt = a("xt", [P, KD, T])
                self.ut = a("ut", [P, KD, T])
                self.v = a("v", [P, NT, SG])
                self.ws = a("ws", [P, SGG, P])
                self.bs = a("bs", [P, SGG, P])
                self.gbc = a("gbc", [P, D])
                self.tmp = a("tmp", [P, 2, 512])
                self.norm = NormTranspose("n1", A["norm_mix"][1:2, :], self.xt, self.v[:, 0:4, :], self.gbc, h_ready)
                self.units = [stream.dense(2) for _ in range(4)]
                self.s_ws, self.s_bs, self.s_mask, self.s_u, self.s_ue, self.s_v, self.s_ve, self.s_sq, self.s_r, self.s_vs, self.s_s, self.s_t, self.s_y = (
                    Count(sem("gmlp_" + n), 0) for n in ("ws", "bs", "mask", "u", "ue", "v", "ve", "sq", "r", "vs", "s", "t", "y"))

            def sp(self, sp):
                for c, u in enumerate(self.units):
                    for half in range(2):
                        load_unit(sp, u + half, A["w_in_o"][c][:, half * UNIT:(half + 1) * UNIT], UNIT)

            def sp_small(self, sp):
                sp.dma_start(self.ws[:], A["w_s_t"]).then_inc(self.s_ws.sem, 16)
                sp.dma_start(self.bs[:].rearrange("p g t -> p (g t)"), A["b_s"].partition_broadcast(P))\
                  .then_inc(self.s_bs.sem, 16)

            def pool(self, pool):
                pool.wait_ge(*self.s_ws(16))
                pool.affine_select(out=self.ws[:], in_=self.ws[:], compare_op=ALU.is_ge, fill=0.0, base=0,
                                   pattern=[[0, SGG], [1, P]], channel_multiplier=-1).then_inc(self.s_mask.sem, 1)

            def pe(self, pe):
                for s, v in self.norm.done:
                    pe.wait_ge(s, v)
                g = 0
                for c in range(2):
                    u = self.units[c]
                    for b in range(4):
                        for hf in range(2):
                            if g >= 4:
                                pe.wait_ge(*self.s_ue(g - 3))
                            for k in range(KD):
                                if b == 0 and hf == 0 and k % 4 == 0:
                                    full(pe, u + k // 4)
                                o = (k % 4) * 512 + b * P
                                ins = pe.matmul(bank(4 + g % 4), ring[:, (u + k // 4) % RING, o:o + P],
                                                self.xt[:, k, hf * 512:(hf + 1) * 512],
                                                start=(k == 0), stop=(k == KD - 1))
                            ins.then_inc(self.s_u.sem, 1)
                            g += 1
                    pe.wait_ge(*self.s_u(g))
                    pe.nop().then_inc(unit_pe, 2)
                for c in range(2):
                    u = self.units[2 + c]
                    for t in range(NT):
                        n = c * NT + t
                        if n >= 4:
                            pe.wait_ge(*self.s_ve(n - 3))
                        for k in range(KD):
                            if t == 0 and k % 4 == 0:
                                full(pe, u + k // 4)
                            ins = pe.matmul(bank(n % 4), self.xt[:, k, t * P:(t + 1) * P],
                                            ring[:, (u + k // 4) % RING, (k % 4) * 512:(k % 4 + 1) * 512],
                                            start=(k == 0), stop=(k == KD - 1))
                        ins.then_inc(self.s_v.sem, 1)
                    pe.wait_ge(*self.s_v((c + 1) * NT))
                    pe.nop().then_inc(unit_pe, 2)
                pe.wait_ge(*self.s_mask(1))
                pe.wait_ge(*self.s_vs(NT))
                pe.wait_ge(*self.s_ue(16))
                for g in range(SGG):
                    for hf in range(2):
                        n = 2 * g + hf
                        if n >= 4:
                            pe.wait_ge(*self.s_t(n - 3))
                        for t in range(4):
                            ins = pe.matmul(bank(4 + n % 4)[:, t * P:(t + 1) * P],
                                            self.v[:, 4 * hf + t, g * P:(g + 1) * P], self.ws[:, g, :],
                                            start=True, stop=True)
                        ins.then_inc(self.s_s.sem, 1)

            def act(self, act):
                for g in range(16):
                    b, hf = divmod(g, 2)
                    act.wait_ge(*self.s_u(g + 1))
                    act.activation(self.ut[:, b, hf * 512:(hf + 1) * 512], bank(4 + g % 4),
                                   ACT.Gelu_apprx_tanh).then_inc(self.s_ue.sem, 1)
                for n in range(16):
                    c, t = divmod(n, NT)
                    act.wait_ge(*self.s_v(n + 1))
                    act.activation(self.v[:, t, c * 512:(c + 1) * 512], bank(n % 4),
                                   ACT.Gelu_apprx_tanh).then_inc(self.s_ve.sem, 1)
                act.wait_ge(*self.s_ve(16))
                for t in range(NT):
                    act.activation(self.xt[:, t, :], self.v[:, t, :], ACT.Square,
                                   accum_out=ss[:, t:t + 1]).then_inc(self.s_sq.sem, 1)
                act.wait_ge(*self.s_r(1))
                act.activation(rstd[:], rstd[:], ACT.Sqrt).then_inc(self.s_r.sem, 1)

            def dve(self, dve):
                dve.wait_ge(*self.s_sq(NT))
                dve.tensor_scalar(rstd[:], ss[:], 1.0 / SG, EPS, ALU.mult, ALU.add).then_inc(self.s_r.sem, 1)
                dve.wait_ge(*self.s_r(2))
                dve_chain.link(dve, dve.reciprocal(rstd[:], rstd[:]))
                for t in range(NT):
                    dve.tensor_scalar(self.v[:, t, :], self.v[:, t, :], rstd[:, t:t + 1], None, ALU.mult)\
                       .then_inc(self.s_vs.sem, 1)
                dve.wait_ge(*self.s_bs(16))
                dve.wait_ge(*self.s_ue(16))
                for n in range(16):
                    g, hf = divmod(n, 2)
                    uts = self.ut[:, g, hf * 512:(hf + 1) * 512]
                    tmp = self.tmp[:, n % 2, :]
                    dve.wait_ge(*self.s_s(n + 1))
                    dve.scalar_tensor_tensor(tmp.rearrange("p (t c) -> p t c", c=P),
                                             bank(4 + n % 4).rearrange("p (t c) -> p t c", c=P),
                                             cols[:, C_VN + g:C_VN + g + 1],
                                             self.bs[:, g, :].unsqueeze(1).to_broadcast([P, 4, P]),
                                             ALU.mult, ALU.add).then_inc(self.s_t.sem, 1)
                    dve.wait_ge(*self.s_t(n + 1))
                    dve.tensor_tensor(uts, uts, tmp, ALU.mult).then_inc(self.s_y.sem, 1)

        class Final:
            def __init__(self, h_ready):
                a = Arena("fin")
                self.gbc = a("gbc", [P, D])
                self.o = a("o", [P, NT, D])
                self.h_ready = h_ready
                self.s_g, self.s_ss, self.s_r, self.s_o, self.s_out = (
                    Count(sem("final_" + n), 0) for n in ("g", "ss", "r", "o", "out"))

            def sp(self, sp):
                for s, v in self.h_ready:
                    sp.wait_ge(s, v)
                sp.dma_start(self.gbc[:], A["final_norm"].partition_broadcast(P)).then_inc(self.s_g.sem, 16)
                for t in range(NT):
                    sp.wait_ge(*self.s_o(t + 1))
                    sp.dma_start(out[t * P:(t + 1) * P, :], self.o[:, t, :]).then_inc(self.s_out.sem, 16)
                sp.wait_ge(*self.s_out(16 * NT))

            def act(self, act):
                for s, v in self.h_ready:
                    act.wait_ge(s, v)
                for t in range(NT):
                    act.activation(self.o[:, t, :], h[:, t, :], ACT.Square, accum_out=ss[:, t:t + 1])\
                       .then_inc(self.s_ss.sem, 1)
                act.wait_ge(*self.s_r(1))
                act.activation(rstd[:], rstd[:], ACT.Sqrt).then_inc(self.s_r.sem, 1)

            def dve(self, dve):
                dve.wait_ge(*self.s_ss(NT))
                dve.tensor_scalar(rstd[:], ss[:], 1.0 / D, EPS, ALU.mult, ALU.add).then_inc(self.s_r.sem, 1)
                dve.wait_ge(*self.s_r(2))
                dve_chain.link(dve, dve.reciprocal(rstd[:], rstd[:]))
                dve.wait_ge(*self.s_g(16))
                for t in range(NT):
                    dve.scalar_tensor_tensor(self.o[:, t, :], h[:, t, :], rstd[:, t:t + 1], self.gbc[:],
                                             ALU.mult, ALU.mult).then_inc(self.s_o.sem, 1)

        moe0 = Moe(0, out0.done)
        ple0 = Ple(0, moe0.done)
        gate1 = SpatialGate(ple0.done)
        out1 = OutProj("out1", gate1.ut, A["w_out_o"], [gate1.s_y(16)])
        moe1 = Moe(1, out1.done)
        ple1 = Ple(1, moe1.done)
        final = Final(ple1.done)

        block = ctx.enter_context(nc.Block())

        @block.sync
        def _(sp):
            setup_sp(sp)
            sp.dma_start(gbc0[:], A["norm_mix"][0:1, :].partition_broadcast(P)).then_inc(norm0.s_g.sem, 16)
            in_sp(sp)
            zero_sp(sp)
            att_sp(sp)
            out0.sp(sp)
            for moe, ple in ((moe0, ple0), (moe1, ple1)):
                moe.norm.sp(sp)
                moe.route_sp(sp)
                moe.norm.sp_store(sp)
                moe.sp(sp)
                moe.beyond_sp(sp)
                ple.sp(sp)
                ple.norm.sp(sp)
                ple.sp_pt(sp)
                if moe is moe0:
                    gate1.norm.sp(sp)
                    gate1.sp_small(sp)
                    gate1.sp(sp)
                    out1.sp(sp)
            final.sp(sp)

        @block.gpsimd
        def _(pool):
            setup_pool(pool)
            zero_pool(pool)
            for moe in (moe0, moe1):
                moe.iotas(pool)
                moe.pool(pool)
                moe.beyond_pool(pool)
                moe.combine_pool(pool)
                if moe is moe0:
                    gate1.pool(pool)

        @block.scalar
        def _(act):
            norm0.act(act)
            in_act(act)
            values_out(act, lambda o, x: act.activation(o, x, ACT.Copy), 0, s_va)
            att_act(act)
            yt_act(act)
            for moe, ple in ((moe0, ple0), (moe1, ple1)):
                moe.norm.act(act)
                moe.route_act(act)
                moe.act(act)
                moe.beyond_act(act)
                ple.norm.act(act)
                ple.act(act)
                if moe is moe0:
                    gate1.norm.act(act)
                    gate1.act(act)
            final.act(act)

        @block.vector
        def _(dve):
            norm0.dve(dve)
            in_dve(dve)
            values_out(dve, dve.tensor_copy, 1, s_vd)
            att_dve(dve)
            out0.dve(dve)
            for moe, ple in ((moe0, ple0), (moe1, ple1)):
                moe.norm.dve(dve)
                moe.route_dve(dve)
                moe.dve(dve)
                moe.beyond_dve(dve)
                moe.combine_dve(dve)
                ple.norm.dve(dve)
                ple.dve(dve)
                if moe is moe0:
                    gate1.norm.dve(dve)
                    gate1.dve(dve)
                    out1.dve(dve)
            final.dve(dve)

        @block.tensor
        def _(pe):
            for s, v in CONSTS:
                pe.wait_ge(s, v)
            norm0.pe(pe)
            in_pe(pe)
            values_pe(pe)
            att_pe(pe)
            yt_pe(pe)
            out0.pe(pe)
            for moe, ple in ((moe0, ple0), (moe1, ple1)):
                moe.norm.pe(pe)
                moe.route_pe(pe)
                moe.pe(pe)
                moe.beyond_pe(pe)
                ple.norm.pe(pe)
                ple.pe(pe)
                if moe is moe0:
                    gate1.norm.pe(pe)
                    gate1.pe(pe)
                    out1.pe(pe)


def _panels(w, width):
    k = w.shape[0] // P
    return np.ascontiguousarray(w.reshape(k, P, -1, width).transpose(2, 1, 0, 3).reshape(-1, P, k * width))


def _layout(x, p, positions, norm_mix, norm_ffn, w_in_e, conv_w, q_norm, w_q_up, kv_norm, w_kv_up, w_out_e,
            w_in_o, v_norm, w_s, b_s, w_out_o, w_router_group, w_router_expert, w_gate, w_up, w_down,
            norm_ple, w_ple_gate, w_ple_proj, final_norm):
    w_in = w_in_e[0]
    conv = w_in[:, :3 * CONV].reshape(D, 3, 4, P).transpose(0, 2, 1, 3).reshape(D, 4 * 3 * P)
    half = ROPE // 2
    inv = (1.0 / (10000.0 ** (np.arange(0, ROPE, 2, dtype=np.float32) / np.float32(ROPE)))).astype(np.float32)
    rope = np.zeros((P, 2), np.float32)
    rope[64:96, 0] = np.concatenate([inv, inv])
    rope[64:96, 1] = np.concatenate([-np.ones(half), np.ones(half)])
    col = lambda v: v.reshape(-1, P).T
    cols = np.concatenate([col(q_norm[0]), col(kv_norm[0]), col(v_norm[0]),
                           conv_w[0].reshape(3, 4, P).transpose(2, 1, 0).reshape(P, 12), rope], axis=1)
    wq = w_q_up[0].reshape(3, P, H, DQK).transpose(2, 1, 0, 3).reshape(H, P, 3 * DQK)
    w_kv = w_kv_up[0].reshape(2, P, H, NOPE + VD)
    wk = w_kv[..., :NOPE].transpose(2, 1, 0, 3).reshape(H, P, 2 * NOPE)
    wv = w_kv[..., NOPE:].transpose(1, 0, 2, 3).reshape(P, 2 * H * VD)
    router = np.concatenate([w_router_group, w_router_expert], axis=2)
    return {
        "x": x[0], "cols": cols, "positions": positions,
        "norm_mix": norm_mix, "norm_ffn": norm_ffn, "norm_ple": norm_ple, "final_norm": final_norm[None],
        "w_in_e": _panels(np.concatenate([conv, w_in[:, 3 * CONV:3 * CONV + QR]], axis=1), 3 * P),
        "w_in_kv": _panels(w_in[:, 3 * CONV + QR:], KVR + ROPE)[0],
        "w_heads": np.concatenate([wq, wk], axis=2), "w_v": wv,
        "w_out_e": _panels(w_out_e[0], 512), "w_in_o": _panels(w_in_o[0], 512), "w_out_o": _panels(w_out_o[0], 512),
        "w_s_t": w_s[0].transpose(2, 0, 1), "b_s": b_s[0].reshape(1, SGG * P),
        "w_router": router.reshape(DEPTH, KD, P, NG + E).transpose(0, 2, 1, 3),
        "w_gate": w_gate, "w_up": w_up, "w_down": w_down,
        "w_ple_gate": np.stack([_panels(w, 512) for w in w_ple_gate]),
        "w_ple_proj": np.stack([_panels(w, 512) for w in w_ple_proj]),
        "p_t": p[:, 0].reshape(DEPTH, T, 2, P).transpose(0, 3, 2, 1),
    }


def kernel(**inputs):
    import concourse.bacc as _bacc
    from concourse.bass_utils import run_bass_kernel_spmd as _run

    nc = _bacc.Bacc("TRN2", target_bir_lowering=False, num_devices=1)
    arrays = {n: np.ascontiguousarray(a) for n, a in _layout(**{k: np.asarray(v) for k, v in inputs.items()}).items()}
    aps = {n: nc.dram_tensor(n, a.shape, mybir.dt.from_np(a.dtype), kind="ExternalInput").ap()
           for n, a in arrays.items()}
    out = nc.dram_tensor("out_0", (T, D), F32, kind="ExternalOutput").ap()
    program(nc, aps, out)
    r = _run(nc, [arrays], core_ids=[0])
    return r.results[0]["out_0"].reshape(1, T, D)
```

```python
from contextlib import ExitStack

import numpy as np

import concourse.bass as bass
from concourse import mybir

F32 = mybir.dt.float32
F32R = mybir.dt.float32r
I32 = mybir.dt.int32
BF16 = mybir.dt.bfloat16
ALU = mybir.AluOpType
ACT = mybir.ActivationFunctionType
AXX = mybir.AxisListType.X

P = 128
D = 1024
T = 1024
NT = T // P
KD = D // P
DEPTH = 2
EPS = 1e-6
NEG = -1e30
CONV = 512
QR, KVR = 384, 256
H, NOPE, ROPE, VD = 8, 64, 32, 64
DQK = NOPE + ROPE
E, NG, EG, F = 32, 4, 8, 512
SG, SGG = 1024, 8
ROWS = 3
UNIT = 2048
RING = 6
SPLIT = 4
OVB = 2 * T // P - 1
NB = E + OVB
EMPTY = 8192
SCALE = float(DQK) ** -0.5
SBUF_END = 229344
TWO_PI_HI, TWO_PI_LO = 6.28125, 0.0019353071795864769
PI = 3.141592653589793

C_QN, C_KVN, C_VN, C_CONV, C_ROPE = 0, 3, 5, 13, 25
N_COLS = C_ROPE + 2


class Tally:

    def __init__(self, sem):
        self.sem, self.base, self.k = sem, 0, 0

    def inc(self, ins, n=1):
        ins.then_inc(self.sem, n)
        self.k += n
        return self.value()

    def value(self):
        return self.base + self.k

    def link(self, eng, ins):
        eng.wait_ge(self.sem, self.inc(ins))

    def enter(self, i, per):
        self._start, self._per = self.value(), per
        self.base, self.k = i * per + self._start, 0

    def leave(self, turns):
        assert self.k == self._per, (self.k, self._per)
        self.base, self.k = self._start + turns * self._per, 0


class Count:

    def __init__(self, sem, base):
        self.sem, self.base = sem, base

    def __call__(self, n):
        return self.sem, n + self.base


def program(nc, A, out):
    with ExitStack() as ctx:
        names = {}

        def sem(name):
            assert name not in names, name
            names[name] = ctx.enter_context(nc.semaphore(name))
            return names[name]

        counts = {}

        def count(name, total):
            c, at = counts.get(name) or (sem(name), 0)
            counts[name] = c, at + total
            return Count(c, at)

        top = [(nc.sbuf_base + 63) // 64 * 64]

        def keep(name, shape, dt=F32):
            t = nc.alloc_sbuf_tensor_at(name, shape, dt, offset=top[0])
            top[0] += (int(np.prod(shape[1:])) * 4 + 31) // 32 * 32
            return t

        h = keep("h", [P, NT, D])
        ring = keep("ring", [P, RING, UNIT])
        ident = keep("ident", [P, P])
        ones = keep("ones", [P, P])
        causal = keep("causal", [P, P])
        ones_b = keep("ones_b", [P, P], BF16)
        before_b = keep("before_b", [P, P], BF16)
        cols = keep("cols", [P, N_COLS])
        wr = keep("wr", [P, KD, NG + E])
        ss = keep("ss", [P, NT])
        rstd = keep("rstd", [P, NT])
        eps_c = keep("eps_c", [P, 1])
        idx_y = keep("idx_y", [P, NB], I32)
        idx_x = keep("idx_x", [P, NB], I32)
        ov_e = keep("ov_e", [P, OVB + 1], I32)
        w_tok = keep("w_tok", [P, 2 * NT])
        gain = keep("gain", [P, D])
        fence = keep("fence", [P, 10])
        ARENA = top[0]

        class Arena:
            def __init__(self, tag):
                self.tag, self.at = tag, ARENA

            def __call__(self, name, shape, dt=F32):
                t = nc.alloc_sbuf_tensor_at(f"{self.tag}_{name}", shape, dt, offset=self.at)
                self.at += (int(np.prod(shape[1:])) * 4 + 31) // 32 * 32
                assert self.at <= SBUF_END, (name, self.at - SBUF_END)
                return t

        banks = ctx.enter_context(nc.psum_tensor("banks", [P, 8 * 512], F32))

        def bank(b, n=1):
            return banks[:, b * 512:(b + n) * 512]

        xn_dram = nc.dram_tensor("xn_dram", (T, D), F32, kind="Internal").ap()
        y_dram = nc.dram_tensor("y_dram", (2 * T, D), F32, kind="Internal").ap()

        act_chain = Tally(sem("act_chain"))
        dve_chain = Tally(sem("dve_chain"))
        pool_chain = Tally(sem("pool_chain"))
        s_const = sem("s_const")
        s_load = sem("s_load")
        s_x = [sem(f"s_x{n}") for n in range(4)]
        ring_full = [sem(f"ring_full{i}") for i in range(RING)]
        unit_pe = sem("unit_pe")
        unit_dve = sem("unit_dve")

        class Stream:

            def __init__(self):
                self.owner = []
                self.n_pe = self.n_dve = 0

            def dense(self, n):
                first = len(self.owner)
                for _ in range(n):
                    self.n_pe += 1
                    self.owner.append((unit_pe, self.n_pe))
                return first

            def expert(self, n):
                first = len(self.owner)
                for _ in range(n):
                    self.n_dve += 1
                    self.owner.append((unit_dve, self.n_dve))
                return first

            def wait_free(self, sp, u):
                if u >= RING:
                    sp.wait_ge(*self.owner[u - RING])

        stream = Stream()

        def full(eng, u):
            eng.wait_ge(ring_full[u % RING], 16 * (u // RING + 1))

        def load_unit(sp, u, src, n, parts=P):
            stream.wait_free(sp, u)
            sp.dma_start(ring[:, u % RING, 0:n], src).then_inc(ring_full[u % RING], 16)

        class NormTranspose:

            prior = None

            def __init__(self, gain_row, xt, xn, ready, store=None):
                self.gain_row, self.xt, self.xn, self.ready, self.store = gain_row, xt, xn, ready, store
                self.prior, NormTranspose.prior = NormTranspose.prior, self
                self.nbuf = xn.shape[1]
                self.s_g = count("norm_gain", 16)
                self.s_ss = count("norm_squares", NT)
                self.s_mean = count("norm_mean", 2)
                self.s_root = count("norm_root", 2)
                self.s_xn = count("norm_xn", NT)
                self.s_tr = count("norm_tr", 2 * NT)
                self.s_evA = count("norm_evA", NT)
                self.s_evD = count("norm_evD", NT)
                self.s_st = [count(f"norm_store{i}", 16 * NT // self.nbuf) for i in range(self.nbuf)] \
                    if store is not None else None
                self.done = [self.s_evA(NT), self.s_evD(NT)]

            def sp(self, sp):
                if self.prior:
                    sp.wait_ge(*self.prior.s_xn(NT))
                sp.dma_start(gain[:], self.gain_row.partition_broadcast(P)).then_inc(self.s_g.sem, 16)

            def sp_store(self, sp):
                for t in range(NT):
                    sp.wait_ge(*self.s_xn(t + 1))
                    sp.dma_start(self.store[t * P:(t + 1) * P, :], self.xn[:, t % self.nbuf, :])\
                      .then_inc(self.s_st[t % self.nbuf].sem, 16)

            def act(self, act, last=None):
                def square(t):
                    act.wait_ge(*self.ready(t))
                    if t:
                        act.wait_ge(*self.s_ss(t))
                    act.activation(bank(2, 2), h[:, t, :], ACT.Square, accum_out=ss[:, t:t + 1])\
                       .then_inc(self.s_ss.sem, 1)

                def root(n):
                    act.wait_ge(*self.s_mean(n + 1))
                    act.activation(rstd[:, 4 * n:4 * n + 4], rstd[:, 4 * n:4 * n + 4], ACT.Sqrt)\
                       .then_inc(self.s_root.sem, 1)

                def out(t):
                    act.wait_ge(*self.s_tr(2 * t + 1))
                    act.activation(self.xt[:, 0:4, t * P:(t + 1) * P],
                                   bank(2 * (t % 2)).rearrange("p (k c) -> p k c", c=P),
                                   ACT.Copy).then_inc(self.s_evA.sem, 1)

                for t in range(NT):
                    if last:
                        last(t)
                    if t >= 1:
                        square(t - 1)
                    if t == 5:
                        root(0)
                square(NT - 1)
                out(0)
                root(1)
                for t in range(1, NT):
                    out(t)

            def dve(self, dve, last=None):
                def mean(n):
                    dve.wait_ge(*self.s_ss(4 * n + 4))
                    dve.tensor_scalar(rstd[:, 4 * n:4 * n + 4], ss[:, 4 * n:4 * n + 4], 1.0 / D, EPS,
                                      ALU.mult, ALU.add).then_inc(self.s_mean.sem, 1)

                def invert(n):
                    dve.wait_ge(*self.s_root(n + 1))
                    dve_chain.link(dve, dve.reciprocal(rstd[:, 4 * n:4 * n + 4], rstd[:, 4 * n:4 * n + 4]))

                def scale(t):
                    b = t % self.nbuf
                    if t >= self.nbuf:
                        dve.wait_ge(*self.s_tr(2 * (t - self.nbuf + 1)))
                        if self.s_st:
                            dve.wait_ge(*self.s_st[b](16 * (t // self.nbuf)))
                    dve.scalar_tensor_tensor(self.xn[:, b, :], h[:, t, :], rstd[:, t:t + 1], gain[:],
                                             ALU.mult, ALU.mult).then_inc(self.s_xn.sem, 1)

                def out(t):
                    dve.wait_ge(*self.s_tr(2 * t + 2))
                    dve.tensor_copy(self.xt[:, 4:8, t * P:(t + 1) * P],
                                    bank(2 * (t % 2) + 1).rearrange("p (k c) -> p k c", c=P))\
                       .then_inc(self.s_evD.sem, 1)

                last = last or (lambda t: None)
                for t in range(5):
                    last(t)
                mean(0)
                last(5)
                invert(0)
                dve.wait_ge(*self.s_g(16))
                scale(0)
                last(6)
                scale(1)
                last(7)
                scale(2)
                mean(1)
                out(0)
                scale(3)
                invert(1)
                for t in range(1, NT):
                    out(t)
                    if t + 3 < NT:
                        scale(t + 3)

            def pe(self, pe):
                for t in range(NT):
                    pe.wait_ge(*self.s_xn(t + 1))
                    if t == 1:
                        pe.wait_ge(*self.s_ss(NT))
                    for half in range(2):
                        if t >= 2:
                            pe.wait_ge(*(self.s_evA, self.s_evD)[half](t - 1))
                        for k in range(4):
                            ins = pe.transpose(bank(2 * (t % 2) + half)[:, k * P:(k + 1) * P],
                                               self.xn[:, t % self.nbuf, (4 * half + k) * P:(4 * half + k + 1) * P],
                                               ident[:])
                        ins.then_inc(self.s_tr.sem, 1)

        class TokenMajor:

            def __init__(self, tag, xt, panels, kd, width, first_bank=4, nbanks=4):
                self.xt, self.panels, self.kd, self.width = xt, panels, kd, width
                self.units = [stream.dense(2) for _ in panels]
                self.b0, self.nb = first_bank, nbanks
                self.n = len(panels) * NT
                self.s_mm = count("out_mm", self.n)
                self.s_take = count("out_take", self.n)

            def sp(self, sp):
                for u, src in zip(self.units, self.panels):
                    for half in range(2):
                        load_unit(sp, u + half, src[:, half * UNIT:(half + 1) * UNIT], UNIT)

            def pe(self, pe, ready):
                for s, v in ready:
                    pe.wait_ge(s, v)
                for c, u in enumerate(self.units):
                    for t in range(NT):
                        g = c * NT + t
                        if g >= self.nb:
                            pe.wait_ge(*self.s_take(g - self.nb + 1))
                        for k in range(self.kd):
                            if t == 0 and k % 4 == 0:
                                full(pe, u + k // 4)
                            w = ring[:, (u + k // 4) % RING, (k % 4) * 512:(k % 4 + 1) * 512]
                            ins = pe.matmul(bank(self.b0 + g % self.nb), self.xt[:, k, t * P:(t + 1) * P], w,
                                            start=(k == 0), stop=(k == self.kd - 1))
                        ins.then_inc(self.s_mm.sem, 1)

            def bank_of(self, g):
                return bank(self.b0 + g % self.nb)

        def setup_sp(sp):
            for n in range(4):
                sp.dma_start(h[:, 2 * n:2 * n + 2, :], A["x"].rearrange("(t p) d -> p t d", p=P)[:, 2 * n:2 * n + 2, :])\
                  .then_inc(s_x[n], 16)
            sp.dma_start(cols[:], A["cols"]).then_inc(s_load, 16)

        def setup_pool(pool):
            pool.memset(ident[:], 0.0).then_inc(pool_chain.sem, 1)
            pool.memset(ones[:], 1.0).then_inc(pool_chain.sem, 1)
            pool.memset(before_b[:], 1.0).then_inc(pool_chain.sem, 1)
            pool.memset(ones_b[:], 1.0).then_inc(pool_chain.sem, 1)
            pool.memset(causal[:], 0.0).then_inc(pool_chain.sem, 1)
            pool.memset(fence[:], 0.0).then_inc(pool_chain.sem, 1)
            pool.memset(eps_c[:], EPS).then_inc(pool_chain.sem, 1)
            pool_chain.k += 7
            pool.wait_ge(pool_chain.sem, 7)
            pool.affine_select(out=ident[:], in_=ident[:], compare_op=ALU.not_equal, fill=1.0, base=0,
                               pattern=[[-1, P]], channel_multiplier=1).then_inc(s_const, 1)
            pool.affine_select(out=before_b[:], in_=before_b[:], compare_op=ALU.is_gt, fill=0.0, base=0,
                               pattern=[[1, P]], channel_multiplier=-1).then_inc(s_const, 1)
            pool.affine_select(out=causal[:], in_=causal[:], compare_op=ALU.is_ge, fill=NEG, base=0,
                               pattern=[[-1, P]], channel_multiplier=1).then_inc(s_const, 1)

        CONSTS = [(s_const, 3)]

        a0 = Arena("mix0")
        xt0 = a0("xt", [P, KD, T])
        yt0 = a0("yt", [P, KD, T])
        cq = a0("cq", [P, 3, T])
        ckv = a0("ckv", [P, 2, T])
        trig = a0("trig", [P, 2, T])
        qk = a0("qk", [P, 4, T])
        rt = a0("rt", [P, 2, T])
        wh = a0("wh", [P, 2, 3 * DQK + 2 * NOPE])
        lrow = a0("lrow", [P, 3 * NT])
        ytok = xt0[:, 0:4, :].rearrange("p a b -> p (a b)").rearrange("p (t c) -> p t c", c=H * VD)
        pt = xt0[:, 4:6, :]
        vals = [z[:, 6:8, :].rearrange("p a b -> p (a b)").rearrange("p (t c) -> p t c", c=H * VD)
                for z in (xt0, yt0)]
        prob = yt0[:, 4:6, :]
        posi = yt0[:, 0, :].bitcast(I32)
        ZB, AB, GB = yt0[:, 4, :], yt0[:, 5, :], yt0[:, 6, :]
        REG = slice(64, 96)

        norm0 = NormTranspose(A["norm_mix"][0:1, :], xt0, qk, lambda t: (s_x[t // 2], 16))

        IN_W = [3 * P, KVR + ROPE] + [3 * P] * 4
        in_units = [stream.dense(2) for _ in IN_W]
        wv_unit = stream.dense(1)
        s_in = sem("s_in")
        s_in_a = sem("s_in_a")
        s_in_d = sem("s_in_d")
        s_trig = sem("s_trig")
        s_pos = sem("s_pos")
        s_sq = sem("s_sq")
        s_latn = sem("s_latn")
        s_wh = [sem("s_wh0"), sem("s_wh1")]
        s_v = sem("s_v")
        s_va, s_vd = sem("s_va"), sem("s_vd")
        s_proj = sem("s_proj")
        s_qkv = sem("s_qkv")
        s_rope = sem("s_rope")
        s_sc = sem("s_sc")
        s_max = sem("s_max")
        s_exp = sem("s_exp")
        s_ptr = sem("s_ptr")
        s_pta = sem("s_pta")
        s_ptd = sem("s_ptd")
        s_pv = sem("s_pv")
        s_o = sem("s_o")
        s_yt = sem("s_yt")
        s_yte = sem("s_yte")

        def in_sp(sp):
            sp.dma_start(posi[REG, :], A["positions"].partition_broadcast(32)).then_inc(s_pos, 16)
            for n, (u, w) in enumerate(zip(in_units, IN_W)):
                src = A["w_in_kv"] if n == 1 else A["w_in_e"][4 if n == 0 else n - 2]
                for half in range(2):
                    load_unit(sp, u + half, src[:, half * 4 * w:(half + 1) * 4 * w], 4 * w)
                if n == 1:
                    for b in range(2):
                        sp.dma_start(wh[:, b, :], A["w_heads"][b]).then_inc(s_wh[b], 16)
            load_unit(sp, wv_unit, A["w_v"], 2 * H * VD)

        GROUPS = []
        for n in range(6):
            GROUPS += [("in", n, b, hf) for b in range(3) for hf in range(2)]
            if n == 2:
                GROUPS += [("sq", m, hf) for m in range(2) for hf in range(2)]
            if n == 3:
                GROUPS += [("head", m, hf) for m in range(2) for hf in range(2)]

        def place(*group):
            return GROUPS.index(group)

        reader, a_read, d_read = {}, 0, 0
        for g, group in enumerate(GROUPS):
            if group[0] == "in" and group[1] >= 2 and group[2] < 2:
                d_read += 1
                reader[g] = (s_in_d, d_read)
            else:
                a_read += 1
                reader[g] = (s_in_a, a_read)

        LAT = [(cq, 3, QR, C_QN, [qk[:, 0, :], qk[:, 1, :], qk[:, 2, :]]),
               (ckv, 2, KVR, C_KVN, [qk[:, 3, :], yt0[:, 7, :]])]
        WQ = 3 * DQK

        def head_product(pe, dst, m, hf, b):
            rank, nk, first, step, w = ((cq, 3, 0, DQK, DQK), (ckv, 2, WQ, NOPE, NOPE))[m]
            for k in range(nk):
                ins = pe.matmul(dst[0:w, :], wh[:, b, first + k * step:first + k * step + w],
                                rank[:, k, hf * 512:(hf + 1) * 512], start=(k == 0), stop=(k == nk - 1))
            return ins

        def head_copy(act, src, m, hf, b):
            sl = slice(hf * 512, (hf + 1) * 512)
            if m == 0:
                return act.activation(qk[0:DQK, b, sl], src[0:DQK, :], ACT.Copy, scale=SCALE)
            return act.activation(qk[0:NOPE, 2 + b, sl], src[0:NOPE, :], ACT.Copy)

        def in_pe(pe):
            for s, v in norm0.done:
                pe.wait_ge(s, v)
            for g, group in enumerate(GROUPS):
                if g >= 8:
                    pe.wait_ge(*reader[g - 8])
                if group[0] == "in":
                    n, b, hf = group[1:]
                    u, w = in_units[n], IN_W[n]
                    m = ROPE if (n, b) == (1, 2) else P
                    po = 64 if m == ROPE else 0
                    for k in range(KD):
                        if b == 0 and hf == 0 and k % 4 == 0:
                            full(pe, u + k // 4)
                        lhs = ring[:, (u + k // 4) % RING, (k % 4) * w + b * P:(k % 4) * w + b * P + m]
                        ins = pe.matmul(bank(g % 8)[po:po + m, :], lhs, xt0[:, k, hf * 512:(hf + 1) * 512],
                                        start=(k == 0), stop=(k == KD - 1))
                elif group[0] == "sq":
                    m, hf = group[1:]
                    pe.wait_ge(s_sq, 5)
                    squares = LAT[m][4]
                    for k, src in enumerate(squares):
                        ins = pe.matmul(bank(g % 8), ones[:], src[:, hf * 512:(hf + 1) * 512],
                                        start=(k == 0), stop=(k == len(squares) - 1))
                else:
                    m, hf = group[1:]
                    pe.wait_ge(s_latn, 5)
                    pe.wait_ge(s_wh[0], 16)
                    ins = head_product(pe, bank(g % 8), m, hf, 0)
                ins.then_inc(s_in, 1)
                if group[0] == "in" and group[2:] == (2, 1):
                    pe.wait_ge(s_in, g + 1)
                    pe.nop().then_inc(unit_pe, 2)

        def in_act(act):
            for g, group in enumerate(GROUPS):
                if g in reader and reader[g][0] is s_in_d:
                    continue
                hf = group[-1]
                sl = slice(hf * 512, (hf + 1) * 512)
                src = bank(g % 8)
                if group[0] == "in":
                    n, b = group[1:3]
                    act.wait_ge(s_in, g + 1)
                    if n == 0:
                        dst = cq[:, b, sl]
                    elif n == 1:
                        dst, src = (ckv[:, b, sl], src) if b < 2 else (rt[REG, 0, sl], src[REG, :])
                    else:
                        if n > 2 and hf == 0:
                            act.wait_ge(s_in_d, 4 * (n - 2) - 2)
                        dst = GB[:, sl]
                    ins = act.activation(dst, src, ACT.Copy)
                elif group[0] == "sq":
                    m = group[1]
                    act.wait_ge(s_in, place("sq", m, 1) + 1)
                    ins = act.activation(qk[:, m, sl], src, ACT.Sqrt, scale=1.0 / LAT[m][2], bias=eps_c[:])
                else:
                    act.wait_ge(s_in, g + 1)
                    ins = head_copy(act, src, group[1], hf, 0)
                ins.then_inc(s_in_a, 1)
                if group == ("in", 0, 2, 1):
                    trig_act(act)
                if group == ("in", 1, 2, 1):
                    act.wait_ge(*reader[g])
                    for c, nk, _, _, squares in LAT:
                        for k in range(nk):
                            act.activation(squares[k], c[:, k, :], ACT.Square).then_inc(s_sq, 1)

        def conv_dve(dve, n):
            wc = C_CONV + 3 * n
            dve.wait_ge(*reader[place("in", 2 + n, 2, 1)])
            for hf in range(2):
                sl = slice(hf * 512, (hf + 1) * 512)
                dve.tensor_tensor(ZB[:, sl], bank(place("in", 2 + n, 0, hf) % 8), GB[:, sl],
                                  ALU.mult).then_inc(s_in_d, 1)
            dve.wait_ge(s_in_d, 4 * n + 2)
            L = dve_chain.link
            L(dve, dve.tensor_scalar(AB[:, :], ZB[:, :], cols[:, wc + 2:wc + 3], None, ALU.mult))
            L(dve, dve.scalar_tensor_tensor(AB[:, 1:T], ZB[:, 0:T - 1], cols[:, wc + 1:wc + 2],
                                            AB[:, 1:T], ALU.mult, ALU.add))
            L(dve, dve.scalar_tensor_tensor(AB[:, 2:T], ZB[:, 0:T - 2], cols[:, wc:wc + 1],
                                            AB[:, 2:T], ALU.mult, ALU.add))
            for hf in range(2):
                sl = slice(hf * 512, (hf + 1) * 512)
                dve.tensor_tensor(yt0[:, n, sl], bank(place("in", 2 + n, 1, hf) % 8), AB[:, sl],
                                  ALU.mult).then_inc(s_in_d, 1)

        def trig_dve(dve):
            ang, k_i, kf, w1 = rt[REG, 1, :], yt0[REG, 1, :].bitcast(I32), trig[REG, 1, :], trig[REG, 0, :]
            L = dve_chain.link
            dve.wait_ge(s_pos, 16)
            L(dve, dve.tensor_copy(w1, posi[REG, :]))
            L(dve, dve.tensor_scalar(ang, w1, cols[REG, C_ROPE:C_ROPE + 1], None, ALU.mult))
            L(dve, dve.tensor_scalar(w1, ang, 1.0 / (2 * PI), None, ALU.mult))
            L(dve, dve.tensor_copy(k_i, w1))
            L(dve, dve.tensor_copy(kf, k_i))
            L(dve, dve.scalar_tensor_tensor(ang, kf, -TWO_PI_HI, ang, ALU.mult, ALU.add))
            L(dve, dve.scalar_tensor_tensor(ang, kf, -TWO_PI_LO, ang, ALU.mult, ALU.add))

            def wrap(x, tmp):
                L(dve, dve.tensor_scalar(tmp, x, PI, -2 * PI, ALU.is_gt, ALU.mult))
                L(dve, dve.tensor_tensor(x, x, tmp, ALU.add))
                L(dve, dve.tensor_scalar(tmp, x, -PI, 2 * PI, ALU.is_lt, ALU.mult))
                L(dve, dve.tensor_tensor(x, x, tmp, ALU.add))

            wrap(ang, kf)
            L(dve, dve.tensor_scalar(w1, ang, PI / 2, None, ALU.add))
            wrap(w1, kf)
            L(dve, dve.tensor_scalar(w1, w1, 3.1415925, -3.1415925, ALU.min, ALU.max))
            dve.tensor_scalar(ang, ang, 3.1415925, -3.1415925, ALU.min, ALU.max).then_inc(s_trig, 1)

        def trig_act(act):
            act.wait_ge(s_trig, 1)
            act.activation(trig[REG, 0, :], trig[REG, 0, :], ACT.Sin).then_inc(s_trig, 1)
            act.activation(trig[REG, 1, :], rt[REG, 1, :], ACT.Sin).then_inc(s_trig, 1)

        def latent_dve(dve):
            for m, (c, nk, _, col, _) in enumerate(LAT):
                dve.wait_ge(*reader[place("sq", m, 1)])
                dve_chain.link(dve, dve.reciprocal(qk[:, m, :], qk[:, m, :]))
                for k in range(nk):
                    dve.scalar_tensor_tensor(c[:, k, :], c[:, k, :], cols[:, col + k:col + k + 1],
                                             qk[:, m, :], ALU.mult, ALU.mult).then_inc(s_latn, 1)
            L = dve_chain.link
            dve.wait_ge(s_trig, 3)
            L(dve, dve.tensor_scalar(trig[REG, 1, :], trig[REG, 1, :], cols[REG, C_ROPE + 1:C_ROPE + 2], None,
                                     ALU.mult))
            L(dve, dve.stream_shuffle(rt[REG, 1, :], rt[REG, 0, :], [(j + 16) % 32 for j in range(32)]))
            L(dve, dve.tensor_tensor(rt[REG, 1, :], rt[REG, 1, :], trig[REG, 1, :], ALU.mult))
            L(dve, dve.tensor_tensor(rt[REG, 0, :], rt[REG, 0, :], trig[REG, 0, :], ALU.mult))
            dve.tensor_tensor(qk[REG, 2, :], rt[REG, 0, :], rt[REG, 1, :], ALU.add).then_inc(s_rope, 1)
            dve.tensor_tensor(qk[REG, 3, :], rt[REG, 0, :], rt[REG, 1, :], ALU.add).then_inc(s_rope, 1)
            dve.wait_ge(s_rope, 2)

        def rope_step(dve, b, n):
            if n == 0:
                ins = dve.tensor_tensor(rt[REG, 0, :], qk[REG, b, :], trig[REG, 0, :], ALU.mult)
            elif n == 1:
                ins = dve.stream_shuffle(rt[REG, 1, :], qk[REG, b, :], [(j + 16) % 32 for j in range(32)])
            elif n == 2:
                ins = dve.tensor_tensor(rt[REG, 1, :], rt[REG, 1, :], trig[REG, 1, :], ALU.mult)
            else:
                dve.tensor_tensor(qk[REG, b, :], rt[REG, 0, :], rt[REG, 1, :], ALU.add).then_inc(s_rope, 1)
                return
            dve_chain.link(dve, ins)

        def in_dve(dve):
            dve.wait_ge(s_load, 16)
            trig_dve(dve)
            conv_dve(dve, 0)
            latent_dve(dve)
            conv_dve(dve, 1)
            dve.wait_ge(*reader[place("head", 0, 1)])
            for n in range(4):
                rope_step(dve, 0, n)
            conv_dve(dve, 2)
            conv_dve(dve, 3)

        def values_pe(pe):
            full(pe, wv_unit)
            for t in range(NT):
                if t < 4:
                    for g in range(len(GROUPS) - 8, len(GROUPS)):
                        if g % 8 == t:
                            pe.wait_ge(*reader[g])
                else:
                    pe.wait_ge((s_va, s_vd)[t % 2], (t - 4) // 2 + 1)
                for k in range(2):
                    ins = pe.matmul(bank(t % 4), ckv[:, k, t * P:(t + 1) * P],
                                    ring[:, wv_unit % RING, k * 512:(k + 1) * 512], start=(k == 0), stop=(k == 1))
                ins.then_inc(s_v, 1)
            for g in range(len(GROUPS) - 8, len(GROUPS)):
                pe.wait_ge(*reader[g])
            pe.wait_ge(s_v, NT)
            pe.nop().then_inc(unit_pe, 1)

        def values_out(eng, write, parity, s_done):
            eng.wait_ge(s_in_d, d_read)
            for t in range(parity, NT, 2):
                eng.wait_ge(s_v, t + 1)
                write(vals[t // 4][:, t % 4, :], bank(t % 4)).then_inc(s_done, 1)

        FILL = (1, 1, 1, 3)
        TURNS = H // 2
        STEPS = 2 * NT

        def ahead(eng, *sems):
            for s in sems:
                eng.nop().then_inc(s, 1)

        PT_GROUPS = []
        for n in range(STEPS):
            for j0 in range(0, n % NT + 1, 4):
                PT_GROUPS.append((n, j0, min(4, n % NT + 1 - j0), len(PT_GROUPS)))
        GT = len(PT_GROUPS)

        def groups_through(n):
            return sum(1 for x in PT_GROUPS if x[0] <= n)

        def turns(eng, turn):
            with eng.Fori(0, TURNS - 1) as i:
                turn(i, False)
            turn(TURNS - 1, True)

        def att_sp(sp):
            sp.wait_ge(s_in, place("head", 1, 1) + 1)
            sp.dma_start(wh[:, 0, :], A["w_heads"][2]).then_inc(s_wh[0], 16)
            with sp.Fori(0, TURNS - 2) as i:
                for u in range(2):
                    sp.wait_ge(s_proj, 8 * i + (4 * u + 4))
                    sp.dma_start(wh[:, 1 - u, :], A["w_heads"][bass.ds(2 * i + (u + 3), 1)]
                                 .rearrange("a p c -> (a p) c")).then_inc(s_wh[1 - u], 16)
            sp.wait_ge(s_proj, 8 * (TURNS - 2) + 4)
            sp.dma_start(wh[:, 1, :], A["w_heads"][H - 1]).then_inc(s_wh[1], 16)

        def att_pe(pe):
            ahead(pe, s_ptr, s_pv)

            def scores(i, n, last=False):
                u, b = n // NT % 2, n % NT
                if b in (4, 5) and not (last and u == 1):
                    pe.wait_ge(s_qkv, 8 * i + (4 * u + b))
                if n >= 1:
                    pe.wait_ge(s_exp, STEPS * i + (n - 1 + 1))
                if b == 0 and n > 0:
                    pe.wait_ge(s_qkv, 8 * i + (4 * (n // NT) + 1))
                    pe.wait_ge(s_rope, 2 * i + (n // NT + 3))
                for c in range(0, (b + 1) * P, 512):
                    w = min(512, (b + 1) * P - c)
                    dst = bank(2 * (n % 2), 2)[:, c:c + w]
                    last = c + w == (b + 1) * P
                    ins = pe.matmul(dst, qk[0:DQK, u, b * P:(b + 1) * P], qk[0:DQK, 2 + u, c:c + w],
                                    start=True, stop=not last)
                pe.matmul(dst[:, w - P:w], ident[:], causal[:], start=False, stop=True).then_inc(s_sc, 1)

            def turn(i, last):
                for n in range(STEPS):
                    u, b = n // NT, n % NT
                    if not (last and n + 1 == STEPS):
                        scores(i, n + 1, last)
                    if b < 4 and not (last and u == 1):
                        if b == 0:
                            pe.wait_ge(s_wh[1 - u], 16 * i + 16 * (1 + u))
                        pe.wait_ge(s_qkv, 8 * i + (4 * u + b + 1))
                        head_product(pe, bank(FILL[b]), b // 2, b % 2, 1 - u).then_inc(s_proj, 1)
                    pe.wait_ge(s_exp, STEPS * i + (n + 2))
                    for nn, j0, cnt, g in PT_GROUPS:
                        if nn == n:
                            pe.wait_ge((s_pta, s_ptd)[g % 2], GT // 2 * i + (g // 2 + 1))
                            for j in range(j0, j0 + cnt):
                                ins = pe.transpose(bank(4 + g % 2)[:, (j - j0) * P:(j - j0 + 1) * P],
                                                   prob[:, n % 2, j * P:(j + 1) * P], ident[:])
                            ins.then_inc(s_ptr, 1)
                    if n >= 1:
                        weigh(i, n - 1)
                weigh(i, STEPS - 1)

            def weigh(i, n):
                u, b = n // NT, n % NT
                for nn, _, _, g in PT_GROUPS:
                    if nn == n:
                        pe.wait_ge((s_pta, s_ptd)[g % 2], GT // 2 * i + (g // 2 + 2))
                pe.wait_ge(s_o, STEPS * i + max(n, 1))
                for j in range(b + 1):
                    ins = pe.matmul(bank(6 + n % 2)[:, 0:VD], pt[:, n % 2, j * P:(j + 1) * P],
                                    vals[j // 4][:, j % 4, bass.ds(2 * VD * i + VD * u, VD)],
                                    start=(j == 0), stop=(j == b))
                ins.then_inc(s_pv, 1)

            pe.wait_ge(*reader[place("head", 1, 1)])
            pe.wait_ge(s_rope, 3)
            pe.wait_ge(s_va, NT // 2)
            pe.wait_ge(s_vd, NT // 2)
            scores(0, 0)
            turns(pe, turn)

        def pt_out(eng, write, parity, s_done, i, n):
            for nn, j0, cnt, g in PT_GROUPS:
                if nn == n and g % 2 == parity:
                    eng.wait_ge(s_ptr, GT * i + (g + 2))
                    eng.wait_ge(s_pv, STEPS * i + (max(n - 1, 0) + 1))
                    write(pt[:, n % 2, j0 * P:(j0 + cnt) * P], bank(4 + g % 2)[:, 0:cnt * P]).then_inc(s_done, 1)

        def att_act(act):
            ahead(act, s_qkv, s_exp, s_pta)

            def exps(i, n):
                act.wait_ge(s_max, STEPS * i + (n + 1))
                if n >= 1:
                    act.wait_ge(s_ptr, GT * i + (groups_through(n - 2) + 1))
                u, b = n // NT % 2, n % NT
                w = (b + 1) * P
                act.activation(prob[:, n % 2, 0:w], bank(2 * (n % 2), 2)[:, 0:w], ACT.Exp,
                               bias=lrow[:, 2 * NT + b:2 * NT + b + 1],
                               accum_out=lrow[:, u * NT + b:u * NT + b + 1]).then_inc(s_exp, 1)

            def turn(i, last):
                for n in range(STEPS):
                    u, b = n // NT, n % NT
                    if not (last and n + 1 == STEPS):
                        exps(i, n + 1)
                    pt_out(act, lambda o, x: act.activation(o, x, ACT.Copy), 0, s_pta, i, n)
                    if b < 4 and not (last and u == 1):
                        act.wait_ge(s_proj, 8 * i + (4 * u + b + 1))
                        head_copy(act, bank(FILL[b]), b // 2, b % 2, 1 - u).then_inc(s_qkv, 1)

            exps(0, 0)
            turns(act, turn)

        def att_dve(dve):
            ahead(dve, s_ptd, s_o)
            L = dve_chain.link

            def row_max(i, n):
                b = n % NT
                dve.wait_ge(s_sc, STEPS * i + (n + 1))
                dve.tensor_reduce(lrow[:, 2 * NT + b:2 * NT + b + 1], bank(2 * (n % 2), 2)[:, 0:(b + 1) * P],
                                  axis=AXX, op=ALU.max, negate=True).then_inc(s_max, 1)

            def norm_out(i, n):
                u, b = n // NT, n % NT
                total = lrow[:, u * NT + b:u * NT + b + 1]
                L(dve, dve.reciprocal(total, total))
                dve.wait_ge(s_pv, STEPS * i + (n + 2))
                dve.tensor_scalar(ytok[:, b, bass.ds(2 * VD * i + VD * u, VD)], bank(6 + n % 2)[:, 0:VD],
                                  total, None, ALU.mult).then_inc(s_o, 1)

            def turn(i, last):
                for n in range(STEPS):
                    u, b = n // NT, n % NT
                    if not (last and n + 1 == STEPS):
                        row_max(i, n + 1)
                    pt_out(dve, dve.tensor_copy, 1, s_ptd, i, n)
                    if 3 <= b < 7 and not (last and u == 1):
                        if b == 3:
                            dve.wait_ge(s_qkv, 8 * i + (4 * u + 3))
                        rope_step(dve, 1 - u, b - 3)
                    if n >= 1:
                        norm_out(i, n - 1)
                norm_out(i, STEPS - 1)

            row_max(0, 0)
            with dve.Fori(0, TURNS - 1) as i:
                dve_chain.enter(i, 2 * 3 + STEPS)
                turn(i, False)
            dve_chain.leave(TURNS - 1)
            turn(TURNS - 1, True)

        def yt_pe(pe):
            pe.wait_ge(s_o, 1 + H * NT)
            for t in range(NT):
                if t >= 2:
                    pe.wait_ge(s_yte, t - 1)
                for k in range(4):
                    ins = pe.transpose(bank(t % 2)[:, k * P:(k + 1) * P], ytok[:, t, k * P:(k + 1) * P], ident[:])
                ins.then_inc(s_yt, 1)

        def yt_act(act):
            for t in range(NT):
                act.wait_ge(s_yt, t + 1)
                act.activation(yt0[:, 4:8, t * P:(t + 1) * P], bank(t % 2).rearrange("p (k c) -> p k c", c=P),
                               ACT.Copy).then_inc(s_yte, 1)

        class OutProj:

            def __init__(self, tag, xt, w, ready):
                self.g = TokenMajor(tag, xt, [w[c] for c in range(2)], KD, 512)
                self.ready = ready

            def sp(self, sp):
                self.g.sp(sp)

            def pe(self, pe):
                self.g.pe(pe, self.ready)
                pe.wait_ge(*self.g.s_mm(self.g.n))
                pe.nop().then_inc(unit_pe, 4)

            def tile(self, t):
                return self.g.s_take(NT + t + 1)

            def dve(self, dve, c, t):
                n = c * NT + t
                dve.wait_ge(*self.g.s_mm(n + 1))
                dve.tensor_tensor(h[:, t, c * 512:(c + 1) * 512], h[:, t, c * 512:(c + 1) * 512],
                                  self.g.bank_of(n), ALU.add).then_inc(self.g.s_take.sem, 1)

        out0 = OutProj("out0", yt0, A["w_out_e"], [(s_yte, NT)])

        class Moe:

            def __init__(self, l, ready):
                self.l = l
                tag = self.tag = f"m{l}_"
                a = Arena(tag)
                self.hi = a("hi", [P, SPLIT, UNIT], F32R)
                self.lo = a("lo", [P, SPLIT, UNIT], F32R)
                self.xh = a("xh", [P, 2, D], F32R)
                self.xl = a("xl", [P, 2, D], F32R)
                self.sg = a("sg", [P, F])
                self.hm = a("hm", [P, F])
                self.hh = a("hh", [P, F], F32R)
                self.hl = a("hl", [P, F], F32R)
                self.y = a("y", [P, 2, D])
                self.xf = a("xf", [P, D])
                self.hf = a("hf", [P, F])
                self.ovi = a("ovi", [P, 2], I32)
                self.xg = a("xg", [P, 2, D])
                b = Arena(tag + "r")
                self.xt = b("xt", [P, KD, T])
                self.lgt = b("lgt", [P, T])
                self.lg = b("lg", [P, NT, NG + E])
                self.oh = b("oh", [P, 2, NT, E])
                self.em = b("em", [P, NT, E])
                self.tmp = b("tmp", [P, 2, NT, E])
                self.both = b("both", [P, NT, E], BF16)
                self.small = b("small", [P, 24, NT])
                self.row = b("row", [P, 4, E])
                self.over = b("over", [P, E, T // P - 1])
                self.iog = b("iog", [P, NG])
                self.ioe = b("ioe", [P, E])
                self.iob = b("iob", [P, NB])
                self.ios = b("ios", [P, P])
                self.iot = b("iot", [P, T // P - 1])
                self.part = b("part", [P, 1])
                self.base = b("base", [P, 2, NT])
                self.q_s = b("q_s", [P, 2 * NT, P], BF16)
                self.q_b = b("q_b", [P, 2 * NT, NB])
                self.q_v = b("q_v", [P, 2 * NT, 2, NB], BF16)
                self.tab = b("tab", [P, 3, NB])
                assert b.at <= ARENA + 64 * 1024
                b.at = ARENA + 64 * 1024
                self.xn = b("xn", [P, 4, D])
                self.ovc = b("ovc", [P, OVB, E])
                self.ovf = b("ovf", [P, OVB + 1])
                self.norm = NormTranspose(A["norm_ffn"][l:l + 1, :], self.xt, self.xn, ready, store=xn_dram)
                def S(n, total):
                    return count("moe_" + n, total)

                self.s_io, self.s_wr, self.s_lg = S("iota", 7), S("w_router", 16), S("logits", 3)
                self.s_lt = S("logits_out", 2)
                self.s_exd, self.s_ex = S("exp_in", 2), S("exp", 2)
                self.s_A, self.s_rk, self.s_q = S("chosen", 1), S("ranks", 1), S("one_hots", 1)
                self.s_tab, self.s_rt, self.s_xg = S("table", 1), S("routed", 1), S("x_cleared", 1)
                self.s_gx = [S("gathered0", 8 * E), S("gathered1", 8 * E)]
                self.s_yst = [S("stored0", 8 * E), S("stored1", 8 * E)]
                self.s_xtr, self.s_xh, self.s_xl = S("x_transposed", E), S("x_hi", E), S("x_lo", E)
                self.s_hi, self.s_use = S("w_hi", 6 * E), S("w_used", 6 * E)
                self.s_sg, self.s_hm = S("silu", E), S("hidden", E)
                self.s_htr, self.s_hh, self.s_hl = S("h_transposed", E), S("h_hi", E), S("h_lo", E)
                self.s_ya, self.s_yd = S("y_act", E), S("y_dve", E)
                self.s_of, self.s_ow, self.s_oi, self.s_ox, self.s_op, self.s_oa, self.s_od, self.s_oy = (
                    Count(sem(f"beyond{l}_{n}"), 0)
                    for n in ("free", "weights", "index", "gathered", "pe", "act", "dve", "stored"))
                self.s_odone = S("beyond_done", 1)
                self.s_row = [S(f"row{i}", 16 * len(range(i, NT, ROWS))) for i in range(ROWS)]
                self.s_comb = S("combined", 2 * NT)
                self.first = stream.expert(6 * E)

            def tile(self, t):
                return self.s_comb(2 * t + 2)

            def iotas(self, pool):
                pool.wait_ge(*self.norm.s_tr(1))
                kw = dict(allow_small_or_imprecise_dtypes=True)
                for tile, pat, base, cm in ((self.iog, [[-1, NG]], NG, 0), (self.ioe, [[-1, E]], E, 0),
                                            (self.iob, [[1, NB]], 0, 0), (self.ios, [[1, P]], 0, 0),
                                            (self.iot, [[P, T // P - 1]], P, 0), (self.part, [[0, 1]], 0, 1),
                                            (self.base, [[T, 2], [P, NT]], -EMPTY, 0)):
                    pool.iota(tile[:], pattern=pat, base=base, channel_multiplier=cm, **kw).then_inc(self.s_io.sem, 1)
                pool.memset(self.xg[:], 0.0).then_inc(self.s_xg.sem, 1)

            def route_sp(self, sp):
                if self.l:
                    sp.wait_ge(self.s_lg.sem, 2)
                sp.dma_start(wr[:], A["w_router"][self.l]).then_inc(self.s_wr.sem, 16)

            def route_pe(self, pe):
                for s, v in self.norm.done:
                    pe.wait_ge(s, v)
                pe.wait_ge(*self.s_wr(16))
                for hf in range(2):
                    for k in range(KD):
                        ins = pe.matmul(bank(4 + hf)[0:NG + E, :], wr[:, k, :],
                                        self.xt[:, k, hf * 512:(hf + 1) * 512],
                                        start=(k == 0), stop=(k == KD - 1))
                    ins.then_inc(self.s_lg.sem, 1)
                for t in range(NT):
                    if t % 4 == 0:
                        pe.wait_ge(*self.s_lt(t // 4 + 1))
                    ins = pe.transpose(bank(6)[:, t * (NG + E):(t + 1) * (NG + E)],
                                       self.lgt[0:NG + E, t * P:(t + 1) * P], ident[0:NG + E, 0:NG + E])
                ins.then_inc(self.s_lg.sem, 1)
                pe.wait_ge(*self.s_A(1))
                for t in range(NT):
                    for s in range(t + 1):
                        ins = pe.matmul(bank(5)[:, t * E:(t + 1) * E], before_b[:] if s == t else ones_b[:],
                                        self.both[:, s, :], start=(s == 0), stop=(s == t))
                for t in range(NT):
                    ins = pe.matmul(bank(7)[:, 0:E], ones_b[:], self.both[:, t, :], start=(t == 0),
                                    stop=(t == NT - 1))
                ins.then_inc(self.s_rk.sem, 1)
                pe.wait_ge(*self.s_q(1))
                for n in range(2 * NT):
                    ins = pe.matmul(bank(4)[:, 0:2 * NB], self.q_s[:, n, :],
                                    self.q_v[:, n, :, :].rearrange("p a b -> p (a b)"), start=(n == 0),
                                    stop=(n == 2 * NT - 1))
                ins.then_inc(self.s_tab.sem, 1)

            def route_act(self, act):
                for hf in range(2):
                    act.wait_ge(*self.s_lg(hf + 1))
                    act.activation(self.lgt[0:NG + E, hf * 512:(hf + 1) * 512], bank(4 + hf)[0:NG + E, :],
                                   ACT.Copy).then_inc(self.s_lt.sem, 1)
                act.wait_ge(*self.s_exd(1))
                act.activation(self.small[:, 4:8, :], self.small[:, 4:8, :], ACT.Exp).then_inc(self.s_ex.sem, 1)
                act.wait_ge(*self.s_exd(2))
                act.activation(self.small[:, 10, :], self.small[:, 10, :], ACT.Exp).then_inc(self.s_ex.sem, 1)

            def route_dve(self, dve):
                L = dve_chain.link
                sm, em, tmp = self.small, self.em, self.tmp
                dve.wait_ge(*self.s_io(7))
                dve.wait_ge(*self.s_lg(3))
                L(dve, dve.tensor_copy(self.lg[:].rearrange("p t c -> p (t c)"), bank(6)[:, 0:NT * (NG + E)]))
                gl = self.lg[:, :, 0:NG]
                el = self.lg[:, :, NG:NG + E]

                def bc(v, n):
                    return v.unsqueeze(2).to_broadcast([P, NT, n])

                def rowbc(v, n):
                    return v.unsqueeze(1).to_broadcast([P, NT, n])

                L(dve, dve.reduce_max(sm[:, 0, :], gl, AXX))
                g4 = tmp[:, 0, :, 0:NG]
                L(dve, dve.tensor_tensor(g4, gl, bc(sm[:, 0, :], NG), ALU.is_ge))
                L(dve, dve.tensor_tensor(g4, g4, rowbc(self.iog[:], NG), ALU.mult))
                L(dve, dve.reduce_max(sm[:, 1, :], g4, AXX))
                goh = tmp[:, 0, :, NG:2 * NG]
                L(dve, dve.tensor_tensor(goh, g4, bc(sm[:, 1, :], NG), ALU.is_equal))
                ge = sm[:, 4:8, :].rearrange("p g t -> p t g")
                dve.tensor_tensor(ge, gl, bc(sm[:, 0, :], NG), ALU.subtract).then_inc(self.s_exd.sem, 1)
                L(dve, dve.tensor_scalar(g4, goh, 1.0, -NEG, ALU.subtract, ALU.mult))
                for g in range(NG):
                    sl = slice(g * EG, (g + 1) * EG)
                    ins = dve.tensor_tensor(em[:, :, sl], el[:, :, sl], bc(goh[:, :, g], EG), ALU.mult)
                L(dve, ins)
                for g in range(NG):
                    sl = slice(g * EG, (g + 1) * EG)
                    ins = dve.tensor_tensor(em[:, :, sl], em[:, :, sl], bc(g4[:, :, g], EG), ALU.add)
                L(dve, ins)
                for k in range(2):
                    m, first, oh = sm[:, 2 + k, :], sm[:, 8 + k, :], self.oh[:, k]
                    L(dve, dve.reduce_max(m, em[:], AXX))
                    L(dve, dve.tensor_tensor(tmp[:, k], em[:], bc(m, E), ALU.is_ge))
                    L(dve, dve.tensor_tensor(tmp[:, k], tmp[:, k], rowbc(self.ioe[:], E), ALU.mult))
                    L(dve, dve.reduce_max(first, tmp[:, k], AXX))
                    L(dve, dve.tensor_tensor(oh, tmp[:, k], bc(first, E), ALU.is_equal))
                    if k == 0:
                        L(dve, dve.scalar_tensor_tensor(em[:].rearrange("p t e -> p (t e)"),
                                                        oh.rearrange("p t e -> p (t e)"), 2 * NEG,
                                                        em[:].rearrange("p t e -> p (t e)"), ALU.mult, ALU.add))
                dve.tensor_tensor(self.both[:], self.oh[:, 0], self.oh[:, 1], ALU.add).then_inc(self.s_A.sem, 1)
                dve.tensor_tensor(sm[:, 10, :], sm[:, 3, :], sm[:, 2, :], ALU.subtract).then_inc(self.s_exd.sem, 1)

                def pair(n):
                    return sm[:, n:n + 2, :].rearrange("p k t -> p (k t)")

                rank, exp_, ovs, fl, bk, t2 = (pair(n) for n in (12, 14, 16, 18, 20, 22))
                L(dve, dve.tensor_scalar(exp_, pair(8), -1.0, float(E), ALU.mult, ALU.add))
                dve.wait_ge(*self.s_ex(2))
                L(dve, dve.reduce_sum(sm[:, 11, :], ge, AXX))
                L(dve, dve.tensor_scalar(sm[:, 1, :], sm[:, 10, :], 1.0, None, ALU.add))
                L(dve, dve.tensor_tensor(sm[:, 11, :], sm[:, 11, :], sm[:, 1, :], ALU.mult))
                L(dve, dve.reciprocal(w_tok[:, 0:NT], sm[:, 11, :]))
                L(dve, dve.tensor_tensor(w_tok[:, NT:2 * NT], w_tok[:, 0:NT], sm[:, 10, :], ALU.mult))
                r = self.row
                dve.wait_ge(*self.s_rk(1))
                over = self.over[:]
                nj = T // P - 1
                L(dve, dve.tensor_copy(r[:, 0, :], bank(7)[:, 0:E]))
                L(dve, dve.tensor_tensor(over, r[:, 0, :].unsqueeze(2).to_broadcast([P, E, nj]),
                                         self.iot[:].unsqueeze(1).to_broadcast([P, E, nj]), ALU.is_gt))
                L(dve, dve.reduce_sum(r[:, 1, :], over, AXX))
                L(dve, dve.tensor_tensor_scan(r[:, 2, :], ones[:, 0:E], r[:, 1, :], 0.0, ALU.mult, ALU.add))
                L(dve, dve.tensor_tensor(r[:, 3, :], r[:, 2, :], r[:, 1, :], ALU.subtract))
                for out, src in ((rank, bank(5)[:, 0:NT * E].rearrange("p (t e) -> p t e", e=E)),
                                 (ovs, rowbc(r[:, 3, :], E))):
                    for k in range(2):
                        ins = dve.tensor_tensor(tmp[:, k], self.oh[:, k], src, ALU.mult)
                    L(dve, ins)
                    L(dve, dve.reduce_sum(out, tmp[:].rearrange("p k t e -> p (k t) e"), AXX))
                over = self.over[:, 0:2 * NT, :]
                L(dve, dve.tensor_tensor(over, rank.unsqueeze(2).to_broadcast([P, 2 * NT, nj]),
                                         self.iot[:].unsqueeze(1).to_broadcast([P, 2 * NT, nj]), ALU.is_ge))
                L(dve, dve.reduce_sum(fl, over, AXX))
                L(dve, dve.tensor_tensor(t2, ovs, fl, ALU.add))
                L(dve, dve.scalar_tensor_tensor(t2, t2, float(E - 1), exp_, ALU.add, ALU.subtract))
                L(dve, dve.scalar_tensor_tensor(t2, fl, 1.0, t2, ALU.min, ALU.mult))
                dve.scalar_tensor_tensor(rank, fl, -float(P), rank, ALU.mult, ALU.add)
                L(dve, dve.tensor_tensor(bk, exp_, t2, ALU.add))
                def over_n(v, n):
                    return v.unsqueeze(2).to_broadcast([P, 2 * NT, n])

                dve.tensor_tensor(self.q_s[:], self.ios[:].unsqueeze(1).to_broadcast([P, 2 * NT, P]),
                                  over_n(rank, P), ALU.is_equal)
                L(dve, dve.tensor_tensor(self.q_b[:], self.iob[:].unsqueeze(1).to_broadcast([P, 2 * NT, NB]),
                                         over_n(bk, NB), ALU.is_equal))
                dve.tensor_tensor(self.q_v[:, :, 0, :], self.q_b[:],
                                  over_n(self.base[:].rearrange("p k t -> p (k t)"), NB), ALU.mult)
                L(dve, dve.tensor_scalar(self.q_v[:, :, 1, :], self.q_b[:], self.part[:, 0:1], None, ALU.mult))
                dve.engine_nop().then_inc(self.s_q.sem, 1)
                L(dve, dve.tensor_tensor(self.ovc[:], r[:, 2, :].unsqueeze(1).to_broadcast([P, OVB, E]),
                                         self.iob[:, 0:OVB].unsqueeze(2).to_broadcast([P, OVB, E]), ALU.is_le))
                L(dve, dve.reduce_sum(self.ovf[:, 0:OVB], self.ovc[:], AXX))
                L(dve, dve.tensor_scalar(self.ovf[:, 0:OVB], self.ovf[:, 0:OVB], float(E - 1), None, ALU.min))
                L(dve, dve.tensor_copy(self.ovf[:, OVB:OVB + 1], r[:, 2, E - 1:E]))
                L(dve, dve.tensor_copy(ov_e[:], self.ovf[:]))
                dve.wait_ge(*self.s_tab(1))
                tab = [self.tab[:, n, :] for n in range(3)]
                L(dve, dve.tensor_scalar(tab[0], bank(4)[:, 0:NB], float(EMPTY), None, ALU.add))
                L(dve, dve.tensor_tensor(tab[1], tab[0], bank(4)[:, NB:2 * NB], ALU.add))
                dve.tensor_copy(idx_y[:], tab[1])
                L(dve, dve.tensor_scalar(tab[2], tab[1], float(T), -float(T), ALU.is_ge, ALU.mult))
                L(dve, dve.tensor_tensor(tab[2], tab[2], tab[1], ALU.add))
                dve.tensor_copy(idx_x[:], tab[2]).then_inc(self.s_rt.sem, 1)

            def unit(self, e, what, half):
                if what == "d":
                    e = e + 1
                    if isinstance(e, int) and e == E:
                        return 4 + 6 * (E - 1) + half
                if isinstance(e, int) and e == 0:
                    return {"g": 0, "u": 2}[what] + half
                return 4 + 6 * (e - 1) + {"g": 0, "d": 2, "u": 4}[what] + half

            def w_src(self, e, what, half):
                if what == "d":
                    w = A["w_down"][self.l].rearrange("e (p q) n -> e p (q n)", q=F // P)
                else:
                    w = A["w_gate" if what == "g" else "w_up"][self.l].rearrange("e (p k) n -> e p (k n)", k=KD)
                if isinstance(e, int):
                    return w[e, :, half * UNIT:(half + 1) * UNIT]
                return w[bass.ds(e, 1), :, half * UNIT:(half + 1) * UNIT].rearrange("a p c -> (a p) c")

            def rep(self, e, r):
                return e if isinstance(e, int) else r

            def load(self, sp, e, r, what, half):
                u, ur = self.unit(e, what, half), self.unit(r, what, half)
                g, gr = self.first + u, self.first + ur
                if isinstance(u, int):
                    stream.wait_free(sp, g)
                else:
                    sp.wait_ge(unit_dve, stream.owner[self.first][1] - 1 + u - RING + 1)
                sp.dma_start(ring[:, gr % RING, :], self.w_src(e, what, half)).then_inc(ring_full[gr % RING], 16)

            def full(self, eng, e, r, what, half):
                u, ur = self.unit(e, what, half), self.unit(r, what, half)
                g0, gr = self.first, self.first + self.unit(r, what, half)
                turns = gr // RING + 1
                if isinstance(e, int):
                    eng.wait_ge(ring_full[gr % RING], 16 * turns)
                else:
                    eng.wait_ge(ring_full[gr % RING], (e - r) * 16 + 16 * turns)

            def steps(self, e):
                if isinstance(e, int) and e == 0:
                    return [(e, "g"), (e, "u")]
                if isinstance(e, int) and e == E:
                    return [(e - 1, "d")]
                return [(e, "g"), (e - 1, "d"), (e, "u")]

            def sp(self, sp):
                self.over_loop(sp, lambda e, r: [self.load(sp, x, rx, w, hf)
                                                 for (x, w), (rx, _) in zip(self.steps(e), self.steps(r))
                                                 for hf in range(2)])

            def over_loop(self, eng, step):
                step(0, 0)
                step(1, 1)
                with eng.Fori(0, (E - 4) // 2) as i:
                    step(2 * i + 2, 2)
                    step(2 * i + 3, 3)
                step(E - 2, E - 2)
                step(E - 1, E - 1)
                step(E, E)

            def split(self, eng, e, r, what, half):
                u, ur = self.unit(e, what, half), self.unit(r, what, half)
                slot = ur % SPLIT
                src = ring[:, (self.first + ur) % RING, :]
                if eng is nc.scalar:
                    self.full(eng, e, r, what, half)
                    if not isinstance(u, int) or u >= SPLIT:
                        eng.wait_ge(*self.s_use(u - SPLIT + 1))
                    eng.activation(self.hi[:, slot, :], src, ACT.Copy).then_inc(self.s_hi.sem, 1)
                else:
                    eng.wait_ge(*self.s_hi(u + 1))
                    eng.tensor_tensor(self.lo[:, slot, :], src, self.hi[:, slot, :].bitcast(F32), ALU.subtract)\
                       .then_inc(unit_dve, 1)

            def unit_ready(self, pe, u):
                pe.wait_ge(unit_dve, stream.owner[self.first][1] + u)

            def x_transpose(self, pe, e, r):
                b = r % 2
                pe.wait_ge(*self.s_gx[b]((e // 2) * 16 + 16 if isinstance(e, int) else (e - r) * 8 + 16 * (r // 2 + 1)))
                if not isinstance(e, int) or e >= 1:
                    pe.wait_ge(*self.s_xl(e))
                for k in range(KD):
                    ins = pe.transpose(bank(0, 2)[:, k * P:(k + 1) * P], self.xg[:, b, k::KD], ident[:])
                ins.then_inc(self.s_xtr.sem, 1)

            def product(self, pe, out, xs, e, r, what, half, first, last):
                u, ur = self.unit(e, what, half), self.unit(r, what, half)
                self.unit_ready(pe, u)
                slot = ur % SPLIT
                n = UNIT // 512
                mats = []
                for q in range(n):
                    if what == "d":
                        row, col = q // 2, q % 2
                        k, o, st = 2 * half + row, out[:, col * 512:(col + 1) * 512], first and row == 0
                        en = last and row == 1
                    else:
                        k, o, st, en = 4 * half + q, out, first and q == 0, last and q == n - 1
                    mats.append((k, o, self.hi[:, slot, q * 512:(q + 1) * 512],
                                 self.lo[:, slot, q * 512:(q + 1) * 512], st, en))
                for k, o, wh_, wl_, st, en in mats:
                    xhk, xlk = xs(k)
                    pe.matmul(o, xhk, wh_, start=st, stop=False)
                    pe.matmul(o, xhk, wl_, start=False, stop=False)
                    ins = pe.matmul(o, xlk, wh_, start=False, stop=en)
                ins.then_inc(self.s_use.sem, 1)
                return ins

            def pe(self, pe):
                def xs(r):
                    return lambda k: (self.xh[:, r % 2, k * P:(k + 1) * P], self.xl[:, r % 2, k * P:(k + 1) * P])

                def hs(k):
                    return self.hh[:, k * P:(k + 1) * P], self.hl[:, k * P:(k + 1) * P]

                def step(e, r):
                    if r < E:
                        pe.wait_ge(*self.s_xl(e + 1))
                        if not isinstance(e, int) or e >= 1:
                            pe.wait_ge(*self.s_sg(e))
                        for half in range(2):
                            self.product(pe, bank(2), xs(r), e, r, "g", half, half == 0, half == 1)
                    if r >= 1:
                        pe.wait_ge(*self.s_hm(e))
                        for q in range(F // P):
                            ins = pe.transpose(bank(4)[:, q * P:(q + 1) * P], self.hm[:, q::F // P], ident[:])
                        ins.then_inc(self.s_htr.sem, 1)
                    if r + 1 < E:
                        self.x_transpose(pe, e + 1, r + 1)
                    if r >= 1:
                        pe.wait_ge(*self.s_hl(e))
                        if not isinstance(e, int) or e >= 2:
                            pe.wait_ge(*self.s_ya(e - 1))
                            pe.wait_ge(*self.s_yd(e - 1))
                        for half in range(2):
                            self.product(pe, bank(5, 2), hs, e - 1, r - 1, "d", half, half == 0, half == 1)
                    if r < E:
                        for half in range(2):
                            self.product(pe, bank(3), xs(r), e, r, "u", half, half == 0, half == 1)

                self.x_transpose(pe, 0, 0)
                self.over_loop(pe, step)

            def used(self, e, what):
                return self.unit(e, what, 1) + 1

            def act(self, act):
                def x_hi(e, r):
                    act.wait_ge(*self.s_xtr(e + 1))
                    if not isinstance(e, int) or e >= 2:
                        act.wait_ge(*self.s_use(self.used(e - 2, "u")))
                    act.activation(self.xh[:, r % 2, :], bank(0, 2), ACT.Copy).then_inc(self.s_xh.sem, 1)

                def step(e, r):
                    if r >= 1:
                        for half in range(2):
                            self.split(act, e - 1, r - 1, "d", half)
                    if r < E:
                        self.split(act, e, r, "u", 0)
                        act.wait_ge(*self.s_use(self.used(e, "g")))
                        if not isinstance(e, int) or e >= 1:
                            act.wait_ge(*self.s_hm(e))
                        act.activation(self.sg[:], bank(2), ACT.Silu).then_inc(self.s_sg.sem, 1)
                    if r >= 1:
                        act.wait_ge(*self.s_htr(e))
                        act.activation(self.hh[:], bank(4), ACT.Copy).then_inc(self.s_hh.sem, 1)
                    if r + 1 < E:
                        x_hi(e + 1, r + 1)
                    if r < E:
                        self.split(act, e, r, "u", 1)
                        if r + 1 < E:
                            for half in range(2):
                                self.split(act, e + 1, r + 1, "g", half)
                    if r >= 1:
                        act.wait_ge(*self.s_use(self.used(e - 1, "d")))
                        if not isinstance(e, int) or e >= 3:
                            act.wait_ge(*self.s_yst[(r - 1) % 2](self.stored(e - 3, r - 3)))
                        act.activation(self.y[:, (r - 1) % 2, 0:512], bank(5), ACT.Copy).then_inc(self.s_ya.sem, 1)

                act.wait_ge(*self.s_tab(1))
                for half in range(2):
                    self.split(act, 0, 0, "g", half)
                x_hi(0, 0)
                self.over_loop(act, step)

            def stored(self, e, r):
                if isinstance(e, int):
                    return 16 * (e // 2 + 1)
                return (e - r) * 8 + 16 * (r // 2 + 1)

            def dve(self, dve):
                def x_lo(e, r):
                    dve.wait_ge(*self.s_xh(e + 1))
                    dve.tensor_tensor(self.xl[:, r % 2, :], bank(0, 2), self.xh[:, r % 2, :].bitcast(F32),
                                      ALU.subtract).then_inc(self.s_xl.sem, 1)

                def step(e, r):
                    if r >= 1:
                        dve.wait_ge(*self.s_use(self.used(e - 1, "u")))
                        dve.wait_ge(*self.s_sg(e))
                        dve.tensor_tensor(self.hm[:], self.sg[:], bank(3), ALU.mult).then_inc(self.s_hm.sem, 1)
                        for half in range(2):
                            self.split(dve, e - 1, r - 1, "d", half)
                    if r < E:
                        self.split(dve, e, r, "u", 0)
                    if r >= 1:
                        dve.wait_ge(*self.s_hh(e))
                        dve.tensor_tensor(self.hl[:], bank(4), self.hh[:].bitcast(F32),
                                          ALU.subtract).then_inc(self.s_hl.sem, 1)
                    if r + 1 < E:
                        x_lo(e + 1, r + 1)
                    if r < E:
                        self.split(dve, e, r, "u", 1)
                        if r + 1 < E:
                            for half in range(2):
                                self.split(dve, e + 1, r + 1, "g", half)
                    if r >= 1:
                        dve.wait_ge(*self.s_use(self.used(e - 1, "d")))
                        if not isinstance(e, int) or e >= 3:
                            dve.wait_ge(*self.s_yst[(r - 1) % 2](self.stored(e - 3, r - 3)))
                        dve.tensor_copy(self.y[:, (r - 1) % 2, 512:1024], bank(6)).then_inc(self.s_yd.sem, 1)

                for half in range(2):
                    self.split(dve, 0, 0, "g", half)
                x_lo(0, 0)
                self.over_loop(dve, step)

            def gather(self, pool, idx, rows):
                return pool.indirect_dma_start(rows, None, xn_dram, bass.IndirectOffsetOnAxis(ap=idx, axis=0),
                                               bounds_check=T - 1, oob_is_err=False)

            def scatter(self, pool, idx, rows):
                return pool.indirect_dma_start(y_dram, bass.IndirectOffsetOnAxis(ap=idx, axis=0), rows, None,
                                               bounds_check=2 * T - 1, oob_is_err=False)

            def pool(self, pool):
                def gather(e):
                    self.gather(pool, idx_x[:, e:e + 1], self.xg[:, e % 2, :]).then_inc(self.s_gx[e % 2].sem, 16)

                def store(e):
                    pool.wait_ge(*self.s_ya(e + 1))
                    pool.wait_ge(*self.s_yd(e + 1))
                    self.scatter(pool, idx_y[:, e:e + 1], self.y[:, e % 2, :]).then_inc(self.s_yst[e % 2].sem, 16)

                pool.wait_ge(*self.s_xg(1))
                pool.wait_ge(*self.s_rt(1))
                for n in range(4):
                    pool.wait_ge(*self.norm.s_st[n](16 * (NT // 4)))
                gather(0)
                gather(1)
                for e in range(E):
                    if e + 2 < E:
                        pool.wait_ge(*self.s_xtr(e + 1))
                        gather(e + 2)
                    if e >= 1:
                        store(e - 1)
                store(E - 1)
                for b in range(2):
                    pool.wait_ge(*self.s_yst[b](16 * (E // 2)))

            def number(self, eng):
                eng.wait_ge(*self.s_rt(1))
                return eng.value_load(ov_e[0:1, OVB:OVB + 1], min_val=0, max_val=OVB)

            def beyond_sp(self, sp):
                sp.wait_ge(unit_dve, stream.owner[self.first + 6 * E - 1][1])
                n = self.number(sp)
                with sp.If(n > 0):
                    with sp.Fori(0, n) as j:
                        sp.wait_ge(*self.s_of(j + 1))
                        e = sp.value_load(ov_e[0:1, bass.ds(j, 1)], min_val=0, max_val=E - 1)
                        for m, (w, q) in enumerate((("w_gate", KD), ("w_up", KD), ("w_down", F // P))):
                            src = A[w][self.l].rearrange("e (p q) n -> e p (q n)", q=q)[bass.ds(e, 1)]
                            sp.dma_start(ring[:, 2 * m:2 * m + 2, :].rearrange("p a c -> p (a c)"),
                                         src.rearrange("a p c -> (a p) c")).then_inc(self.s_ow.sem, 16)
                sp.wait_ge(*self.s_odone(1))

            def beyond_pool(self, pool):
                def step(n):
                    n += 5 * self.l
                    return pool.tensor_tensor(fence[:, n:n + 1], ones[:, 0:1], ones[:, 0:1], ALU.add)

                step(0).then_inc(self.s_of.sem, 1)
                n = self.number(pool)
                with pool.If(n > 0):
                    with pool.Fori(0, n) as j:
                        pool.wait_ge(*self.s_of(j + 1))
                        pool.tensor_copy(self.ovi[:, 0:1], idx_x[:, bass.ds(j + E, 1)]).then_inc(self.s_oi.sem, 1)
                        pool.tensor_copy(self.ovi[:, 1:2], idx_y[:, bass.ds(j + E, 1)]).then_inc(self.s_oi.sem, 1)
                        pool.wait_ge(*self.s_oi(4 * j + 2))
                        step(1).then_inc(self.s_oi.sem, 1)
                        self.gather(pool, self.ovi[:, 0:1], self.xg[:, 0, :]).then_inc(self.s_ox.sem, 16)
                        pool.wait_ge(*self.s_oa(4 * j + 4))
                        step(4).then_inc(self.s_oi.sem, 1)
                        self.scatter(pool, self.ovi[:, 1:2], self.y[:, 0, :]).then_inc(self.s_oy.sem, 16)
                        pool.wait_ge(*self.s_oi(4 * j + 4))
                        pool.wait_ge(*self.s_oy(16 * j + 16))
                        step(2).then_inc(self.s_of.sem, 1)
                step(3).then_inc(self.s_odone.sem, 1)

            def beyond_pe(self, pe):
                n = self.number(pe)
                pe.wait_ge(*self.s_ya(E))
                pe.wait_ge(*self.s_yd(E))
                with pe.If(n > 0):
                    with pe.Fori(0, n) as j:
                        pe.wait_ge(*self.s_ox(16 * j + 16))
                        for k in range(KD):
                            ins = pe.transpose(bank(0, 2)[:, k * P:(k + 1) * P], self.xg[:, 0, k::KD], ident[:])
                        ins.then_inc(self.s_op.sem, 1)
                        pe.wait_ge(*self.s_oa(4 * j + 1))
                        pe.wait_ge(*self.s_ow(48 * j + 48))
                        for m in range(2):
                            for k in range(KD):
                                w = ring[:, 2 * m + k // 4, (k % 4) * 512:(k % 4 + 1) * 512]
                                ins = pe.matmul(bank(2 + m), self.xf[:, k * P:(k + 1) * P], w, start=(k == 0),
                                                stop=(k == KD - 1))
                        ins.then_inc(self.s_op.sem, 1)
                        pe.wait_ge(*self.s_od(j + 1))
                        for q in range(F // P):
                            ins = pe.transpose(bank(4)[:, q * P:(q + 1) * P], self.hm[:, q::F // P], ident[:])
                        ins.then_inc(self.s_op.sem, 1)
                        pe.wait_ge(*self.s_oa(4 * j + 3))
                        for c in range(2):
                            for q in range(F // P):
                                w = ring[:, 4 + q // 2, (q % 2) * D + c * 512:(q % 2) * D + (c + 1) * 512]
                                ins = pe.matmul(bank(5 + c), self.hf[:, q * P:(q + 1) * P], w, start=(q == 0),
                                                stop=(q == F // P - 1))
                        ins.then_inc(self.s_op.sem, 1)

            def beyond_act(self, act):
                n = self.number(act)
                with act.If(n > 0):
                    with act.Fori(0, n) as j:
                        act.wait_ge(*self.s_op(4 * j + 1))
                        act.activation(self.xf[:], bank(0, 2), ACT.Copy).then_inc(self.s_oa.sem, 1)
                        act.wait_ge(*self.s_op(4 * j + 2))
                        act.activation(self.sg[:], bank(2), ACT.Silu).then_inc(self.s_oa.sem, 1)
                        act.wait_ge(*self.s_op(4 * j + 3))
                        act.activation(self.hf[:], bank(4), ACT.Copy).then_inc(self.s_oa.sem, 1)
                        act.wait_ge(*self.s_op(4 * j + 4))
                        act.activation(self.y[:, 0, :], bank(5, 2), ACT.Copy).then_inc(self.s_oa.sem, 1)

            def beyond_dve(self, dve):
                n = self.number(dve)
                with dve.If(n > 0):
                    with dve.Fori(0, n) as j:
                        dve.wait_ge(*self.s_oa(4 * j + 2))
                        dve.tensor_tensor(self.hm[:], self.sg[:], bank(3), ALU.mult).then_inc(self.s_od.sem, 1)

            def combine_pool(self, pool, rows):
                both = y_dram.rearrange("(k t p) d -> t p k d", k=2, p=P)
                for t in range(NT):
                    if t >= ROWS:
                        pool.wait_ge(*self.s_comb(2 * (t - ROWS + 1)))
                    pool.dma_start(rows[:, t % ROWS, :, :], both[t]).then_inc(self.s_row[t % ROWS].sem, 16)

            def combine_dve(self, dve, rows, t):
                dve.wait_ge(*self.s_row[t % ROWS](16 * (t // ROWS + 1)))
                for k in range(2):
                    if k:
                        dve.wait_ge(*self.s_comb(2 * t + 1))
                    dve.scalar_tensor_tensor(h[:, t, :], rows[:, t % ROWS, k, :],
                                             w_tok[:, k * NT + t:k * NT + t + 1], h[:, t, :],
                                             ALU.mult, ALU.add).then_inc(self.s_comb.sem, 1)

        class Ple:

            def __init__(self, l, ready):
                a = Arena(f"p{l}")
                self.l = l
                self.xt = a("xt", [P, KD, T])
                self.proj = a("proj", [P, NT, D])
                self.xn = a("xn", [P, 4, D])
                self.rows = a("rows", [P, ROWS, 2, D])
                self.sg = self.rows[:, 0, :, :].rearrange("p a (b c) -> p (a b) c", c=512)
                self.pt = a("pt", [P, 2, T])
                self.norm = NormTranspose(A["norm_ple"][l:l + 1, :], self.xt, self.xn, ready)
                self.s_p, self.s_pr, self.s_pro, self.s_g, self.s_sg, self.s_mul, self.s_add = (
                    count("ple_" + n, t) for n, t in (("p", 16), ("proj", 2 * NT), ("proj_out", 2 * NT),
                                                      ("gate", 2 * NT), ("sigmoid", 2 * NT), ("mul", 2 * NT),
                                                      ("add", 2 * NT)))
                self.proj_units = stream.dense(2)
                self.units = [stream.dense(2) for _ in range(2)]

            def tile(self, t):
                return self.s_add(NT + t + 1)

            def sp(self, sp):
                load_unit(sp, self.proj_units, A["w_ple_proj"][self.l, 0], 2 * 512)
                sp.dma_start(self.pt[:], A["p_t"][self.l]).then_inc(self.s_p.sem, 16)
                load_unit(sp, self.proj_units + 1, A["w_ple_proj"][self.l, 1], 2 * 512)

            def sp_gate(self, sp):
                sp.wait_ge(*self.s_pr(NT))
                for c, u in enumerate(self.units):
                    for half in range(2):
                        load_unit(sp, u + half, A["w_ple_gate"][self.l, c][:, half * UNIT:(half + 1) * UNIT], UNIT)

            def pe_proj(self, pe, moe):
                pe.wait_ge(*moe.s_odone(1))
                pe.wait_ge(*self.s_p(16))
                for g in range(2 * NT):
                    t, c = divmod(g, 2)
                    if g < 2:
                        full(pe, self.proj_units + c)
                    if g >= 4:
                        pe.wait_ge(*self.s_pro(g - 3))
                    for k in range(2):
                        ins = pe.matmul(bank(4 + g % 4), self.pt[:, k, t * P:(t + 1) * P],
                                        ring[:, (self.proj_units + c) % RING, k * 512:(k + 1) * 512],
                                        start=(k == 0), stop=(k == 1))
                    ins.then_inc(self.s_pr.sem, 1)
                pe.wait_ge(*self.s_pr(2 * NT))
                pe.nop().then_inc(unit_pe, 2)

            def act_proj(self, act, t):
                for c in range(2):
                    g = 2 * t + c
                    act.wait_ge(*self.s_pr(g + 1))
                    act.activation(self.proj[:, t, c * 512:(c + 1) * 512], bank(4 + g % 4), ACT.Copy)\
                       .then_inc(self.s_pro.sem, 1)

            def pe(self, pe):
                for s, v in self.norm.done:
                    pe.wait_ge(s, v)
                for c, u in enumerate(self.units):
                    for t in range(NT):
                        g = c * NT + t
                        if g < 4:
                            pe.wait_ge(*self.s_pro(2 * NT - 3 + g))
                        else:
                            pe.wait_ge(*self.s_sg(g - 3))
                        for k in range(KD):
                            if t == 0 and k % 4 == 0:
                                full(pe, u + k // 4)
                            ins = pe.matmul(bank(4 + g % 4), self.xt[:, k, t * P:(t + 1) * P],
                                            ring[:, (u + k // 4) % RING, (k % 4) * 512:(k % 4 + 1) * 512],
                                            start=(k == 0), stop=(k == KD - 1))
                        ins.then_inc(self.s_g.sem, 1)
                    pe.wait_ge(*self.s_g((c + 1) * NT))
                    pe.nop().then_inc(unit_pe, 2)

            def act(self, act, c, t):
                g = c * NT + t
                act.wait_ge(*self.s_g(g + 1))
                if g >= 4:
                    act.wait_ge(*self.s_add(g - 3))
                act.activation(self.sg[:, g % 4, :], bank(4 + g % 4), ACT.Sigmoid).then_inc(self.s_sg.sem, 1)

            def dve(self, dve, c, t):
                g = c * NT + t
                hs = h[:, t, c * 512:(c + 1) * 512]
                dve.wait_ge(*self.s_sg(g + 1))
                dve.tensor_tensor(self.sg[:, g % 4, :], self.sg[:, g % 4, :], self.proj[:, t, c * 512:(c + 1) * 512],
                                  ALU.mult).then_inc(self.s_mul.sem, 1)
                dve.wait_ge(*self.s_mul(g + 1))
                dve.tensor_tensor(hs, hs, self.sg[:, g % 4, :], ALU.add).then_inc(self.s_add.sem, 1)

        class SpatialGate:
            def __init__(self, ready):
                a = Arena("mix1")
                self.xt = a("xt", [P, KD, T])
                self.ut = a("ut", [P, KD, T])
                self.v = a("v", [P, NT, SG])
                self.ws = a("ws", [P, SGG, P])
                self.bs = a("bs", [P, SGG, P])
                self.tmp = a("tmp", [P, 2, 512])
                self.norm = NormTranspose(A["norm_mix"][1:2, :], self.xt, self.v[:, 0:4, :], ready)
                self.units = [stream.dense(2) for _ in range(4)]
                self.s_ws, self.s_bs, self.s_mask, self.s_u, self.s_ue, self.s_v, self.s_ve, self.s_sq, self.s_r, self.s_vs, self.s_s, self.s_t, self.s_y = (
                    Count(sem("gmlp_" + n), 0) for n in ("ws", "bs", "mask", "u", "ue", "v", "ve", "sq", "r", "vs", "s", "t", "y"))

            def sp(self, sp):
                for c, u in enumerate(self.units):
                    for half in range(2):
                        load_unit(sp, u + half, A["w_in_o"][c][:, half * UNIT:(half + 1) * UNIT], UNIT)

            def sp_small(self, sp):
                sp.wait_ge(*self.norm.prior.s_tr(2 * NT))
                sp.dma_start(self.ws[:], A["w_s_t"]).then_inc(self.s_ws.sem, 16)
                sp.dma_start(self.bs[:].rearrange("p g t -> p (g t)"), A["b_s"].partition_broadcast(P))\
                  .then_inc(self.s_bs.sem, 16)

            def pool(self, pool):
                pool.wait_ge(*self.s_ws(16))
                pool.affine_select(out=self.ws[:], in_=self.ws[:], compare_op=ALU.is_ge, fill=0.0, base=0,
                                   pattern=[[0, SGG], [1, P]], channel_multiplier=-1).then_inc(self.s_mask.sem, 1)

            def pe(self, pe):
                for s, v in self.norm.done:
                    pe.wait_ge(s, v)
                g = 0
                for c in range(2):
                    u = self.units[c]
                    for b in range(4):
                        for hf in range(2):
                            if g >= 4:
                                pe.wait_ge(*self.s_ue(g - 3))
                            for k in range(KD):
                                if b == 0 and hf == 0 and k % 4 == 0:
                                    full(pe, u + k // 4)
                                o = (k % 4) * 512 + b * P
                                ins = pe.matmul(bank(4 + g % 4), ring[:, (u + k // 4) % RING, o:o + P],
                                                self.xt[:, k, hf * 512:(hf + 1) * 512],
                                                start=(k == 0), stop=(k == KD - 1))
                            ins.then_inc(self.s_u.sem, 1)
                            g += 1
                    pe.wait_ge(*self.s_u(g))
                    pe.nop().then_inc(unit_pe, 2)
                for c in range(2):
                    u = self.units[2 + c]
                    for t in range(NT):
                        n = c * NT + t
                        if n >= 4:
                            pe.wait_ge(*self.s_ve(n - 3))
                        for k in range(KD):
                            if t == 0 and k % 4 == 0:
                                full(pe, u + k // 4)
                            ins = pe.matmul(bank(n % 4), self.xt[:, k, t * P:(t + 1) * P],
                                            ring[:, (u + k // 4) % RING, (k % 4) * 512:(k % 4 + 1) * 512],
                                            start=(k == 0), stop=(k == KD - 1))
                        ins.then_inc(self.s_v.sem, 1)
                    pe.wait_ge(*self.s_v((c + 1) * NT))
                    pe.nop().then_inc(unit_pe, 2)
                pe.wait_ge(*self.s_mask(1))
                pe.wait_ge(*self.s_vs(NT))
                pe.wait_ge(*self.s_ue(16))
                for g in range(SGG):
                    for hf in range(2):
                        n = 2 * g + hf
                        if n >= 4:
                            pe.wait_ge(*self.s_t(n - 3))
                        for t in range(4):
                            ins = pe.matmul(bank(4 + n % 4)[:, t * P:(t + 1) * P],
                                            self.v[:, 4 * hf + t, g * P:(g + 1) * P], self.ws[:, g, :],
                                            start=True, stop=True)
                        ins.then_inc(self.s_s.sem, 1)

            def act(self, act):
                for g in range(16):
                    b, hf = divmod(g, 2)
                    act.wait_ge(*self.s_u(g + 1))
                    act.activation(self.ut[:, b, hf * 512:(hf + 1) * 512], bank(4 + g % 4),
                                   ACT.Gelu_apprx_tanh).then_inc(self.s_ue.sem, 1)
                for n in range(16):
                    c, t = divmod(n, NT)
                    act.wait_ge(*self.s_v(n + 1))
                    act.activation(self.v[:, t, c * 512:(c + 1) * 512], bank(n % 4),
                                   ACT.Gelu_apprx_tanh).then_inc(self.s_ve.sem, 1)
                act.wait_ge(*self.s_ve(16))
                for t in range(NT):
                    act.activation(self.xt[:, t, :], self.v[:, t, :], ACT.Square,
                                   accum_out=ss[:, t:t + 1]).then_inc(self.s_sq.sem, 1)
                act.wait_ge(*self.s_r(1))
                act.activation(rstd[:], rstd[:], ACT.Sqrt).then_inc(self.s_r.sem, 1)

            def dve(self, dve):
                dve.wait_ge(*self.s_sq(NT))
                dve.tensor_scalar(rstd[:], ss[:], 1.0 / SG, EPS, ALU.mult, ALU.add).then_inc(self.s_r.sem, 1)
                dve.wait_ge(*self.s_r(2))
                dve_chain.link(dve, dve.reciprocal(rstd[:], rstd[:]))
                for t in range(NT):
                    dve.tensor_scalar(self.v[:, t, :], self.v[:, t, :], rstd[:, t:t + 1], None, ALU.mult)\
                       .then_inc(self.s_vs.sem, 1)
                dve.wait_ge(*self.s_bs(16))
                dve.wait_ge(*self.s_ue(16))
                for n in range(16):
                    g, hf = divmod(n, 2)
                    uts = self.ut[:, g, hf * 512:(hf + 1) * 512]
                    tmp = self.tmp[:, n % 2, :]
                    dve.wait_ge(*self.s_s(n + 1))
                    dve.scalar_tensor_tensor(tmp.rearrange("p (t c) -> p t c", c=P),
                                             bank(4 + n % 4).rearrange("p (t c) -> p t c", c=P),
                                             cols[:, C_VN + g:C_VN + g + 1],
                                             self.bs[:, g, :].unsqueeze(1).to_broadcast([P, 4, P]),
                                             ALU.mult, ALU.add).then_inc(self.s_t.sem, 1)
                    dve.wait_ge(*self.s_t(n + 1))
                    dve.tensor_tensor(uts, uts, tmp, ALU.mult).then_inc(self.s_y.sem, 1)

        class Final:
            def __init__(self, ready):
                self.ready, self.prior = ready, NormTranspose.prior
                self.s_g, self.s_ss, self.s_mean, self.s_root, self.s_o, self.s_out = (
                    Count(sem("final_" + n), 0) for n in ("gain", "squares", "mean", "root", "o", "out"))

            def sp(self, sp):
                sp.wait_ge(*self.prior.s_xn(NT))
                sp.dma_start(gain[:], A["final_norm"].partition_broadcast(P)).then_inc(self.s_g.sem, 16)
                for t in range(NT):
                    sp.wait_ge(*self.s_o(t + 1))
                    sp.dma_start(out[t * P:(t + 1) * P, :], h[:, t, :]).then_inc(self.s_out.sem, 16)
                sp.wait_ge(*self.s_out(16 * NT))

            def act(self, act, last):
                def square(t):
                    act.wait_ge(*self.ready(t))
                    if t:
                        act.wait_ge(*self.s_ss(t))
                    act.activation(bank(2, 2), h[:, t, :], ACT.Square, accum_out=ss[:, t:t + 1])\
                       .then_inc(self.s_ss.sem, 1)

                def root(n):
                    act.wait_ge(*self.s_mean(n + 1))
                    act.activation(rstd[:, 4 * n:4 * n + 4], rstd[:, 4 * n:4 * n + 4], ACT.Sqrt)\
                       .then_inc(self.s_root.sem, 1)

                for t in range(NT):
                    last(t)
                    if t >= 1:
                        square(t - 1)
                    if t == 5:
                        root(0)
                square(NT - 1)
                root(1)

            def dve(self, dve, last):
                def mean(n):
                    dve.wait_ge(*self.s_ss(4 * n + 4))
                    dve.tensor_scalar(rstd[:, 4 * n:4 * n + 4], ss[:, 4 * n:4 * n + 4], 1.0 / D, EPS,
                                      ALU.mult, ALU.add).then_inc(self.s_mean.sem, 1)

                def scale(n):
                    dve.wait_ge(*self.s_root(n // 4 + 1))
                    if n % 4 == 0:
                        dve_chain.link(dve, dve.reciprocal(rstd[:, n:n + 4], rstd[:, n:n + 4]))
                    dve.scalar_tensor_tensor(h[:, n, :], h[:, n, :], rstd[:, n:n + 1], gain[:],
                                             ALU.mult, ALU.mult).then_inc(self.s_o.sem, 1)

                for t in range(5):
                    last(t)
                mean(0)
                last(5)
                dve.wait_ge(*self.s_g(16))
                scale(0)
                scale(1)
                last(6)
                scale(2)
                scale(3)
                last(7)
                mean(1)
                for t in range(4, NT):
                    scale(t)

        moe0 = Moe(0, out0.tile)
        ple0 = Ple(0, moe0.tile)
        gate1 = SpatialGate(ple0.tile)
        out1 = OutProj("out1", gate1.ut, A["w_out_o"], [gate1.s_y(16)])
        moe1 = Moe(1, out1.tile)
        ple1 = Ple(1, moe1.tile)
        final = Final(ple1.tile)

        block = ctx.enter_context(nc.Block())

        @block.sync
        def _(sp):
            setup_sp(sp)
            norm0.sp(sp)
            in_sp(sp)
            att_sp(sp)
            out0.sp(sp)
            for moe, ple in ((moe0, ple0), (moe1, ple1)):
                moe.norm.sp(sp)
                moe.route_sp(sp)
                moe.norm.sp_store(sp)
                ple.norm.sp(sp)
                moe.sp(sp)
                moe.beyond_sp(sp)
                ple.sp(sp)
                ple.sp_gate(sp)
                if moe is moe0:
                    gate1.norm.sp(sp)
                    gate1.sp_small(sp)
                    gate1.sp(sp)
                    out1.sp(sp)
            final.sp(sp)

        @block.gpsimd
        def _(pool):
            setup_pool(pool)
            for moe, ple in ((moe0, ple0), (moe1, ple1)):
                moe.iotas(pool)
                moe.pool(pool)
                moe.beyond_pool(pool)
                moe.combine_pool(pool, ple.rows)
                if moe is moe0:
                    gate1.pool(pool)

        @block.scalar
        def _(act):
            norm0.act(act)
            in_act(act)
            values_out(act, lambda o, x: act.activation(o, x, ACT.Copy), 0, s_va)
            att_act(act)
            yt_act(act)
            for moe, ple in ((moe0, ple0), (moe1, ple1)):
                moe.norm.act(act)
                moe.route_act(act)
                moe.act(act)
                moe.beyond_act(act)
                ple.norm.act(act, lambda t: ple.act_proj(act, t))
                for t in range(NT):
                    ple.act(act, 0, t)
                if moe is moe0:
                    gate1.norm.act(act, lambda t: ple.act(act, 1, t))
                    gate1.act(act)
                else:
                    final.act(act, lambda t: ple.act(act, 1, t))

        @block.vector
        def _(dve):
            norm0.dve(dve)
            in_dve(dve)
            values_out(dve, dve.tensor_copy, 1, s_vd)
            att_dve(dve)
            for moe, ple, out_proj in ((moe0, ple0, out0), (moe1, ple1, out1)):
                for t in range(NT):
                    out_proj.dve(dve, 0, t)
                moe.norm.dve(dve, lambda t: out_proj.dve(dve, 1, t))
                moe.route_dve(dve)
                moe.dve(dve)
                moe.beyond_dve(dve)
                ple.norm.dve(dve, lambda t: moe.combine_dve(dve, ple.rows, t))
                for t in range(NT):
                    ple.dve(dve, 0, t)
                if moe is moe0:
                    gate1.norm.dve(dve, lambda t: ple.dve(dve, 1, t))
                    gate1.dve(dve)
                else:
                    final.dve(dve, lambda t: ple.dve(dve, 1, t))

        @block.tensor
        def _(pe):
            for s, v in CONSTS:
                pe.wait_ge(s, v)
            norm0.pe(pe)
            in_pe(pe)
            values_pe(pe)
            att_pe(pe)
            yt_pe(pe)
            out0.pe(pe)
            for moe, ple in ((moe0, ple0), (moe1, ple1)):
                moe.norm.pe(pe)
                moe.route_pe(pe)
                moe.pe(pe)
                moe.beyond_pe(pe)
                ple.pe_proj(pe, moe)
                ple.norm.pe(pe)
                ple.pe(pe)
                if moe is moe0:
                    gate1.norm.pe(pe)
                    gate1.pe(pe)
                    out1.pe(pe)


def _panels(w, width):
    k = w.shape[0] // P
    return np.ascontiguousarray(w.reshape(k, P, -1, width).transpose(2, 1, 0, 3).reshape(-1, P, k * width))


def _layout(x, p, positions, norm_mix, norm_ffn, w_in_e, conv_w, q_norm, w_q_up, kv_norm, w_kv_up, w_out_e,
            w_in_o, v_norm, w_s, b_s, w_out_o, w_router_group, w_router_expert, w_gate, w_up, w_down,
            norm_ple, w_ple_gate, w_ple_proj, final_norm):
    w_in = w_in_e[0]
    conv = w_in[:, :3 * CONV].reshape(D, 3, 4, P).transpose(0, 2, 1, 3).reshape(D, 4 * 3 * P)
    half = ROPE // 2
    inv = (1.0 / (10000.0 ** (np.arange(0, ROPE, 2, dtype=np.float32) / np.float32(ROPE)))).astype(np.float32)
    rope = np.zeros((P, 2), np.float32)
    rope[64:96, 0] = np.concatenate([inv, inv])
    rope[64:96, 1] = np.concatenate([-np.ones(half), np.ones(half)])
    col = lambda v: v.reshape(-1, P).T
    cols = np.concatenate([col(q_norm[0]), col(kv_norm[0]), col(v_norm[0]),
                           conv_w[0].reshape(3, 4, P).transpose(2, 1, 0).reshape(P, 12), rope], axis=1)
    wq = w_q_up[0].reshape(3, P, H, DQK).transpose(2, 1, 0, 3).reshape(H, P, 3 * DQK)
    w_kv = w_kv_up[0].reshape(2, P, H, NOPE + VD)
    wk = w_kv[..., :NOPE].transpose(2, 1, 0, 3).reshape(H, P, 2 * NOPE)
    wv = w_kv[..., NOPE:].transpose(1, 0, 2, 3).reshape(P, 2 * H * VD)
    router = np.concatenate([w_router_group, w_router_expert], axis=2)
    return {
        "x": x[0], "cols": cols, "positions": positions,
        "norm_mix": norm_mix, "norm_ffn": norm_ffn, "norm_ple": norm_ple, "final_norm": final_norm[None],
        "w_in_e": _panels(np.concatenate([conv, w_in[:, 3 * CONV:3 * CONV + QR]], axis=1), 3 * P),
        "w_in_kv": _panels(w_in[:, 3 * CONV + QR:], KVR + ROPE)[0],
        "w_heads": np.concatenate([wq, wk], axis=2), "w_v": wv,
        "w_out_e": _panels(w_out_e[0], 512), "w_in_o": _panels(w_in_o[0], 512), "w_out_o": _panels(w_out_o[0], 512),
        "w_s_t": w_s[0].transpose(2, 0, 1), "b_s": b_s[0].reshape(1, SGG * P),
        "w_router": router.reshape(DEPTH, KD, P, NG + E).transpose(0, 2, 1, 3),
        "w_gate": w_gate, "w_up": w_up, "w_down": w_down,
        "w_ple_gate": np.stack([_panels(w, 512) for w in w_ple_gate]),
        "w_ple_proj": np.stack([_panels(w, 512) for w in w_ple_proj]),
        "p_t": p[:, 0].reshape(DEPTH, T, 2, P).transpose(0, 3, 2, 1),
    }


def kernel(**inputs):
    import concourse.bacc as _bacc
    from concourse.bass_utils import run_bass_kernel_spmd as _run

    nc = _bacc.Bacc("TRN2", target_bir_lowering=False, num_devices=1)
    arrays = {n: np.ascontiguousarray(a) for n, a in _layout(**{k: np.asarray(v) for k, v in inputs.items()}).items()}
    aps = {n: nc.dram_tensor(n, a.shape, mybir.dt.from_np(a.dtype), kind="ExternalInput").ap()
           for n, a in arrays.items()}
    out = nc.dram_tensor("out_0", (T, D), F32, kind="ExternalOutput").ap()
    program(nc, aps, out)
    r = _run(nc, [arrays], core_ids=[0])
    return r.results[0]["out_0"].reshape(1, T, D)
```

```python
from contextlib import ExitStack

import numpy as np

import concourse.bass as bass
from concourse import mybir

F32 = mybir.dt.float32
F32R = mybir.dt.float32r
I32 = mybir.dt.int32
BF16 = mybir.dt.bfloat16
ALU = mybir.AluOpType
ACT = mybir.ActivationFunctionType
AXX = mybir.AxisListType.X

P = 128
D = 1024
T = 1024
NT = T // P
KD = D // P
DEPTH = 2
EPS = 1e-6
NEG = -1e30
CONV = 512
QR, KVR = 384, 256
H, NOPE, ROPE, VD = 8, 64, 32, 64
DQK = NOPE + ROPE
E, NG, EG, F = 32, 4, 8, 512
SG, SGG = 1024, 8
ROWS = 3
UNIT = 2048
RING = 6
SPLIT = 4
OVB = 2 * T // P - 1
NB = E + OVB
EMPTY = 8192
SCALE = float(DQK) ** -0.5
SBUF_END = 229344
TWO_PI_HI, TWO_PI_LO = 6.28125, 0.0019353071795864769
PI = 3.141592653589793

C_QN, C_KVN, C_VN, C_CONV, C_ROPE = 0, 3, 5, 13, 25
N_COLS = C_ROPE + 2


class Tally:

    def __init__(self, sem):
        self.sem, self.base, self.k = sem, 0, 0

    def inc(self, ins, n=1):
        ins.then_inc(self.sem, n)
        self.k += n
        return self.value()

    def value(self):
        return self.base + self.k

    def link(self, eng, ins):
        eng.wait_ge(self.sem, self.inc(ins))

    def enter(self, i, per):
        self._start, self._per = self.value(), per
        self.base, self.k = i * per + self._start, 0

    def leave(self, turns):
        assert self.k == self._per, (self.k, self._per)
        self.base, self.k = self._start + turns * self._per, 0


class Count:

    def __init__(self, sem, base):
        self.sem, self.base = sem, base

    def __call__(self, n):
        return self.sem, n + self.base


def program(nc, A, out):
    with ExitStack() as ctx:
        names = {}

        def sem(name):
            assert name not in names, name
            names[name] = ctx.enter_context(nc.semaphore(name))
            return names[name]

        counts = {}

        def count(name, total):
            c, at = counts.get(name) or (sem(name), 0)
            counts[name] = c, at + total
            return Count(c, at)

        top = [(nc.sbuf_base + 63) // 64 * 64]

        def keep(name, shape, dt=F32):
            t = nc.alloc_sbuf_tensor_at(name, shape, dt, offset=top[0])
            top[0] += (int(np.prod(shape[1:])) * (2 if dt is BF16 else 4) + 31) // 32 * 32
            return t

        h = keep("h", [P, NT, D])
        ring_lo = nc.alloc_sbuf_tensor_at("ring_lo", [P, RING, UNIT], F32R, offset=top[0])
        ring = keep("ring", [P, RING, UNIT])
        ident = keep("ident", [P, P])
        ones = keep("ones", [P, P])
        causal = keep("causal", [P, P])
        ones_b = keep("ones_b", [P, P], BF16)
        before_b = keep("before_b", [P, P], BF16)
        cols = keep("cols", [P, N_COLS])
        wr = keep("wr", [P, KD, NG + E])
        ss = keep("ss", [P, NT])
        rstd = keep("rstd", [P, NT])
        eps_c = keep("eps_c", [P, 1])
        idx_y = keep("idx_y", [P, NB], I32)
        idx_x = keep("idx_x", [P, NB], I32)
        ov_e = keep("ov_e", [P, OVB + 1], I32)
        w_tok = keep("w_tok", [P, 2 * NT])
        gain = keep("gain", [P, D])
        fence = keep("fence", [P, 10])
        ARENA = top[0]

        class Arena:
            def __init__(self, tag):
                self.tag, self.at = tag, ARENA

            def go(self, kib):
                self.at = ARENA + kib * 1024
                return self

            def __call__(self, name, shape, dt=F32):
                t = nc.alloc_sbuf_tensor_at(f"{self.tag}_{name}", shape, dt, offset=self.at)
                self.at += (int(np.prod(shape[1:])) * 4 + 31) // 32 * 32
                assert self.at <= SBUF_END, (name, self.at - SBUF_END)
                return t

        banks = ctx.enter_context(nc.psum_tensor("banks", [P, 8 * 512], F32))

        def bank(b, n=1):
            return banks[:, b * 512:(b + n) * 512]

        xn_dram = nc.dram_tensor("xn_dram", (T, D), F32, kind="Internal").ap()
        y_dram = nc.dram_tensor("y_dram", (2 * T, D), F32, kind="Internal").ap()

        dve_chain = Tally(sem("dve_chain"))
        s_set = sem("s_set")
        s_const = sem("s_const")
        s_load = sem("s_load")
        s_x = [sem(f"s_x{n}") for n in range(4)]
        ring_full = [sem(f"ring_full{i}") for i in range(RING)]
        unit_pe = sem("unit_pe")
        unit_dve = sem("unit_dve")

        class Stream:

            def __init__(self):
                self.owner = []
                self.n_pe = self.n_dve = 0

            def dense(self, n):
                first = len(self.owner)
                for _ in range(n):
                    self.n_pe += 1
                    self.owner.append((unit_pe, self.n_pe))
                return first

            def expert(self, n):
                first = len(self.owner)
                for _ in range(n):
                    self.n_dve += 1
                    self.owner.append((unit_dve, self.n_dve))
                return first

            def wait_free(self, sp, u):
                if u >= RING:
                    sp.wait_ge(*self.owner[u - RING])

        stream = Stream()

        def full(eng, u):
            eng.wait_ge(ring_full[u % RING], 16 * (u // RING + 1))

        def load_unit(sp, u, src, n, parts=P):
            stream.wait_free(sp, u)
            sp.dma_start(ring[:, u % RING, 0:n], src).then_inc(ring_full[u % RING], 16)

        class NormTranspose:

            prior = None

            def __init__(self, gain_row, xt, xn, ready, store=None, product=None):
                self.product = product
                self.second = 0
                self.gain_row, self.xt, self.xn, self.ready, self.store = gain_row, xt, xn, ready, store
                self.prior, NormTranspose.prior = NormTranspose.prior, self
                self.nbuf = xn.shape[1]
                self.s_g = count("norm_gain", 16)
                self.s_ss = count("norm_squares", NT)
                self.s_mean = count("norm_mean", 2)
                self.s_root = count("norm_root", 2)
                self.s_xn = count("norm_xn", NT)
                self.s_tr = count("norm_tr", 2 * NT)
                if not product:
                    self.s_evA, self.s_evD = count("norm_evA", NT), count("norm_evD", NT)
                    self.done = [self.s_evA(NT), self.s_evD(NT)]
                self.s_st = [count(f"norm_store{i}", 16 * NT // self.nbuf) for i in range(self.nbuf)] \
                    if store is not None else None

            def sp(self, sp):
                if self.prior:
                    sp.wait_ge(*self.prior.s_xn(NT))
                sp.dma_start(gain[:], self.gain_row.partition_broadcast(P)).then_inc(self.s_g.sem, 16)

            def sp_store(self, sp):
                for t in range(NT):
                    sp.wait_ge(*self.s_xn(t + 1))
                    sp.dma_start(self.store[t * P:(t + 1) * P, :], self.xn[:, t % self.nbuf, :])\
                      .then_inc(self.s_st[t % self.nbuf].sem, 16)

            def act(self, act, last=None):
                def square(t):
                    act.wait_ge(*self.ready(t))
                    if t:
                        act.wait_ge(*self.s_ss(t))
                    act.activation(bank(6, 2), h[:, t, :], ACT.Square, accum_out=ss[:, t:t + 1])\
                       .then_inc(self.s_ss.sem, 1)

                def root(n):
                    act.wait_ge(*self.s_mean(n + 1))
                    act.activation(rstd[:, 4 * n:4 * n + 4], rstd[:, 4 * n:4 * n + 4], ACT.Sqrt)\
                       .then_inc(self.s_root.sem, 1)

                for t in range(NT):
                    if last:
                        last(t)
                    if t >= 1:
                        square(t - 1)
                    if t == 5:
                        root(0)
                square(NT - 1)
                self.out_act(act, 0)
                root(1)
                for t in range(1, 2 if self.product else NT):
                    self.out_act(act, t)

            def pair(self, t):
                return 2 * (t % 2) + (self.second if t >= 4 else 0)

            def out_act(self, act, t):
                if self.product:
                    act.wait_ge(*self.s_tr(2 * t + 2))
                    self.product.x_hi(act, t, bank(self.pair(t), 2))
                else:
                    act.wait_ge(*self.s_tr(2 * t + 1))
                    act.activation(self.xt[:, 0:4, t * P:(t + 1) * P],
                                   bank(2 * (t % 2)).rearrange("p (k c) -> p k c", c=P),
                                   ACT.Copy).then_inc(self.s_evA.sem, 1)

            def out_dve(self, dve, t):
                if self.product:
                    self.product.x_lo(dve, t, bank(self.pair(t), 2))
                else:
                    dve.wait_ge(*self.s_tr(2 * t + 2))
                    dve.tensor_copy(self.xt[:, 4:8, t * P:(t + 1) * P],
                                    bank(2 * (t % 2) + 1).rearrange("p (k c) -> p k c", c=P))\
                       .then_inc(self.s_evD.sem, 1)

            def scale(self, dve, t):
                b = t % self.nbuf
                if t >= self.nbuf:
                    dve.wait_ge(*self.s_tr(2 * (t - self.nbuf + 1)))
                    if self.s_st:
                        dve.wait_ge(*self.s_st[b](16 * (t // self.nbuf)))
                dve.scalar_tensor_tensor(self.xn[:, b, :], h[:, t, :], rstd[:, t:t + 1], gain[:],
                                         ALU.mult, ALU.mult).then_inc(self.s_xn.sem, 1)

            def dve(self, dve, last=None):
                def mean(n):
                    dve.wait_ge(*self.s_ss(4 * n + 4))
                    dve.tensor_scalar(rstd[:, 4 * n:4 * n + 4], ss[:, 4 * n:4 * n + 4], 1.0 / D, EPS,
                                      ALU.mult, ALU.add).then_inc(self.s_mean.sem, 1)

                def invert(n):
                    dve.wait_ge(*self.s_root(n + 1))
                    dve_chain.link(dve, dve.reciprocal(rstd[:, 4 * n:4 * n + 4], rstd[:, 4 * n:4 * n + 4]))

                scale, out = (lambda t: self.scale(dve, t)), (lambda t: self.out_dve(dve, t))
                last = last or (lambda t: None)
                for t in range(5):
                    last(t)
                mean(0)
                last(5)
                invert(0)
                dve.wait_ge(*self.s_g(16))
                scale(0)
                last(6)
                scale(1)
                last(7)
                scale(2)
                mean(1)
                out(0)
                scale(3)
                invert(1)
                for t in range(1, 2 if self.product else NT):
                    out(t)
                    if t + 3 < NT:
                        scale(t + 3)

            def tile_dve(self, dve, t):
                if t + 2 < NT:
                    self.out_dve(dve, t + 2)
                if t + 5 < NT:
                    self.scale(dve, t + 5)

            def transposes(self, pe, t):
                pe.wait_ge(*self.s_xn(t + 1))
                for half in range(2):
                    if t >= 2:
                        pe.wait_ge(*(self.product.s_xl if self.product else (self.s_evA, self.s_evD)[half])(t - 1))
                    for k in range(4):
                        ins = pe.transpose(bank(self.pair(t) + half)[:, k * P:(k + 1) * P],
                                           self.xn[:, t % self.nbuf, (4 * half + k) * P:(4 * half + k + 1) * P],
                                           ident[:])
                    ins.then_inc(self.s_tr.sem, 1)

            def pe(self, pe):
                for t in range(NT):
                    self.transposes(pe, t)

        class TileProduct:

            def __init__(self, panels, hi, xh, xl, taken, on_pool=()):
                self.panels, self.hi, self.xh, self.xl, self.taken = panels, hi, xh, xl, taken
                self.on_pool = on_pool
                self.first = stream.dense(4)
                self.s_wh = count("dense_w_hi", 4)
                dve, pool = count("dense_w_lo", 4 - len(on_pool)), count("dense_w_lo_pool", len(on_pool))
                by_dve = [n for n in range(4) if n not in on_pool]
                self.lo_made = [pool(on_pool.index(n) + 1) if n in on_pool else dve(by_dve.index(n) + 1)
                                for n in range(4)]
                self.s_xh, self.s_xl = count("dense_x_hi", NT), count("dense_x_lo", NT)
                self.s_mm = count("dense_mm", 2 * NT)

            def sp(self, sp):
                for n in range(4):
                    load_unit(sp, self.first + n, self.panels[n // 2][:, n % 2 * UNIT:(n % 2 + 1) * UNIT], UNIT)

            def slot(self, n):
                return (self.first + n) % RING

            def w_hi(self, act, n):
                full(act, self.first + n)
                act.activation(self.hi[n], ring[:, self.slot(n), :], ACT.Copy).then_inc(self.s_wh.sem, 1)

            def w_lo(self, eng, n):
                eng.wait_ge(*self.s_wh(n + 1))
                eng.tensor_tensor(ring_lo[:, self.slot(n), :], ring[:, self.slot(n), :], self.hi[n].bitcast(F32),
                                  ALU.subtract).then_inc(self.lo_made[n][0], 1)

            def x_hi(self, act, t, src):
                if t >= 2:
                    act.wait_ge(*self.s_mm(2 * (t - 1)))
                act.activation(self.as_(self.xh, t, src), src, ACT.Copy).then_inc(self.s_xh.sem, 1)

            def x_lo(self, dve, t, src):
                dve.wait_ge(*self.s_xh(t + 1))
                dve.tensor_tensor(self.as_(self.xl, t, src), src, self.as_(self.xh, t, src).bitcast(F32),
                                  ALU.subtract).then_inc(self.s_xl.sem, 1)

            def as_(self, x, t, src):
                b = x[:, t % 2, :]
                return b.rearrange("p (k c) -> p k c", c=P) if len(src.shape) == 3 else b

            def pe(self, pe, t):
                pe.wait_ge(*self.s_xl(t + 1))
                for c in range(2):
                    if t >= 1:
                        pe.wait_ge(*self.taken(2 * t + c - 1))
                    for k in range(KD):
                        n = 2 * c + k // 4
                        if t == 0 and k % 4 == 0:
                            pe.wait_ge(*self.lo_made[n])
                        xs = slice(k * P, (k + 1) * P)
                        ws = slice(k % 4 * 512, (k % 4 + 1) * 512)
                        x_hi, x_lo = self.xh[:, t % 2, xs], self.xl[:, t % 2, xs]
                        w_hi, w_lo = self.hi[n][:, ws], ring_lo[:, self.slot(n), ws]
                        pe.matmul(bank(4 + c), x_hi, w_hi, start=(k == 0), stop=False)
                        pe.matmul(bank(4 + c), x_hi, w_lo, start=False, stop=False)
                        ins = pe.matmul(bank(4 + c), x_lo, w_hi, start=False, stop=(k == KD - 1))
                    ins.then_inc(self.s_mm.sem, 1)
                if t == NT - 1:
                    pe.wait_ge(*self.s_mm(2 * NT))
                    pe.nop().then_inc(unit_pe, 4)

        def setup_sp(sp):
            for n in range(4):
                sp.dma_start(h[:, 2 * n:2 * n + 2, :], A["x"].rearrange("(t p) d -> p t d", p=P)[:, 2 * n:2 * n + 2, :])\
                  .then_inc(s_x[n], 16)
            sp.dma_start(cols[:], A["cols"]).then_inc(s_load, 16)

        def setup_pool(pool):
            pool.memset(ident[:], 0.0).then_inc(s_set, 1)
            pool.memset(ones[:], 1.0).then_inc(s_set, 1)
            pool.memset(before_b[:], 1.0).then_inc(s_set, 1)
            pool.memset(ones_b[:], 1.0).then_inc(s_set, 1)
            pool.memset(causal[:], 0.0).then_inc(s_set, 1)
            pool.memset(fence[:], 0.0).then_inc(s_set, 1)
            pool.memset(eps_c[:], EPS).then_inc(s_set, 1)
            pool.wait_ge(s_set, 7)
            pool.affine_select(out=ident[:], in_=ident[:], compare_op=ALU.not_equal, fill=1.0, base=0,
                               pattern=[[-1, P]], channel_multiplier=1).then_inc(s_const, 1)
            pool.affine_select(out=before_b[:], in_=before_b[:], compare_op=ALU.is_gt, fill=0.0, base=0,
                               pattern=[[1, P]], channel_multiplier=-1).then_inc(s_const, 1)
            pool.affine_select(out=causal[:], in_=causal[:], compare_op=ALU.is_ge, fill=NEG, base=0,
                               pattern=[[-1, P]], channel_multiplier=1).then_inc(s_const, 1)

        CONSTS = [(s_const, 3)]

        a0 = Arena("mix0")
        xt0 = a0("xt", [P, KD, T])
        yt0 = a0("yt", [P, KD, T])
        cq = a0("cq", [P, 3, T])
        ckv = a0("ckv", [P, 2, T])
        trig = a0("trig", [P, 2, T])
        qk = a0("qk", [P, 4, T])
        rt = a0("rt", [P, 2, T])
        wh = a0("wh", [P, 2, 3 * DQK + 2 * NOPE])
        lrow = a0("lrow", [P, 3 * NT])
        ytok = xt0[:, 0:4, :].rearrange("p a b -> p (a b)").rearrange("p (t c) -> p t c", c=H * VD)
        pt = xt0[:, 4:6, :]
        vals = [z[:, 6:8, :].rearrange("p a b -> p (a b)").rearrange("p (t c) -> p t c", c=H * VD)
                for z in (xt0, yt0)]
        prob = yt0[:, 4:6, :]
        posi = yt0[:, 0, :].bitcast(I32)
        ZB, AB, GB = yt0[:, 4, :], yt0[:, 5, :], yt0[:, 6, :]
        REG = slice(64, 96)

        norm0 = NormTranspose(A["norm_mix"][0:1, :], xt0, qk, lambda t: (s_x[t // 2], 16))

        IN_W = [3 * P, KVR + ROPE] + [3 * P] * 4
        in_units = [stream.dense(2) for _ in IN_W]
        wv_unit = stream.dense(1)
        s_in = sem("s_in")
        s_in_a = sem("s_in_a")
        s_in_d = sem("s_in_d")
        s_trig = sem("s_trig")
        s_pos = sem("s_pos")
        s_sq = sem("s_sq")
        s_latn = sem("s_latn")
        s_wh = [sem("s_wh0"), sem("s_wh1")]
        s_v = sem("s_v")
        s_va, s_vd = sem("s_va"), sem("s_vd")
        s_proj = sem("s_proj")
        s_qkv = sem("s_qkv")
        s_rope = sem("s_rope")
        s_sc = sem("s_sc")
        s_max = sem("s_max")
        s_exp = sem("s_exp")
        s_ptr = sem("s_ptr")
        s_pta, s_ptd = sem("s_pta"), sem("s_ptd")
        s_pv = sem("s_pv")
        s_o = sem("s_o")
        s_yt, s_yte = sem("s_yt"), sem("s_yte")

        def in_sp(sp):
            sp.dma_start(posi[REG, :], A["positions"].partition_broadcast(32)).then_inc(s_pos, 16)
            for n, (u, w) in enumerate(zip(in_units, IN_W)):
                src = A["w_in_kv"] if n == 1 else A["w_in_e"][4 if n == 0 else n - 2]
                for half in range(2):
                    load_unit(sp, u + half, src[:, half * 4 * w:(half + 1) * 4 * w], 4 * w)
                if n == 1:
                    for b in range(2):
                        sp.dma_start(wh[:, b, :], A["w_heads"][b]).then_inc(s_wh[b], 16)
            load_unit(sp, wv_unit, A["w_v"], 2 * H * VD)

        GROUPS = []
        for n in range(6):
            GROUPS += [("in", n, b, hf) for b in range(3) for hf in range(2)]
            if n == 2:
                GROUPS += [("sq", m, hf) for m in range(2) for hf in range(2)]
            if n == 3:
                GROUPS += [("head", m, hf) for m in range(2) for hf in range(2)]

        def place(*group):
            return GROUPS.index(group)

        reader, a_read, d_read = {}, 0, 0
        for g, group in enumerate(GROUPS):
            if group[0] == "in" and group[1] >= 2 and group[2] < 2:
                d_read += 1
                reader[g] = (s_in_d, d_read)
            else:
                a_read += 1
                reader[g] = (s_in_a, a_read)

        LAT = [(cq, 3, QR, C_QN, [qk[:, 0, :], qk[:, 1, :], qk[:, 2, :]]),
               (ckv, 2, KVR, C_KVN, [qk[:, 3, :], yt0[:, 7, :]])]
        WQ = 3 * DQK

        def head_product(pe, dst, m, hf, b):
            rank, nk, first, step, w = ((cq, 3, 0, DQK, DQK), (ckv, 2, WQ, NOPE, NOPE))[m]
            for k in range(nk):
                ins = pe.matmul(dst[0:w, :], wh[:, b, first + k * step:first + k * step + w],
                                rank[:, k, hf * 512:(hf + 1) * 512], start=(k == 0), stop=(k == nk - 1))
            return ins

        def head_copy(act, src, m, hf, b):
            sl = slice(hf * 512, (hf + 1) * 512)
            if m == 0:
                return act.activation(qk[0:DQK, b, sl], src[0:DQK, :], ACT.Copy, scale=SCALE)
            return act.activation(qk[0:NOPE, 2 + b, sl], src[0:NOPE, :], ACT.Copy)

        def in_pe(pe):
            for s, v in norm0.done:
                pe.wait_ge(s, v)
            for g, group in enumerate(GROUPS):
                if g >= 8:
                    pe.wait_ge(*reader[g - 8])
                if group[0] == "in":
                    n, b, hf = group[1:]
                    u, w = in_units[n], IN_W[n]
                    m = ROPE if (n, b) == (1, 2) else P
                    po = 64 if m == ROPE else 0
                    for k in range(KD):
                        if b == 0 and hf == 0 and k % 4 == 0:
                            full(pe, u + k // 4)
                        lhs = ring[:, (u + k // 4) % RING, (k % 4) * w + b * P:(k % 4) * w + b * P + m]
                        ins = pe.matmul(bank(g % 8)[po:po + m, :], lhs, xt0[:, k, hf * 512:(hf + 1) * 512],
                                        start=(k == 0), stop=(k == KD - 1))
                elif group[0] == "sq":
                    m, hf = group[1:]
                    pe.wait_ge(s_sq, 5)
                    squares = LAT[m][4]
                    for k, src in enumerate(squares):
                        ins = pe.matmul(bank(g % 8), ones[:], src[:, hf * 512:(hf + 1) * 512],
                                        start=(k == 0), stop=(k == len(squares) - 1))
                else:
                    m, hf = group[1:]
                    pe.wait_ge(s_latn, 5)
                    pe.wait_ge(s_wh[0], 16)
                    ins = head_product(pe, bank(g % 8), m, hf, 0)
                ins.then_inc(s_in, 1)
                if group[0] == "in" and group[2:] == (2, 1):
                    pe.wait_ge(s_in, g + 1)
                    pe.nop().then_inc(unit_pe, 2)

        def in_act(act):
            for g, group in enumerate(GROUPS):
                if g in reader and reader[g][0] is s_in_d:
                    continue
                hf = group[-1]
                sl = slice(hf * 512, (hf + 1) * 512)
                src = bank(g % 8)
                if group[0] == "in":
                    n, b = group[1:3]
                    act.wait_ge(s_in, g + 1)
                    if n == 0:
                        dst = cq[:, b, sl]
                    elif n == 1:
                        dst, src = (ckv[:, b, sl], src) if b < 2 else (rt[REG, 0, sl], src[REG, :])
                    else:
                        if n > 2 and hf == 0:
                            act.wait_ge(s_in_d, 4 * (n - 2) - 2)
                        dst = GB[:, sl]
                    ins = act.activation(dst, src, ACT.Copy)
                elif group[0] == "sq":
                    m = group[1]
                    act.wait_ge(s_in, place("sq", m, 1) + 1)
                    ins = act.activation(qk[:, m, sl], src, ACT.Sqrt, scale=1.0 / LAT[m][2], bias=eps_c[:])
                else:
                    act.wait_ge(s_in, g + 1)
                    ins = head_copy(act, src, group[1], hf, 0)
                ins.then_inc(s_in_a, 1)
                if group == ("in", 0, 2, 1):
                    trig_act(act)
                if group == ("in", 1, 2, 1):
                    act.wait_ge(*reader[g])
                    for c, nk, _, _, squares in LAT:
                        for k in range(nk):
                            act.activation(squares[k], c[:, k, :], ACT.Square).then_inc(s_sq, 1)

        def conv_dve(dve, n):
            wc = C_CONV + 3 * n
            dve.wait_ge(*reader[place("in", 2 + n, 2, 1)])
            for hf in range(2):
                sl = slice(hf * 512, (hf + 1) * 512)
                dve.tensor_tensor(ZB[:, sl], bank(place("in", 2 + n, 0, hf) % 8), GB[:, sl],
                                  ALU.mult).then_inc(s_in_d, 1)
            dve.wait_ge(s_in_d, 4 * n + 2)
            L = dve_chain.link
            L(dve, dve.tensor_scalar(AB[:, :], ZB[:, :], cols[:, wc + 2:wc + 3], None, ALU.mult))
            L(dve, dve.scalar_tensor_tensor(AB[:, 1:T], ZB[:, 0:T - 1], cols[:, wc + 1:wc + 2],
                                            AB[:, 1:T], ALU.mult, ALU.add))
            L(dve, dve.scalar_tensor_tensor(AB[:, 2:T], ZB[:, 0:T - 2], cols[:, wc:wc + 1],
                                            AB[:, 2:T], ALU.mult, ALU.add))
            for hf in range(2):
                sl = slice(hf * 512, (hf + 1) * 512)
                dve.tensor_tensor(yt0[:, n, sl], bank(place("in", 2 + n, 1, hf) % 8), AB[:, sl],
                                  ALU.mult).then_inc(s_in_d, 1)

        def trig_dve(dve):
            ang, k_i, kf, w1 = rt[REG, 1, :], yt0[REG, 1, :].bitcast(I32), trig[REG, 1, :], trig[REG, 0, :]
            L = dve_chain.link
            dve.wait_ge(s_pos, 16)
            L(dve, dve.tensor_copy(w1, posi[REG, :]))
            L(dve, dve.tensor_scalar(ang, w1, cols[REG, C_ROPE:C_ROPE + 1], None, ALU.mult))
            L(dve, dve.tensor_scalar(w1, ang, 1.0 / (2 * PI), None, ALU.mult))
            L(dve, dve.tensor_copy(k_i, w1))
            L(dve, dve.tensor_copy(kf, k_i))
            L(dve, dve.scalar_tensor_tensor(ang, kf, -TWO_PI_HI, ang, ALU.mult, ALU.add))
            L(dve, dve.scalar_tensor_tensor(ang, kf, -TWO_PI_LO, ang, ALU.mult, ALU.add))

            def wrap(x, tmp):
                L(dve, dve.tensor_scalar(tmp, x, PI, -2 * PI, ALU.is_gt, ALU.mult))
                L(dve, dve.tensor_tensor(x, x, tmp, ALU.add))
                L(dve, dve.tensor_scalar(tmp, x, -PI, 2 * PI, ALU.is_lt, ALU.mult))
                L(dve, dve.tensor_tensor(x, x, tmp, ALU.add))

            wrap(ang, kf)
            L(dve, dve.tensor_scalar(w1, ang, PI / 2, None, ALU.add))
            wrap(w1, kf)
            L(dve, dve.tensor_scalar(w1, w1, 3.1415925, -3.1415925, ALU.min, ALU.max))
            dve.tensor_scalar(ang, ang, 3.1415925, -3.1415925, ALU.min, ALU.max).then_inc(s_trig, 1)

        def trig_act(act):
            act.wait_ge(s_trig, 1)
            act.activation(trig[REG, 0, :], trig[REG, 0, :], ACT.Sin).then_inc(s_trig, 1)
            act.activation(trig[REG, 1, :], rt[REG, 1, :], ACT.Sin).then_inc(s_trig, 1)

        def latent_dve(dve):
            for m, (c, nk, _, col, _) in enumerate(LAT):
                dve.wait_ge(*reader[place("sq", m, 1)])
                dve_chain.link(dve, dve.reciprocal(qk[:, m, :], qk[:, m, :]))
                for k in range(nk):
                    dve.scalar_tensor_tensor(c[:, k, :], c[:, k, :], cols[:, col + k:col + k + 1],
                                             qk[:, m, :], ALU.mult, ALU.mult).then_inc(s_latn, 1)
            L = dve_chain.link
            dve.wait_ge(s_trig, 3)
            L(dve, dve.tensor_scalar(trig[REG, 1, :], trig[REG, 1, :], cols[REG, C_ROPE + 1:C_ROPE + 2], None,
                                     ALU.mult))
            L(dve, dve.stream_shuffle(rt[REG, 1, :], rt[REG, 0, :], [(j + 16) % 32 for j in range(32)]))
            L(dve, dve.tensor_tensor(rt[REG, 1, :], rt[REG, 1, :], trig[REG, 1, :], ALU.mult))
            L(dve, dve.tensor_tensor(rt[REG, 0, :], rt[REG, 0, :], trig[REG, 0, :], ALU.mult))
            dve.tensor_tensor(qk[REG, 2, :], rt[REG, 0, :], rt[REG, 1, :], ALU.add).then_inc(s_rope, 1)
            dve.tensor_tensor(qk[REG, 3, :], rt[REG, 0, :], rt[REG, 1, :], ALU.add).then_inc(s_rope, 1)
            dve.wait_ge(s_rope, 2)

        def rope_step(dve, b, n):
            if n == 0:
                ins = dve.tensor_tensor(rt[REG, 0, :], qk[REG, b, :], trig[REG, 0, :], ALU.mult)
            elif n == 1:
                ins = dve.stream_shuffle(rt[REG, 1, :], qk[REG, b, :], [(j + 16) % 32 for j in range(32)])
            elif n == 2:
                ins = dve.tensor_tensor(rt[REG, 1, :], rt[REG, 1, :], trig[REG, 1, :], ALU.mult)
            else:
                dve.tensor_tensor(qk[REG, b, :], rt[REG, 0, :], rt[REG, 1, :], ALU.add).then_inc(s_rope, 1)
                return
            dve_chain.link(dve, ins)

        def in_dve(dve):
            dve.wait_ge(s_load, 16)
            trig_dve(dve)
            conv_dve(dve, 0)
            latent_dve(dve)
            conv_dve(dve, 1)
            dve.wait_ge(*reader[place("head", 0, 1)])
            for n in range(4):
                rope_step(dve, 0, n)
            conv_dve(dve, 2)
            conv_dve(dve, 3)

        def values_pe(pe):
            full(pe, wv_unit)
            for t in range(NT):
                if t < 4:
                    for g in range(len(GROUPS) - 8, len(GROUPS)):
                        if g % 8 == t:
                            pe.wait_ge(*reader[g])
                else:
                    pe.wait_ge((s_va, s_vd)[t % 2], (t - 4) // 2 + 1)
                for k in range(2):
                    ins = pe.matmul(bank(t % 4), ckv[:, k, t * P:(t + 1) * P],
                                    ring[:, wv_unit % RING, k * 512:(k + 1) * 512], start=(k == 0), stop=(k == 1))
                ins.then_inc(s_v, 1)
            for g in range(len(GROUPS) - 8, len(GROUPS)):
                pe.wait_ge(*reader[g])
            pe.wait_ge(s_v, NT)
            pe.nop().then_inc(unit_pe, 1)

        def values_out(eng, write, parity, s_done):
            eng.wait_ge(s_in_d, d_read)
            for t in range(parity, NT, 2):
                eng.wait_ge(s_v, t + 1)
                write(vals[t // 4][:, t % 4, :], bank(t % 4)).then_inc(s_done, 1)

        FILL = (1, 1, 1, 3)
        TURNS = H // 2
        STEPS = 2 * NT

        def ahead(eng, *sems):
            for s in sems:
                eng.nop().then_inc(s, 1)

        PT_GROUPS = []
        for n in range(STEPS):
            for j0 in range(0, n % NT + 1, 4):
                PT_GROUPS.append((n, j0, min(4, n % NT + 1 - j0), len(PT_GROUPS)))
        GT = len(PT_GROUPS)

        def groups_through(n):
            return sum(1 for x in PT_GROUPS if x[0] <= n)

        def turns(eng, turn):
            with eng.Fori(0, TURNS - 1) as i:
                turn(i, False)
            turn(TURNS - 1, True)

        def att_sp(sp):
            sp.wait_ge(s_in, place("head", 1, 1) + 1)
            sp.dma_start(wh[:, 0, :], A["w_heads"][2]).then_inc(s_wh[0], 16)
            with sp.Fori(0, TURNS - 2) as i:
                for u in range(2):
                    sp.wait_ge(s_proj, 8 * i + (4 * u + 4))
                    sp.dma_start(wh[:, 1 - u, :], A["w_heads"][bass.ds(2 * i + (u + 3), 1)]
                                 .rearrange("a p c -> (a p) c")).then_inc(s_wh[1 - u], 16)
            sp.wait_ge(s_proj, 8 * (TURNS - 2) + 4)
            sp.dma_start(wh[:, 1, :], A["w_heads"][H - 1]).then_inc(s_wh[1], 16)

        def att_pe(pe):
            ahead(pe, s_ptr, s_pv)

            def scores(i, n, last=False):
                u, b = n // NT % 2, n % NT
                if b in (4, 5) and not (last and u == 1):
                    pe.wait_ge(s_qkv, 8 * i + (4 * u + b))
                if n >= 1:
                    pe.wait_ge(s_exp, STEPS * i + (n - 1 + 1))
                if b == 0 and n > 0:
                    pe.wait_ge(s_qkv, 8 * i + (4 * (n // NT) + 1))
                    pe.wait_ge(s_rope, 2 * i + (n // NT + 3))
                for c in range(0, (b + 1) * P, 512):
                    w = min(512, (b + 1) * P - c)
                    dst = bank(2 * (n % 2), 2)[:, c:c + w]
                    last = c + w == (b + 1) * P
                    ins = pe.matmul(dst, qk[0:DQK, u, b * P:(b + 1) * P], qk[0:DQK, 2 + u, c:c + w],
                                    start=True, stop=not last)
                pe.matmul(dst[:, w - P:w], ident[:], causal[:], start=False, stop=True).then_inc(s_sc, 1)

            def turn(i, last):
                for n in range(STEPS):
                    u, b = n // NT, n % NT
                    if not (last and n + 1 == STEPS):
                        scores(i, n + 1, last)
                    if b < 4 and not (last and u == 1):
                        if b == 0:
                            pe.wait_ge(s_wh[1 - u], 16 * i + 16 * (1 + u))
                        pe.wait_ge(s_qkv, 8 * i + (4 * u + b + 1))
                        head_product(pe, bank(FILL[b]), b // 2, b % 2, 1 - u).then_inc(s_proj, 1)
                    pe.wait_ge(s_exp, STEPS * i + (n + 2))
                    for nn, j0, cnt, g in PT_GROUPS:
                        if nn == n:
                            pe.wait_ge((s_pta, s_ptd)[g % 2], GT // 2 * i + (g // 2 + 1))
                            for j in range(j0, j0 + cnt):
                                ins = pe.transpose(bank(4 + g % 2)[:, (j - j0) * P:(j - j0 + 1) * P],
                                                   prob[:, n % 2, j * P:(j + 1) * P], ident[:])
                            ins.then_inc(s_ptr, 1)
                    if n >= 1:
                        weigh(i, n - 1)
                weigh(i, STEPS - 1)

            def weigh(i, n):
                u, b = n // NT, n % NT
                for nn, _, _, g in PT_GROUPS:
                    if nn == n:
                        pe.wait_ge((s_pta, s_ptd)[g % 2], GT // 2 * i + (g // 2 + 2))
                pe.wait_ge(s_o, STEPS * i + max(n, 1))
                for j in range(b + 1):
                    ins = pe.matmul(bank(6 + n % 2)[:, 0:VD], pt[:, n % 2, j * P:(j + 1) * P],
                                    vals[j // 4][:, j % 4, bass.ds(2 * VD * i + VD * u, VD)],
                                    start=(j == 0), stop=(j == b))
                ins.then_inc(s_pv, 1)

            pe.wait_ge(*reader[place("head", 1, 1)])
            pe.wait_ge(s_rope, 3)
            pe.wait_ge(s_va, NT // 2)
            pe.wait_ge(s_vd, NT // 2)
            scores(0, 0)
            turns(pe, turn)

        def pt_out(eng, write, parity, s_done, i, n):
            for nn, j0, cnt, g in PT_GROUPS:
                if nn == n and g % 2 == parity:
                    eng.wait_ge(s_ptr, GT * i + (g + 2))
                    eng.wait_ge(s_pv, STEPS * i + (max(n - 1, 0) + 1))
                    write(pt[:, n % 2, j0 * P:(j0 + cnt) * P], bank(4 + g % 2)[:, 0:cnt * P]).then_inc(s_done, 1)

        def att_act(act):
            ahead(act, s_qkv, s_exp, s_pta)

            def exps(i, n):
                act.wait_ge(s_max, STEPS * i + (n + 1))
                if n >= 1:
                    act.wait_ge(s_ptr, GT * i + (groups_through(n - 2) + 1))
                u, b = n // NT % 2, n % NT
                w = (b + 1) * P
                act.activation(prob[:, n % 2, 0:w], bank(2 * (n % 2), 2)[:, 0:w], ACT.Exp,
                               bias=lrow[:, 2 * NT + b:2 * NT + b + 1],
                               accum_out=lrow[:, u * NT + b:u * NT + b + 1]).then_inc(s_exp, 1)

            def turn(i, last):
                for n in range(STEPS):
                    u, b = n // NT, n % NT
                    if not (last and n + 1 == STEPS):
                        exps(i, n + 1)
                    if b < 4 and not (last and u == 1):
                        act.wait_ge(s_proj, 8 * i + (4 * u + b + 1))
                        head_copy(act, bank(FILL[b]), b // 2, b % 2, 1 - u).then_inc(s_qkv, 1)
                    pt_out(act, lambda o, x: act.activation(o, x, ACT.Copy), 0, s_pta, i, n)
                    if last and n in SPLIT_STEPS:
                        out0.g.w_hi(act, SPLIT_STEPS.index(n))

            exps(0, 0)
            turns(act, turn)

        def att_dve(dve):
            ahead(dve, s_ptd, s_o)
            L = dve_chain.link

            def row_max(i, n):
                b = n % NT
                dve.wait_ge(s_sc, STEPS * i + (n + 1))
                dve.tensor_reduce(lrow[:, 2 * NT + b:2 * NT + b + 1], bank(2 * (n % 2), 2)[:, 0:(b + 1) * P],
                                  axis=AXX, op=ALU.max, negate=True).then_inc(s_max, 1)

            def norm_out(i, n):
                u, b = n // NT, n % NT
                total = lrow[:, u * NT + b:u * NT + b + 1]
                L(dve, dve.reciprocal(total, total))
                dve.wait_ge(s_pv, STEPS * i + (n + 2))
                dve.tensor_scalar(ytok[:, b, bass.ds(2 * VD * i + VD * u, VD)], bank(6 + n % 2)[:, 0:VD],
                                  total, None, ALU.mult).then_inc(s_o, 1)

            def turn(i, last):
                for n in range(STEPS):
                    u, b = n // NT, n % NT
                    if not (last and n + 1 == STEPS):
                        row_max(i, n + 1)
                    pt_out(dve, dve.tensor_copy, 1, s_ptd, i, n)
                    if last and n in SPLIT_STEPS:
                        out0.g.w_lo(dve, SPLIT_STEPS.index(n))
                    if 2 <= b < 6 and not (last and u == 1):
                        if b == 2:
                            dve.wait_ge(s_qkv, 8 * i + (4 * u + 3))
                        rope_step(dve, 1 - u, b - 2)
                    if n >= 1:
                        norm_out(i, n - 1)
                norm_out(i, STEPS - 1)

            row_max(0, 0)
            with dve.Fori(0, TURNS - 1) as i:
                dve_chain.enter(i, 2 * 3 + STEPS)
                turn(i, False)
            dve_chain.leave(TURNS - 1)
            turn(TURNS - 1, True)

        def yt_pe(pe, t):
            pe.wait_ge(s_o, 1 + (H - 1) * NT + t + 1)
            if t >= 2:
                pe.wait_ge(s_yte, t - 1)
            for k in range(4):
                ins = pe.transpose(bank(t % 2)[:, k * P:(k + 1) * P], ytok[:, t, k * P:(k + 1) * P], ident[:])
            ins.then_inc(s_yt, 1)

        def yt_act(act, t):
            act.wait_ge(s_yt, t + 1)
            act.activation(yt0[:, 4:8, t * P:(t + 1) * P], bank(t % 2).rearrange("p (k c) -> p k c", c=P),
                           ACT.Copy).then_inc(s_yte, 1)
            act.wait_ge(s_yte, t + 1)

        class OutProj:

            def __init__(self, tag, xt, w, hi_at, tile_pe=None, tile_act=None):
                self.xt, self.tile_pe, self.tile_act = xt, tile_pe, tile_act
                a = Arena(tag)
                hi = [a.go(kib)(f"hi{n}", [P, UNIT], F32R)[:] for n, kib in enumerate(hi_at)]
                a.go(92)
                xh, xl = a("xh", [P, 2, D], F32R), a("xl", [P, 2, D], F32R)
                self.s_take = count("out_take", 2 * NT)
                self.g = TileProduct([w[0], w[1]], hi, xh, xl, self.s_take)

            def tile(self, t):
                return self.s_take(2 * t + 2)

            def x(self, t):
                return self.xt[:, :, t * P:(t + 1) * P]

            def pe(self, pe):
                for t in range(NT):
                    self.g.pe(pe, t)
                    if self.tile_pe and t + 2 < NT:
                        self.tile_pe(pe, t + 2)

            def act(self, act, t):
                if t + 2 < NT:
                    if self.tile_act:
                        self.tile_act(act, t + 2)
                    self.g.x_hi(act, t + 2, self.x(t + 2))

            def dve(self, dve, t):
                for c in range(2):
                    dve.wait_ge(*self.g.s_mm(2 * t + c + 1))
                    dve.tensor_tensor(h[:, t, c * 512:(c + 1) * 512], h[:, t, c * 512:(c + 1) * 512],
                                      bank(4 + c), ALU.add).then_inc(self.s_take.sem, 1)
                if t + 2 < NT:
                    self.g.x_lo(dve, t + 2, self.x(t + 2))

        out0 = OutProj("out0", yt0, A["w_out_e"], (64, 72, 80, 16), yt_pe, yt_act)
        SPLIT_STEPS = (NT + 1, NT + 3, NT + 5)

        def out0_act(act):
            yt_act(act, 0)
            out0.g.x_hi(act, 0, out0.x(0))
            out0.g.w_hi(act, 3)
            yt_act(act, 1)
            out0.g.x_hi(act, 1, out0.x(1))

        def out0_dve(dve):
            out0.g.x_lo(dve, 0, out0.x(0))
            out0.g.w_lo(dve, 3)
            out0.g.x_lo(dve, 1, out0.x(1))

        class Moe:

            def __init__(self, l, ready):
                self.l = l
                tag = self.tag = f"m{l}_"
                a = Arena(tag)
                self.hi = a("hi", [P, SPLIT, UNIT], F32R)
                self.lo = a("lo", [P, SPLIT, UNIT], F32R)
                self.xh = a("xh", [P, 2, D], F32R)
                self.xl = a("xl", [P, 2, D], F32R)
                self.sg = a("sg", [P, F])
                self.hm = a("hm", [P, F])
                self.hh = a("hh", [P, F], F32R)
                self.hl = a("hl", [P, F], F32R)
                self.y = a("y", [P, 2, D])
                self.xf = a("xf", [P, D])
                self.hf = a("hf", [P, F])
                self.ovi = a("ovi", [P, 2], I32)
                self.xg = a("xg", [P, 2, D])
                b = Arena(tag + "r")
                self.xn = b("xn", [P, 4, D])
                b.go(32)
                self.xt = b("xt", [P, KD, T])
                self.lgt = b("lgt", [P, T])
                self.lg = b("lg", [P, NT, NG + E])
                self.oh = b("oh", [P, 2, NT, E])
                self.em = b("em", [P, NT, E])
                self.tmp = b("tmp", [P, 2, NT, E])
                self.both = b("both", [P, NT, E], BF16)
                self.small = b("small", [P, 24, NT])
                self.row = b("row", [P, 4, E])
                self.over = b("over", [P, E, T // P - 1])
                self.iog = b("iog", [P, NG])
                self.ioe = b("ioe", [P, E])
                self.iob = b("iob", [P, NB])
                self.ios = b("ios", [P, P])
                self.iot = b("iot", [P, T // P - 1])
                self.part = b("part", [P, 1])
                self.base = b("base", [P, 2, NT])
                self.q_s = b("q_s", [P, 2 * NT, P], BF16)
                self.q_b = b("q_b", [P, 2 * NT, NB])
                self.q_v = b("q_v", [P, 2 * NT, 2, NB], BF16)
                self.tab = b("tab", [P, 3, NB])
                assert b.at <= ARENA + 102 * 1024
                self.ovc = b("ovc", [P, OVB, E])
                self.ovf = b("ovf", [P, OVB + 1])
                self.norm = NormTranspose(A["norm_ffn"][l:l + 1, :], self.xt, self.xn, ready, store=xn_dram)
                def S(n, total):
                    return count("moe_" + n, total)

                self.s_io, self.s_wr, self.s_lg = S("iota", 7), S("w_router", 16), S("logits", 3)
                self.s_lt = S("logits_out", 2)
                self.s_exd, self.s_ex = S("exp_in", 2), S("exp", 2)
                self.s_A, self.s_rk, self.s_q = S("chosen", 1), S("ranks", 1), S("one_hots", 1)
                self.s_tab, self.s_rt, self.s_xg = S("table", 1), S("routed", 1), S("x_cleared", 1)
                self.s_gx = [S("gathered0", 8 * E), S("gathered1", 8 * E)]
                self.s_yst = [S("stored0", 8 * E), S("stored1", 8 * E)]
                self.s_xtr, self.s_xh, self.s_xl = S("x_transposed", E), S("x_hi", E), S("x_lo", E)
                self.s_hi, self.s_use = S("w_hi", 6 * E), S("w_used", 6 * E)
                self.s_sg, self.s_hm = S("silu", E), S("hidden", E)
                self.s_htr, self.s_hh, self.s_hl = S("h_transposed", E), S("h_hi", E), S("h_lo", E)
                self.s_ya, self.s_yd = S("y_act", E), S("y_dve", E)
                self.s_of, self.s_ow, self.s_oi, self.s_ox, self.s_op, self.s_oa, self.s_od, self.s_oy = (
                    Count(sem(f"beyond{l}_{n}"), 0)
                    for n in ("free", "weights", "index", "gathered", "pe", "act", "dve", "stored"))
                self.s_odone = S("beyond_done", 1)
                self.s_row = [S(f"row{i}", 16 * len(range(i, NT, ROWS))) for i in range(ROWS)]
                self.s_comb = S("combined", 2 * NT)
                self.first = stream.expert(6 * E)

            def tile(self, t):
                return self.s_comb(2 * t + 2)

            def iotas(self, pool):
                pool.wait_ge(*self.norm.s_tr(1))
                kw = dict(allow_small_or_imprecise_dtypes=True)
                for tile, pat, base, cm in ((self.iog, [[-1, NG]], NG, 0), (self.ioe, [[-1, E]], E, 0),
                                            (self.iob, [[1, NB]], 0, 0), (self.ios, [[1, P]], 0, 0),
                                            (self.iot, [[P, T // P - 1]], P, 0), (self.part, [[0, 1]], 0, 1),
                                            (self.base, [[T, 2], [P, NT]], -EMPTY, 0)):
                    pool.iota(tile[:], pattern=pat, base=base, channel_multiplier=cm, **kw).then_inc(self.s_io.sem, 1)
                pool.memset(self.xg[:], 0.0).then_inc(self.s_xg.sem, 1)

            def route_sp(self, sp):
                if self.l:
                    sp.wait_ge(self.s_lg.sem, 2)
                sp.dma_start(wr[:], A["w_router"][self.l]).then_inc(self.s_wr.sem, 16)

            def route_pe(self, pe):
                for s, v in self.norm.done:
                    pe.wait_ge(s, v)
                pe.wait_ge(*self.s_wr(16))
                for hf in range(2):
                    for k in range(KD):
                        ins = pe.matmul(bank(4 + hf)[0:NG + E, :], wr[:, k, :],
                                        self.xt[:, k, hf * 512:(hf + 1) * 512],
                                        start=(k == 0), stop=(k == KD - 1))
                    ins.then_inc(self.s_lg.sem, 1)
                for t in range(NT):
                    if t % 4 == 0:
                        pe.wait_ge(*self.s_lt(t // 4 + 1))
                    ins = pe.transpose(bank(6)[:, t * (NG + E):(t + 1) * (NG + E)],
                                       self.lgt[0:NG + E, t * P:(t + 1) * P], ident[0:NG + E, 0:NG + E])
                ins.then_inc(self.s_lg.sem, 1)
                pe.wait_ge(*self.s_A(1))
                for t in range(NT):
                    for s in range(t + 1):
                        ins = pe.matmul(bank(5)[:, t * E:(t + 1) * E], before_b[:] if s == t else ones_b[:],
                                        self.both[:, s, :], start=(s == 0), stop=(s == t))
                for t in range(NT):
                    ins = pe.matmul(bank(7)[:, 0:E], ones_b[:], self.both[:, t, :], start=(t == 0),
                                    stop=(t == NT - 1))
                ins.then_inc(self.s_rk.sem, 1)
                pe.wait_ge(*self.s_q(1))
                for n in range(2 * NT):
                    ins = pe.matmul(bank(4)[:, 0:2 * NB], self.q_s[:, n, :],
                                    self.q_v[:, n, :, :].rearrange("p a b -> p (a b)"), start=(n == 0),
                                    stop=(n == 2 * NT - 1))
                ins.then_inc(self.s_tab.sem, 1)

            def route_act(self, act):
                for hf in range(2):
                    act.wait_ge(*self.s_lg(hf + 1))
                    act.activation(self.lgt[0:NG + E, hf * 512:(hf + 1) * 512], bank(4 + hf)[0:NG + E, :],
                                   ACT.Copy).then_inc(self.s_lt.sem, 1)
                act.wait_ge(*self.s_exd(1))
                act.activation(self.small[:, 4:8, :], self.small[:, 4:8, :], ACT.Exp).then_inc(self.s_ex.sem, 1)
                act.wait_ge(*self.s_exd(2))
                act.activation(self.small[:, 10, :], self.small[:, 10, :], ACT.Exp).then_inc(self.s_ex.sem, 1)

            def route_dve(self, dve):
                L = dve_chain.link
                sm, em, tmp = self.small, self.em, self.tmp
                dve.wait_ge(*self.s_io(7))
                dve.wait_ge(*self.s_lg(3))
                L(dve, dve.tensor_copy(self.lg[:].rearrange("p t c -> p (t c)"), bank(6)[:, 0:NT * (NG + E)]))
                gl = self.lg[:, :, 0:NG]
                el = self.lg[:, :, NG:NG + E]

                def bc(v, n):
                    return v.unsqueeze(2).to_broadcast([P, NT, n])

                def rowbc(v, n):
                    return v.unsqueeze(1).to_broadcast([P, NT, n])

                L(dve, dve.reduce_max(sm[:, 0, :], gl, AXX))
                g4 = tmp[:, 0, :, 0:NG]
                L(dve, dve.tensor_tensor(g4, gl, bc(sm[:, 0, :], NG), ALU.is_ge))
                L(dve, dve.tensor_tensor(g4, g4, rowbc(self.iog[:], NG), ALU.mult))
                L(dve, dve.reduce_max(sm[:, 1, :], g4, AXX))
                goh = tmp[:, 0, :, NG:2 * NG]
                L(dve, dve.tensor_tensor(goh, g4, bc(sm[:, 1, :], NG), ALU.is_equal))
                ge = sm[:, 4:8, :].rearrange("p g t -> p t g")
                dve.tensor_tensor(ge, gl, bc(sm[:, 0, :], NG), ALU.subtract).then_inc(self.s_exd.sem, 1)
                L(dve, dve.tensor_scalar(g4, goh, 1.0, -NEG, ALU.subtract, ALU.mult))
                for g in range(NG):
                    sl = slice(g * EG, (g + 1) * EG)
                    ins = dve.tensor_tensor(em[:, :, sl], el[:, :, sl], bc(goh[:, :, g], EG), ALU.mult)
                L(dve, ins)
                for g in range(NG):
                    sl = slice(g * EG, (g + 1) * EG)
                    ins = dve.tensor_tensor(em[:, :, sl], em[:, :, sl], bc(g4[:, :, g], EG), ALU.add)
                L(dve, ins)
                for k in range(2):
                    m, first, oh = sm[:, 2 + k, :], sm[:, 8 + k, :], self.oh[:, k]
                    L(dve, dve.reduce_max(m, em[:], AXX))
                    L(dve, dve.tensor_tensor(tmp[:, k], em[:], bc(m, E), ALU.is_ge))
                    L(dve, dve.tensor_tensor(tmp[:, k], tmp[:, k], rowbc(self.ioe[:], E), ALU.mult))
                    L(dve, dve.reduce_max(first, tmp[:, k], AXX))
                    L(dve, dve.tensor_tensor(oh, tmp[:, k], bc(first, E), ALU.is_equal))
                    if k == 0:
                        L(dve, dve.scalar_tensor_tensor(em[:].rearrange("p t e -> p (t e)"),
                                                        oh.rearrange("p t e -> p (t e)"), 2 * NEG,
                                                        em[:].rearrange("p t e -> p (t e)"), ALU.mult, ALU.add))
                dve.tensor_tensor(self.both[:], self.oh[:, 0], self.oh[:, 1], ALU.add).then_inc(self.s_A.sem, 1)
                dve.tensor_tensor(sm[:, 10, :], sm[:, 3, :], sm[:, 2, :], ALU.subtract).then_inc(self.s_exd.sem, 1)

                def pair(n):
                    return sm[:, n:n + 2, :].rearrange("p k t -> p (k t)")

                rank, exp_, ovs, fl, bk, t2 = (pair(n) for n in (12, 14, 16, 18, 20, 22))
                L(dve, dve.tensor_scalar(exp_, pair(8), -1.0, float(E), ALU.mult, ALU.add))
                dve.wait_ge(*self.s_ex(2))
                L(dve, dve.reduce_sum(sm[:, 11, :], ge, AXX))
                L(dve, dve.tensor_scalar(sm[:, 1, :], sm[:, 10, :], 1.0, None, ALU.add))
                L(dve, dve.tensor_tensor(sm[:, 11, :], sm[:, 11, :], sm[:, 1, :], ALU.mult))
                L(dve, dve.reciprocal(w_tok[:, 0:NT], sm[:, 11, :]))
                L(dve, dve.tensor_tensor(w_tok[:, NT:2 * NT], w_tok[:, 0:NT], sm[:, 10, :], ALU.mult))
                r = self.row
                dve.wait_ge(*self.s_rk(1))
                over = self.over[:]
                nj = T // P - 1
                L(dve, dve.tensor_copy(r[:, 0, :], bank(7)[:, 0:E]))
                L(dve, dve.tensor_tensor(over, r[:, 0, :].unsqueeze(2).to_broadcast([P, E, nj]),
                                         self.iot[:].unsqueeze(1).to_broadcast([P, E, nj]), ALU.is_gt))
                L(dve, dve.reduce_sum(r[:, 1, :], over, AXX))
                L(dve, dve.tensor_tensor_scan(r[:, 2, :], ones[:, 0:E], r[:, 1, :], 0.0, ALU.mult, ALU.add))
                L(dve, dve.tensor_tensor(r[:, 3, :], r[:, 2, :], r[:, 1, :], ALU.subtract))
                for out, src in ((rank, bank(5)[:, 0:NT * E].rearrange("p (t e) -> p t e", e=E)),
                                 (ovs, rowbc(r[:, 3, :], E))):
                    for k in range(2):
                        ins = dve.tensor_tensor(tmp[:, k], self.oh[:, k], src, ALU.mult)
                    L(dve, ins)
                    L(dve, dve.reduce_sum(out, tmp[:].rearrange("p k t e -> p (k t) e"), AXX))
                over = self.over[:, 0:2 * NT, :]
                L(dve, dve.tensor_tensor(over, rank.unsqueeze(2).to_broadcast([P, 2 * NT, nj]),
                                         self.iot[:].unsqueeze(1).to_broadcast([P, 2 * NT, nj]), ALU.is_ge))
                L(dve, dve.reduce_sum(fl, over, AXX))
                L(dve, dve.tensor_tensor(t2, ovs, fl, ALU.add))
                L(dve, dve.scalar_tensor_tensor(t2, t2, float(E - 1), exp_, ALU.add, ALU.subtract))
                L(dve, dve.scalar_tensor_tensor(t2, fl, 1.0, t2, ALU.min, ALU.mult))
                dve.scalar_tensor_tensor(rank, fl, -float(P), rank, ALU.mult, ALU.add)
                L(dve, dve.tensor_tensor(bk, exp_, t2, ALU.add))
                def over_n(v, n):
                    return v.unsqueeze(2).to_broadcast([P, 2 * NT, n])

                dve.tensor_tensor(self.q_s[:], self.ios[:].unsqueeze(1).to_broadcast([P, 2 * NT, P]),
                                  over_n(rank, P), ALU.is_equal)
                L(dve, dve.tensor_tensor(self.q_b[:], self.iob[:].unsqueeze(1).to_broadcast([P, 2 * NT, NB]),
                                         over_n(bk, NB), ALU.is_equal))
                dve.tensor_tensor(self.q_v[:, :, 0, :], self.q_b[:],
                                  over_n(self.base[:].rearrange("p k t -> p (k t)"), NB), ALU.mult)
                L(dve, dve.tensor_scalar(self.q_v[:, :, 1, :], self.q_b[:], self.part[:, 0:1], None, ALU.mult))
                dve.engine_nop().then_inc(self.s_q.sem, 1)
                L(dve, dve.tensor_tensor(self.ovc[:], r[:, 2, :].unsqueeze(1).to_broadcast([P, OVB, E]),
                                         self.iob[:, 0:OVB].unsqueeze(2).to_broadcast([P, OVB, E]), ALU.is_le))
                L(dve, dve.reduce_sum(self.ovf[:, 0:OVB], self.ovc[:], AXX))
                L(dve, dve.tensor_scalar(self.ovf[:, 0:OVB], self.ovf[:, 0:OVB], float(E - 1), None, ALU.min))
                L(dve, dve.tensor_copy(self.ovf[:, OVB:OVB + 1], r[:, 2, E - 1:E]))
                L(dve, dve.tensor_copy(ov_e[:], self.ovf[:]))
                dve.wait_ge(*self.s_tab(1))
                tab = [self.tab[:, n, :] for n in range(3)]
                L(dve, dve.tensor_scalar(tab[0], bank(4)[:, 0:NB], float(EMPTY), None, ALU.add))
                L(dve, dve.tensor_tensor(tab[1], tab[0], bank(4)[:, NB:2 * NB], ALU.add))
                dve.tensor_copy(idx_y[:], tab[1])
                L(dve, dve.tensor_scalar(tab[2], tab[1], float(T), -float(T), ALU.is_ge, ALU.mult))
                L(dve, dve.tensor_tensor(tab[2], tab[2], tab[1], ALU.add))
                dve.tensor_copy(idx_x[:], tab[2]).then_inc(self.s_rt.sem, 1)

            def unit(self, e, what, half):
                if what == "d":
                    e = e + 1
                    if isinstance(e, int) and e == E:
                        return 4 + 6 * (E - 1) + half
                if isinstance(e, int) and e == 0:
                    return {"g": 0, "u": 2}[what] + half
                return 4 + 6 * (e - 1) + {"g": 0, "d": 2, "u": 4}[what] + half

            def w_src(self, e, what, half):
                if what == "d":
                    w = A["w_down"][self.l].rearrange("e (p q) n -> e p (q n)", q=F // P)
                else:
                    w = A["w_gate" if what == "g" else "w_up"][self.l].rearrange("e (p k) n -> e p (k n)", k=KD)
                if isinstance(e, int):
                    return w[e, :, half * UNIT:(half + 1) * UNIT]
                return w[bass.ds(e, 1), :, half * UNIT:(half + 1) * UNIT].rearrange("a p c -> (a p) c")

            def load(self, sp, e, r, what, half):
                u, ur = self.unit(e, what, half), self.unit(r, what, half)
                g, gr = self.first + u, self.first + ur
                if isinstance(u, int):
                    stream.wait_free(sp, g)
                else:
                    sp.wait_ge(unit_dve, stream.owner[self.first][1] - 1 + u - RING + 1)
                sp.dma_start(ring[:, gr % RING, :], self.w_src(e, what, half)).then_inc(ring_full[gr % RING], 16)

            def full(self, eng, e, r, what, half):
                gr = self.first + self.unit(r, what, half)
                turns = gr // RING + 1
                if isinstance(e, int):
                    eng.wait_ge(ring_full[gr % RING], 16 * turns)
                else:
                    eng.wait_ge(ring_full[gr % RING], (e - r) * 16 + 16 * turns)

            def steps(self, e):
                if isinstance(e, int) and e == 0:
                    return [(e, "g"), (e, "u")]
                if isinstance(e, int) and e == E:
                    return [(e - 1, "d")]
                return [(e, "g"), (e - 1, "d"), (e, "u")]

            def sp(self, sp):
                self.over_loop(sp, lambda e, r: [self.load(sp, x, rx, w, hf)
                                                 for (x, w), (rx, _) in zip(self.steps(e), self.steps(r))
                                                 for hf in range(2)])

            def over_loop(self, eng, step):
                step(0, 0)
                step(1, 1)
                with eng.Fori(0, (E - 4) // 2) as i:
                    step(2 * i + 2, 2)
                    step(2 * i + 3, 3)
                step(E - 2, E - 2)
                step(E - 1, E - 1)
                step(E, E)

            def split(self, eng, e, r, what, half):
                u, ur = self.unit(e, what, half), self.unit(r, what, half)
                slot = ur % SPLIT
                src = ring[:, (self.first + ur) % RING, :]
                if eng is nc.scalar:
                    self.full(eng, e, r, what, half)
                    if not isinstance(u, int) or u >= SPLIT:
                        eng.wait_ge(*self.s_use(u - SPLIT + 1))
                    eng.activation(self.hi[:, slot, :], src, ACT.Copy).then_inc(self.s_hi.sem, 1)
                else:
                    eng.wait_ge(*self.s_hi(u + 1))
                    eng.tensor_tensor(self.lo[:, slot, :], src, self.hi[:, slot, :].bitcast(F32), ALU.subtract)\
                       .then_inc(unit_dve, 1)

            def unit_ready(self, pe, u):
                pe.wait_ge(unit_dve, stream.owner[self.first][1] + u)

            def x_transpose(self, pe, e, r):
                b = r % 2
                pe.wait_ge(*self.s_gx[b]((e // 2) * 16 + 16 if isinstance(e, int) else (e - r) * 8 + 16 * (r // 2 + 1)))
                if not isinstance(e, int) or e >= 1:
                    pe.wait_ge(*self.s_xl(e))
                for k in range(KD):
                    ins = pe.transpose(bank(0, 2)[:, k * P:(k + 1) * P], self.xg[:, b, k::KD], ident[:])
                ins.then_inc(self.s_xtr.sem, 1)

            def product(self, pe, out, xs, e, r, what, half, first, last):
                u, ur = self.unit(e, what, half), self.unit(r, what, half)
                self.unit_ready(pe, u)
                slot = ur % SPLIT
                n = UNIT // 512
                mats = []
                for q in range(n):
                    if what == "d":
                        row, col = q // 2, q % 2
                        k, o, st = 2 * half + row, out[:, col * 512:(col + 1) * 512], first and row == 0
                        en = last and row == 1
                    else:
                        k, o, st, en = 4 * half + q, out, first and q == 0, last and q == n - 1
                    mats.append((k, o, self.hi[:, slot, q * 512:(q + 1) * 512],
                                 self.lo[:, slot, q * 512:(q + 1) * 512], st, en))
                for k, o, wh_, wl_, st, en in mats:
                    xhk, xlk = xs(k)
                    pe.matmul(o, xhk, wh_, start=st, stop=False)
                    pe.matmul(o, xhk, wl_, start=False, stop=False)
                    ins = pe.matmul(o, xlk, wh_, start=False, stop=en)
                ins.then_inc(self.s_use.sem, 1)
                return ins

            def pe(self, pe):
                def xs(r):
                    return lambda k: (self.xh[:, r % 2, k * P:(k + 1) * P], self.xl[:, r % 2, k * P:(k + 1) * P])

                def hs(k):
                    return self.hh[:, k * P:(k + 1) * P], self.hl[:, k * P:(k + 1) * P]

                def step(e, r):
                    if r < E:
                        pe.wait_ge(*self.s_xl(e + 1))
                        if not isinstance(e, int) or e >= 1:
                            pe.wait_ge(*self.s_sg(e))
                        for half in range(2):
                            self.product(pe, bank(2), xs(r), e, r, "g", half, half == 0, half == 1)
                    if r >= 1:
                        pe.wait_ge(*self.s_hm(e))
                        for q in range(F // P):
                            ins = pe.transpose(bank(4)[:, q * P:(q + 1) * P], self.hm[:, q::F // P], ident[:])
                        ins.then_inc(self.s_htr.sem, 1)
                    if r + 1 < E:
                        self.x_transpose(pe, e + 1, r + 1)
                    if r >= 1:
                        pe.wait_ge(*self.s_hl(e))
                        if not isinstance(e, int) or e >= 2:
                            pe.wait_ge(*self.s_ya(e - 1))
                            pe.wait_ge(*self.s_yd(e - 1))
                        for half in range(2):
                            self.product(pe, bank(5, 2), hs, e - 1, r - 1, "d", half, half == 0, half == 1)
                    if r < E:
                        for half in range(2):
                            self.product(pe, bank(3), xs(r), e, r, "u", half, half == 0, half == 1)

                self.x_transpose(pe, 0, 0)
                self.over_loop(pe, step)

            def used(self, e, what):
                return self.unit(e, what, 1) + 1

            def act(self, act):
                def x_hi(e, r):
                    act.wait_ge(*self.s_xtr(e + 1))
                    if not isinstance(e, int) or e >= 2:
                        act.wait_ge(*self.s_use(self.used(e - 2, "u")))
                    act.activation(self.xh[:, r % 2, :], bank(0, 2), ACT.Copy).then_inc(self.s_xh.sem, 1)

                def step(e, r):
                    if r >= 1:
                        for half in range(2):
                            self.split(act, e - 1, r - 1, "d", half)
                    if r < E:
                        self.split(act, e, r, "u", 0)
                        act.wait_ge(*self.s_use(self.used(e, "g")))
                        if not isinstance(e, int) or e >= 1:
                            act.wait_ge(*self.s_hm(e))
                        act.activation(self.sg[:], bank(2), ACT.Silu).then_inc(self.s_sg.sem, 1)
                    if r >= 1:
                        act.wait_ge(*self.s_htr(e))
                        act.activation(self.hh[:], bank(4), ACT.Copy).then_inc(self.s_hh.sem, 1)
                    if r + 1 < E:
                        x_hi(e + 1, r + 1)
                    if r < E:
                        self.split(act, e, r, "u", 1)
                        if r + 1 < E:
                            for half in range(2):
                                self.split(act, e + 1, r + 1, "g", half)
                    if r >= 1:
                        act.wait_ge(*self.s_use(self.used(e - 1, "d")))
                        if not isinstance(e, int) or e >= 3:
                            act.wait_ge(*self.s_yst[(r - 1) % 2](self.stored(e - 3, r - 3)))
                        act.activation(self.y[:, (r - 1) % 2, 0:512], bank(5), ACT.Copy).then_inc(self.s_ya.sem, 1)

                act.wait_ge(*self.s_tab(1))
                for half in range(2):
                    self.split(act, 0, 0, "g", half)
                x_hi(0, 0)
                self.over_loop(act, step)

            def stored(self, e, r):
                if isinstance(e, int):
                    return 16 * (e // 2 + 1)
                return (e - r) * 8 + 16 * (r // 2 + 1)

            def dve(self, dve):
                def x_lo(e, r):
                    dve.wait_ge(*self.s_xh(e + 1))
                    dve.tensor_tensor(self.xl[:, r % 2, :], bank(0, 2), self.xh[:, r % 2, :].bitcast(F32),
                                      ALU.subtract).then_inc(self.s_xl.sem, 1)

                def step(e, r):
                    if r >= 1:
                        dve.wait_ge(*self.s_use(self.used(e - 1, "u")))
                        dve.wait_ge(*self.s_sg(e))
                        dve.tensor_tensor(self.hm[:], self.sg[:], bank(3), ALU.mult).then_inc(self.s_hm.sem, 1)
                        for half in range(2):
                            self.split(dve, e - 1, r - 1, "d", half)
                    if r < E:
                        self.split(dve, e, r, "u", 0)
                    if r >= 1:
                        dve.wait_ge(*self.s_hh(e))
                        dve.tensor_tensor(self.hl[:], bank(4), self.hh[:].bitcast(F32),
                                          ALU.subtract).then_inc(self.s_hl.sem, 1)
                    if r + 1 < E:
                        x_lo(e + 1, r + 1)
                    if r < E:
                        self.split(dve, e, r, "u", 1)
                        if r + 1 < E:
                            for half in range(2):
                                self.split(dve, e + 1, r + 1, "g", half)
                    if r >= 1:
                        dve.wait_ge(*self.s_use(self.used(e - 1, "d")))
                        if not isinstance(e, int) or e >= 3:
                            dve.wait_ge(*self.s_yst[(r - 1) % 2](self.stored(e - 3, r - 3)))
                        dve.tensor_copy(self.y[:, (r - 1) % 2, 512:1024], bank(6)).then_inc(self.s_yd.sem, 1)

                for half in range(2):
                    self.split(dve, 0, 0, "g", half)
                x_lo(0, 0)
                self.over_loop(dve, step)

            def gather(self, pool, idx, rows):
                return pool.indirect_dma_start(rows, None, xn_dram, bass.IndirectOffsetOnAxis(ap=idx, axis=0),
                                               bounds_check=T - 1, oob_is_err=False)

            def scatter(self, pool, idx, rows):
                return pool.indirect_dma_start(y_dram, bass.IndirectOffsetOnAxis(ap=idx, axis=0), rows, None,
                                               bounds_check=2 * T - 1, oob_is_err=False)

            def pool(self, pool):
                def gather(e):
                    self.gather(pool, idx_x[:, e:e + 1], self.xg[:, e % 2, :]).then_inc(self.s_gx[e % 2].sem, 16)

                def store(e):
                    pool.wait_ge(*self.s_ya(e + 1))
                    pool.wait_ge(*self.s_yd(e + 1))
                    self.scatter(pool, idx_y[:, e:e + 1], self.y[:, e % 2, :]).then_inc(self.s_yst[e % 2].sem, 16)

                pool.wait_ge(*self.s_xg(1))
                pool.wait_ge(*self.s_rt(1))
                for n in range(4):
                    pool.wait_ge(*self.norm.s_st[n](16 * (NT // 4)))
                gather(0)
                gather(1)
                for e in range(E):
                    if e + 2 < E:
                        pool.wait_ge(*self.s_xtr(e + 1))
                        gather(e + 2)
                    if e >= 1:
                        store(e - 1)
                store(E - 1)
                for b in range(2):
                    pool.wait_ge(*self.s_yst[b](16 * (E // 2)))

            def number(self, eng):
                eng.wait_ge(*self.s_rt(1))
                return eng.value_load(ov_e[0:1, OVB:OVB + 1], min_val=0, max_val=OVB)

            def beyond_sp(self, sp):
                sp.wait_ge(unit_dve, stream.owner[self.first + 6 * E - 1][1])
                n = self.number(sp)
                with sp.If(n > 0):
                    with sp.Fori(0, n) as j:
                        sp.wait_ge(*self.s_of(j + 1))
                        e = sp.value_load(ov_e[0:1, bass.ds(j, 1)], min_val=0, max_val=E - 1)
                        for m, (w, q) in enumerate((("w_gate", KD), ("w_up", KD), ("w_down", F // P))):
                            src = A[w][self.l].rearrange("e (p q) n -> e p (q n)", q=q)[bass.ds(e, 1)]
                            sp.dma_start(ring[:, 2 * m:2 * m + 2, :].rearrange("p a c -> p (a c)"),
                                         src.rearrange("a p c -> (a p) c")).then_inc(self.s_ow.sem, 16)
                sp.wait_ge(*self.s_odone(1))

            def beyond_pool(self, pool):
                def step(n):
                    n += 5 * self.l
                    return pool.tensor_tensor(fence[:, n:n + 1], ones[:, 0:1], ones[:, 0:1], ALU.add)

                step(0).then_inc(self.s_of.sem, 1)
                n = self.number(pool)
                with pool.If(n > 0):
                    with pool.Fori(0, n) as j:
                        pool.wait_ge(*self.s_of(j + 1))
                        pool.tensor_copy(self.ovi[:, 0:1], idx_x[:, bass.ds(j + E, 1)]).then_inc(self.s_oi.sem, 1)
                        pool.tensor_copy(self.ovi[:, 1:2], idx_y[:, bass.ds(j + E, 1)]).then_inc(self.s_oi.sem, 1)
                        pool.wait_ge(*self.s_oi(4 * j + 2))
                        step(1).then_inc(self.s_oi.sem, 1)
                        self.gather(pool, self.ovi[:, 0:1], self.xg[:, 0, :]).then_inc(self.s_ox.sem, 16)
                        pool.wait_ge(*self.s_oa(4 * j + 4))
                        step(4).then_inc(self.s_oi.sem, 1)
                        self.scatter(pool, self.ovi[:, 1:2], self.y[:, 0, :]).then_inc(self.s_oy.sem, 16)
                        pool.wait_ge(*self.s_oi(4 * j + 4))
                        pool.wait_ge(*self.s_oy(16 * j + 16))
                        step(2).then_inc(self.s_of.sem, 1)
                step(3).then_inc(self.s_odone.sem, 1)

            def beyond_pe(self, pe):
                n = self.number(pe)
                pe.wait_ge(*self.s_ya(E))
                pe.wait_ge(*self.s_yd(E))
                with pe.If(n > 0):
                    with pe.Fori(0, n) as j:
                        pe.wait_ge(*self.s_ox(16 * j + 16))
                        for k in range(KD):
                            ins = pe.transpose(bank(0, 2)[:, k * P:(k + 1) * P], self.xg[:, 0, k::KD], ident[:])
                        ins.then_inc(self.s_op.sem, 1)
                        pe.wait_ge(*self.s_oa(4 * j + 1))
                        pe.wait_ge(*self.s_ow(48 * j + 48))
                        for m in range(2):
                            for k in range(KD):
                                w = ring[:, 2 * m + k // 4, (k % 4) * 512:(k % 4 + 1) * 512]
                                ins = pe.matmul(bank(2 + m), self.xf[:, k * P:(k + 1) * P], w, start=(k == 0),
                                                stop=(k == KD - 1))
                        ins.then_inc(self.s_op.sem, 1)
                        pe.wait_ge(*self.s_od(j + 1))
                        for q in range(F // P):
                            ins = pe.transpose(bank(4)[:, q * P:(q + 1) * P], self.hm[:, q::F // P], ident[:])
                        ins.then_inc(self.s_op.sem, 1)
                        pe.wait_ge(*self.s_oa(4 * j + 3))
                        for c in range(2):
                            for q in range(F // P):
                                w = ring[:, 4 + q // 2, (q % 2) * D + c * 512:(q % 2) * D + (c + 1) * 512]
                                ins = pe.matmul(bank(5 + c), self.hf[:, q * P:(q + 1) * P], w, start=(q == 0),
                                                stop=(q == F // P - 1))
                        ins.then_inc(self.s_op.sem, 1)

            def beyond_act(self, act):
                n = self.number(act)
                with act.If(n > 0):
                    with act.Fori(0, n) as j:
                        act.wait_ge(*self.s_op(4 * j + 1))
                        act.activation(self.xf[:], bank(0, 2), ACT.Copy).then_inc(self.s_oa.sem, 1)
                        act.wait_ge(*self.s_op(4 * j + 2))
                        act.activation(self.sg[:], bank(2), ACT.Silu).then_inc(self.s_oa.sem, 1)
                        act.wait_ge(*self.s_op(4 * j + 3))
                        act.activation(self.hf[:], bank(4), ACT.Copy).then_inc(self.s_oa.sem, 1)
                        act.wait_ge(*self.s_op(4 * j + 4))
                        act.activation(self.y[:, 0, :], bank(5, 2), ACT.Copy).then_inc(self.s_oa.sem, 1)

            def beyond_dve(self, dve):
                n = self.number(dve)
                with dve.If(n > 0):
                    with dve.Fori(0, n) as j:
                        dve.wait_ge(*self.s_oa(4 * j + 2))
                        dve.tensor_tensor(self.hm[:], self.sg[:], bank(3), ALU.mult).then_inc(self.s_od.sem, 1)

            def combine_pool(self, pool, rows):
                both = y_dram.rearrange("(k t p) d -> t p k d", k=2, p=P)
                for t in range(NT):
                    if t >= ROWS:
                        pool.wait_ge(*self.s_comb(2 * (t - ROWS + 1)))
                    pool.dma_start(rows[:, t % ROWS, :, :], both[t]).then_inc(self.s_row[t % ROWS].sem, 16)

            def combine_dve(self, dve, rows, t):
                dve.wait_ge(*self.s_row[t % ROWS](16 * (t // ROWS + 1)))
                for k in range(2):
                    if k:
                        dve.wait_ge(*self.s_comb(2 * t + 1))
                    dve.scalar_tensor_tensor(h[:, t, :], rows[:, t % ROWS, k, :],
                                             w_tok[:, k * NT + t:k * NT + t + 1], h[:, t, :],
                                             ALU.mult, ALU.add).then_inc(self.s_comb.sem, 1)

        class Ple:

            def __init__(self, l, ready):
                a = Arena(f"p{l}")
                self.l = l
                self.proj = a("proj", [P, NT, D])
                xh, xl = a("xh", [P, 2, D], F32R), a("xl", [P, 2, D], F32R)
                hi = [a(f"hi{n}", [P, UNIT], F32R)[:] for n in range(2)]
                self.xn = a("xn", [P, 4, D])
                self.rows = a("rows", [P, ROWS, 2, D])
                self.pt = a("pt", [P, 2, T])
                self.sg = a("sg", [P, 2, 512])
                a.go(96)
                hi += [a(f"hi{n}", [P, UNIT], F32R)[:] for n in (2, 3)]
                self.s_p, self.s_pr, self.s_pro, self.s_sg, self.s_mul, self.s_add = (
                    count("ple_" + n, t) for n, t in (("p", 16), ("proj", 2 * NT), ("proj_out", 2 * NT),
                                                      ("sigmoid", 2 * NT), ("mul", 2 * NT), ("add", 2 * NT)))
                self.proj_units = stream.dense(2)
                self.g = TileProduct([A["w_ple_gate"][l, c] for c in range(2)], hi, xh, xl, self.s_sg,
                                     on_pool=(1, 3))
                self.norm = NormTranspose(A["norm_ple"][l:l + 1, :], None, self.xn, ready, product=self.g)

            def tile(self, t):
                return self.s_add(2 * t + 2)

            def sp(self, sp):
                load_unit(sp, self.proj_units, A["w_ple_proj"][self.l, 0], 2 * 512)
                sp.dma_start(self.pt[:], A["p_t"][self.l]).then_inc(self.s_p.sem, 16)
                load_unit(sp, self.proj_units + 1, A["w_ple_proj"][self.l, 1], 2 * 512)

            def sp_gate(self, sp):
                sp.wait_ge(*self.s_pr(NT))
                self.g.sp(sp)

            def pe_proj(self, pe, moe):
                pe.wait_ge(*moe.s_odone(1))
                pe.wait_ge(*self.s_p(16))
                for g in range(2 * NT):
                    t, c = divmod(g, 2)
                    if g < 2:
                        full(pe, self.proj_units + c)
                    if g >= 4:
                        pe.wait_ge(*self.s_pro(g - 3))
                    for k in range(2):
                        ins = pe.matmul(bank(g % 4), self.pt[:, k, t * P:(t + 1) * P],
                                        ring[:, (self.proj_units + c) % RING, k * 512:(k + 1) * 512],
                                        start=(k == 0), stop=(k == 1))
                    ins.then_inc(self.s_pr.sem, 1)
                pe.wait_ge(*self.s_pr(2 * NT))
                pe.nop().then_inc(unit_pe, 2)

            def act_proj(self, act, t):
                for c in range(2):
                    g = 2 * t + c
                    act.wait_ge(*self.s_pr(g + 1))
                    act.activation(self.proj[:, t, c * 512:(c + 1) * 512], bank(g % 4), ACT.Copy)\
                       .then_inc(self.s_pro.sem, 1)

            def pe(self, pe):
                pe.wait_ge(*self.s_pro(2 * NT))
                self.norm.transposes(pe, 0)
                for t in range(NT):
                    if t + 1 < NT:
                        self.norm.transposes(pe, t + 1)
                    self.g.pe(pe, t)

            def split_act(self, act):
                for n in range(4):
                    self.g.w_hi(act, n)

            def split_dve(self, dve):
                for n in (0, 2):
                    self.g.w_lo(dve, n)

            def split_pool(self, pool):
                for n in self.g.on_pool:
                    self.g.w_lo(pool, n)

            def act(self, act, t):
                for c in range(2):
                    g = 2 * t + c
                    act.wait_ge(*self.g.s_mm(g + 1))
                    if g >= 2:
                        act.wait_ge(*self.s_add(g - 1))
                    act.activation(self.sg[:, c, :], bank(4 + c), ACT.Sigmoid).then_inc(self.s_sg.sem, 1)
                if t + 2 < NT:
                    self.norm.out_act(act, t + 2)

            def dve(self, dve, t):
                for c in range(2):
                    g = 2 * t + c
                    hs = h[:, t, c * 512:(c + 1) * 512]
                    dve.wait_ge(*self.s_sg(g + 1))
                    dve.tensor_tensor(self.sg[:, c, :], self.sg[:, c, :], self.proj[:, t, c * 512:(c + 1) * 512],
                                      ALU.mult).then_inc(self.s_mul.sem, 1)
                    dve.wait_ge(*self.s_mul(g + 1))
                    dve.tensor_tensor(hs, hs, self.sg[:, c, :], ALU.add).then_inc(self.s_add.sem, 1)
                self.norm.tile_dve(dve, t)

        class SpatialGate:

            SETS = (4, 0, 4, 0, 0, 0, 0, 4)

            def __init__(self, ready):
                a = Arena("mix1")
                self.xh = a("xh", [P, KD, 512], F32R)
                self.xl = a("xl", [P, KD, 512], F32R)
                self.ut = a("ut", [P, KD, T])
                self.v = a("v", [P, NT, SG])
                self.hi = a("hi", [P, 2, UNIT], F32R)
                self.ws = a("ws", [P, SGG, P])
                self.tmp = a("tmp", [P, 512])
                self.ssv = a("ssv", [P, 2, NT])
                self.bs = gain.rearrange("p (g t) -> p g t", g=SGG)
                self.s_xh, self.s_xl = count("gmlp_x_hi", NT), count("gmlp_x_lo", NT)
                self.norm = NormTranspose(A["norm_mix"][1:2, :], None, self.v, ready, product=self)
                self.norm.second = 4
                self.first = stream.dense(16)
                (self.s_ws, self.s_bs, self.s_mask, self.s_wh, self.s_wl, self.s_wu, self.s_grp, self.s_gv, self.s_ev,
                 self.s_mean, self.s_root, self.s_vs, self.s_s, self.s_t, self.s_y) = (
                    Count(sem("gmlp_" + n), 0) for n in
                    ("ws", "bs", "mask", "w_hi", "w_lo", "unit", "group", "gelu_v", "group_out",
                     "mean", "root", "v_normed", "s", "tmp", "y"))

            def slot(self, n):
                return (self.first + n) % RING

            def sp(self, sp):
                for n in range(16):
                    load_unit(sp, self.first + n, A["w_in_o"][n % 8 // 2][:, n % 2 * UNIT:(n % 2 + 1) * UNIT], UNIT)
                    if n == 7:
                        sp.wait_ge(*self.norm.ready(NT - 1))
                        sp.dma_start(self.ws[:], A["w_s_t"]).then_inc(self.s_ws.sem, 16)
                        sp.wait_ge(*self.norm.s_xn(NT))
                        sp.dma_start(gain[:], A["b_s"].partition_broadcast(P)).then_inc(self.s_bs.sem, 16)

            def pool(self, pool):
                pool.wait_ge(*self.s_ws(16))
                pool.affine_select(out=self.ws[:], in_=self.ws[:], compare_op=ALU.is_ge, fill=0.0, base=0,
                                   pattern=[[0, SGG], [1, P]], channel_multiplier=-1).then_inc(self.s_mask.sem, 1)

            def x_part(self, x, t):
                return x[:, :, t % 4 * P:(t % 4 + 1) * P]

            def x_hi(self, act, t, src):
                act.activation(self.x_part(self.xh, t), src.rearrange("p (k c) -> p k c", c=P), ACT.Copy)\
                   .then_inc(self.s_xh.sem, 1)

            def x_lo(self, dve, t, src):
                dve.wait_ge(*self.s_xh(t + 1))
                dve.tensor_tensor(self.x_part(self.xl, t), src.rearrange("p (k c) -> p k c", c=P),
                                  self.x_part(self.xh, t).bitcast(F32), ALU.subtract).then_inc(self.s_xl.sem, 1)

            def w_hi(self, act, n):
                full(act, self.first + n)
                if n >= 2:
                    act.wait_ge(*self.used(n - 2))
                act.activation(self.hi[:, n % 2, :], ring[:, self.slot(n), :], ACT.Copy).then_inc(self.s_wh.sem, 1)

            def w_lo(self, dve, n):
                dve.wait_ge(*self.s_wh(n + 1))
                dve.tensor_tensor(ring_lo[:, self.slot(n), :], ring[:, self.slot(n), :],
                                  self.hi[:, n % 2, :].bitcast(F32), ALU.subtract).then_inc(self.s_wl.sem, 1)

            def unit(self, pe, n):
                panel, second = divmod(n, 2)
                free = {0: self.norm.s_ss(NT), 1: self.s_xl(4), 2: self.s_ev(4), 3: self.s_ev(8), 4: self.s_ev(16),
                        5: self.s_ev(20), 6: self.s_ev(24), 7: self.s_t(SGG)}[panel]
                if not second:
                    pe.wait_ge(*free)
                pe.wait_ge(*self.s_wl(n + 1))
                for j in range(4):
                    for q in range(4):
                        k = 4 * second + q
                        if panel % 4 < 2:
                            ws = slice(q * 512 + j * P, q * 512 + (j + 1) * P)
                            w_hi, w_lo = self.hi[:, n % 2, ws], ring_lo[:, self.slot(n), ws]
                            x_hi, x_lo = self.xh[:, k, :], self.xl[:, k, :]
                            passes = ((w_hi, x_hi), (w_hi, x_lo), (w_lo, x_hi))
                        else:
                            ws = slice(q * 512, (q + 1) * 512)
                            w_hi, w_lo = self.hi[:, n % 2, ws], ring_lo[:, self.slot(n), ws]
                            x_hi, x_lo = (x[:, k, j * P:(j + 1) * P] for x in (self.xh, self.xl))
                            passes = ((x_hi, w_hi), (x_hi, w_lo), (x_lo, w_hi))
                        for m, (stay, move) in enumerate(passes):
                            ins = pe.matmul(bank(self.SETS[panel] + j), stay, move, start=(k == 0 and m == 0),
                                            stop=(k == KD - 1 and m == 2))
                    if second:
                        ins.then_inc(self.s_grp.sem, 1)
                    elif j == 3:
                        ins.then_inc(self.s_wu.sem, 1)
                    if j == 0 and n:
                        pe.wait_ge(*self.used(n - 1))
                        pe.nop().then_inc(unit_pe, 1)

            def used(self, n):
                return self.s_grp(4 * (n // 2) + 4) if n % 2 else self.s_wu(n // 2 + 1)

            def s_bank(self, m):
                return (4 + m % 4) if m < 8 else m - 8

            def gate(self, pe, m):
                hf, g = divmod(m, SGG)
                if m % 8 == 0:
                    pe.wait_ge(*self.s_mask(1))
                    pe.wait_ge(*self.s_vs(4 * hf + 4))
                    pe.wait_ge(*(self.s_ev(32) if hf else self.s_xl(NT)))
                if 4 <= m < 8:
                    pe.wait_ge(*self.s_t(m - 3))
                for t in range(4):
                    ins = pe.matmul(bank(self.s_bank(m))[:, t * P:(t + 1) * P],
                                    self.v[:, 4 * hf + t, g * P:(g + 1) * P], self.ws[:, g, :],
                                    start=True, stop=True)
                ins.then_inc(self.s_s.sem, 1)

            def pe(self, pe):
                for t in range(4):
                    self.norm.transposes(pe, t)
                pe.wait_ge(*self.s_xl(4))
                for n in range(16):
                    if n == 8:
                        pe.wait_ge(*self.s_ev(12))
                        for t in range(4, NT):
                            self.norm.transposes(pe, t)
                        pe.wait_ge(*self.s_xl(NT))
                    if n in (10, 12):
                        for m in range(2 * n - 20, 2 * n - 16):
                            self.gate(pe, m)
                    self.unit(pe, n)
                pe.wait_ge(*self.used(15))
                pe.nop().then_inc(unit_pe, 1)
                for m in range(SGG, 2 * SGG):
                    self.gate(pe, m)

            def panel_out(self, act, panel):
                hf, c = divmod(panel, 4)
                for j in range(4):
                    act.wait_ge(*self.s_grp(4 * panel + j + 1))
                    src = bank(self.SETS[panel] + j)
                    if c < 2:
                        act.activation(self.ut[:, 4 * c + j, hf * 512:(hf + 1) * 512], src,
                                       ACT.Gelu_apprx_tanh).then_inc(self.s_ev.sem, 1)
                    else:
                        t, n = 4 * hf + j, 8 * hf + 4 * (c - 2) + j
                        v = self.v[:, t, (c - 2) * 512:(c - 1) * 512]
                        act.activation(v, src, ACT.Gelu_apprx_tanh).then_inc(self.s_gv.sem, 1)
                        act.wait_ge(*self.s_gv(n + 1))
                        act.activation(src, v, ACT.Square, accum_out=self.ssv[:, c - 2, t:t + 1])\
                           .then_inc(self.s_ev.sem, 1)

            def root(self, act, hf):
                act.wait_ge(*self.s_mean(hf + 1))
                act.activation(rstd[:, 4 * hf:4 * hf + 4], rstd[:, 4 * hf:4 * hf + 4], ACT.Sqrt)\
                   .then_inc(self.s_root.sem, 1)

            def act(self, act):
                self.w_hi(act, 0)
                self.norm.out_act(act, 2)
                self.norm.out_act(act, 3)
                self.w_hi(act, 1)
                for n in range(1, 16):
                    if n == 8:
                        self.panel_out(act, 3)
                        for t in range(4, NT):
                            self.norm.out_act(act, t)
                    if n + 1 < 16:
                        self.w_hi(act, n + 1)
                    if n % 2 == 0 and n != 8:
                        self.panel_out(act, n // 2 - 1)
                    if n == 8:
                        self.root(act, 0)
                    if n >= 14:
                        act.wait_ge(*self.s_s(SGG))
                        out1.g.w_hi(act, n - 14)
                self.panel_out(act, 7)
                self.root(act, 1)
                for n in range(2, 4):
                    out1.g.w_hi(act, n)
                act.wait_ge(*self.s_y(16))
                for t in range(2):
                    out1.g.x_hi(act, t, out1.x(t))

            def v_norm(self, dve, hf):
                four = slice(4 * hf, 4 * hf + 4)
                dve.wait_ge(*self.s_ev(16 * hf + 16))
                dve_chain.link(dve, dve.tensor_tensor(rstd[:, four], self.ssv[:, 0, four], self.ssv[:, 1, four], ALU.add))
                dve.tensor_scalar(rstd[:, four], rstd[:, four], 1.0 / SG, EPS, ALU.mult, ALU.add)\
                   .then_inc(self.s_mean.sem, 1)
                dve.wait_ge(*self.s_root(hf + 1))
                dve_chain.link(dve, dve.reciprocal(rstd[:, four], rstd[:, four]))
                for t in range(4 * hf, 4 * hf + 4):
                    dve.tensor_scalar(self.v[:, t, :], self.v[:, t, :], rstd[:, t:t + 1], None, ALU.mult)\
                       .then_inc(self.s_vs.sem, 1)

            def y(self, dve, m):
                hf, g = divmod(m, SGG)
                uts = self.ut[:, g, hf * 512:(hf + 1) * 512]
                if m:
                    dve.wait_ge(*self.s_y(m))
                dve.wait_ge(*self.s_s(m + 1))
                dve.scalar_tensor_tensor(self.tmp[:].rearrange("p (t c) -> p t c", c=P),
                                         bank(self.s_bank(m)).rearrange("p (t c) -> p t c", c=P),
                                         cols[:, C_VN + g:C_VN + g + 1],
                                         self.bs[:, g, :].unsqueeze(1).to_broadcast([P, 4, P]),
                                         ALU.mult, ALU.add).then_inc(self.s_t.sem, 1)
                dve.wait_ge(*self.s_t(m + 1))
                dve.tensor_tensor(uts, uts, self.tmp[:], ALU.mult).then_inc(self.s_y.sem, 1)

            def dve(self, dve):
                self.w_lo(dve, 0)
                for t in (2, 3):
                    self.norm.scale(dve, t + 3)
                    self.norm.out_dve(dve, t)
                self.norm.scale(dve, 7)
                self.w_lo(dve, 1)
                for n in range(1, 16):
                    if n == 8:
                        for t in range(4, NT):
                            self.norm.out_dve(dve, t)
                    if n + 1 < 16:
                        self.w_lo(dve, n + 1)
                    if n == 8:
                        self.v_norm(dve, 0)
                        dve.wait_ge(*self.s_bs(16))
                    if n in (10, 12):
                        for m in range(2 * n - 20, 2 * n - 16):
                            self.y(dve, m)
                    if n >= 14:
                        out1.g.w_lo(dve, n - 14)
                self.v_norm(dve, 1)
                for m in range(SGG, 2 * SGG):
                    self.y(dve, m)
                    if m in (9, 12):
                        out1.g.w_lo(dve, m // 3 - 1)
                for t in range(2):
                    out1.g.x_lo(dve, t, out1.x(t))

        class Final:
            def __init__(self, ready):
                self.ready, self.prior = ready, NormTranspose.prior
                self.s_g, self.s_ss, self.s_mean, self.s_root, self.s_o, self.s_out = (
                    Count(sem("final_" + n), 0) for n in ("gain", "squares", "mean", "root", "o", "out"))

            def sp(self, sp):
                sp.wait_ge(*self.prior.s_xn(NT))
                sp.dma_start(gain[:], A["final_norm"].partition_broadcast(P)).then_inc(self.s_g.sem, 16)
                for t in range(NT):
                    sp.wait_ge(*self.s_o(t + 1))
                    sp.dma_start(out[t * P:(t + 1) * P, :], h[:, t, :]).then_inc(self.s_out.sem, 16)
                sp.wait_ge(*self.s_out(16 * NT))

            def act(self, act, last):
                def square(t):
                    act.wait_ge(*self.ready(t))
                    if t:
                        act.wait_ge(*self.s_ss(t))
                    act.activation(bank(6, 2), h[:, t, :], ACT.Square, accum_out=ss[:, t:t + 1])\
                       .then_inc(self.s_ss.sem, 1)

                def root(n):
                    act.wait_ge(*self.s_mean(n + 1))
                    act.activation(rstd[:, 4 * n:4 * n + 4], rstd[:, 4 * n:4 * n + 4], ACT.Sqrt)\
                       .then_inc(self.s_root.sem, 1)

                for t in range(NT):
                    last(t)
                    if t >= 1:
                        square(t - 1)
                    if t == 5:
                        root(0)
                square(NT - 1)
                root(1)

            def dve(self, dve, last):
                def mean(n):
                    dve.wait_ge(*self.s_ss(4 * n + 4))
                    dve.tensor_scalar(rstd[:, 4 * n:4 * n + 4], ss[:, 4 * n:4 * n + 4], 1.0 / D, EPS,
                                      ALU.mult, ALU.add).then_inc(self.s_mean.sem, 1)

                def scale(n):
                    dve.wait_ge(*self.s_root(n // 4 + 1))
                    if n % 4 == 0:
                        dve_chain.link(dve, dve.reciprocal(rstd[:, n:n + 4], rstd[:, n:n + 4]))
                    dve.scalar_tensor_tensor(h[:, n, :], h[:, n, :], rstd[:, n:n + 1], gain[:],
                                             ALU.mult, ALU.mult).then_inc(self.s_o.sem, 1)

                for t in range(5):
                    last(t)
                mean(0)
                last(5)
                dve.wait_ge(*self.s_g(16))
                scale(0)
                scale(1)
                last(6)
                scale(2)
                scale(3)
                last(7)
                mean(1)
                for t in range(4, NT):
                    scale(t)

        moe0 = Moe(0, out0.tile)
        ple0 = Ple(0, moe0.tile)
        gate1 = SpatialGate(ple0.tile)
        out1 = OutProj("out1", gate1.ut, A["w_out_o"], (64, 72, 16, 24))
        moe1 = Moe(1, out1.tile)
        ple1 = Ple(1, moe1.tile)
        final = Final(ple1.tile)

        block = ctx.enter_context(nc.Block())

        @block.sync
        def _(sp):
            setup_sp(sp)
            norm0.sp(sp)
            in_sp(sp)
            att_sp(sp)
            out0.g.sp(sp)
            for moe, ple in ((moe0, ple0), (moe1, ple1)):
                moe.norm.sp(sp)
                moe.route_sp(sp)
                moe.norm.sp_store(sp)
                ple.norm.sp(sp)
                moe.sp(sp)
                moe.beyond_sp(sp)
                ple.sp(sp)
                ple.sp_gate(sp)
                if moe is moe0:
                    gate1.norm.sp(sp)
                    gate1.sp(sp)
                    out1.g.sp(sp)
                    sp.wait_ge(*gate1.s_y(16))
            final.sp(sp)

        @block.gpsimd
        def _(pool):
            setup_pool(pool)
            for moe, ple in ((moe0, ple0), (moe1, ple1)):
                moe.iotas(pool)
                moe.pool(pool)
                moe.beyond_pool(pool)
                moe.combine_pool(pool, ple.rows)
                ple.split_pool(pool)
                if moe is moe0:
                    gate1.pool(pool)

        @block.scalar
        def _(act):
            norm0.act(act)
            in_act(act)
            values_out(act, lambda o, x: act.activation(o, x, ACT.Copy), 0, s_va)
            att_act(act)
            out0_act(act)
            for moe, ple, out_proj in ((moe0, ple0, out0), (moe1, ple1, out1)):
                moe.norm.act(act, lambda t: out_proj.act(act, t))
                moe.route_act(act)
                moe.act(act)
                moe.beyond_act(act)
                ple.norm.act(act, lambda t: ple.act_proj(act, t))
                ple.split_act(act)
                if moe is moe0:
                    gate1.norm.act(act, lambda t: ple.act(act, t))
                    gate1.act(act)
                else:
                    final.act(act, lambda t: ple.act(act, t))

        @block.vector
        def _(dve):
            norm0.dve(dve)
            in_dve(dve)
            values_out(dve, dve.tensor_copy, 1, s_vd)
            att_dve(dve)
            out0_dve(dve)
            for moe, ple, out_proj in ((moe0, ple0, out0), (moe1, ple1, out1)):
                moe.norm.dve(dve, lambda t: out_proj.dve(dve, t))
                moe.route_dve(dve)
                moe.dve(dve)
                moe.beyond_dve(dve)
                ple.norm.dve(dve, lambda t: moe.combine_dve(dve, ple.rows, t))
                ple.split_dve(dve)
                if moe is moe0:
                    gate1.norm.dve(dve, lambda t: ple.dve(dve, t))
                    gate1.dve(dve)
                else:
                    final.dve(dve, lambda t: ple.dve(dve, t))

        @block.tensor
        def _(pe):
            for s, v in CONSTS:
                pe.wait_ge(s, v)
            norm0.pe(pe)
            in_pe(pe)
            values_pe(pe)
            att_pe(pe)
            for t in range(2):
                yt_pe(pe, t)
            out0.pe(pe)
            for moe, ple in ((moe0, ple0), (moe1, ple1)):
                moe.norm.pe(pe)
                moe.route_pe(pe)
                moe.pe(pe)
                moe.beyond_pe(pe)
                ple.pe_proj(pe, moe)
                ple.pe(pe)
                if moe is moe0:
                    gate1.pe(pe)
                    out1.pe(pe)


def _panels(w, width):
    k = w.shape[0] // P
    return np.ascontiguousarray(w.reshape(k, P, -1, width).transpose(2, 1, 0, 3).reshape(-1, P, k * width))


def _layout(x, p, positions, norm_mix, norm_ffn, w_in_e, conv_w, q_norm, w_q_up, kv_norm, w_kv_up, w_out_e,
            w_in_o, v_norm, w_s, b_s, w_out_o, w_router_group, w_router_expert, w_gate, w_up, w_down,
            norm_ple, w_ple_gate, w_ple_proj, final_norm):
    w_in = w_in_e[0]
    conv = w_in[:, :3 * CONV].reshape(D, 3, 4, P).transpose(0, 2, 1, 3).reshape(D, 4 * 3 * P)
    half = ROPE // 2
    inv = (1.0 / (10000.0 ** (np.arange(0, ROPE, 2, dtype=np.float32) / np.float32(ROPE)))).astype(np.float32)
    rope = np.zeros((P, 2), np.float32)
    rope[64:96, 0] = np.concatenate([inv, inv])
    rope[64:96, 1] = np.concatenate([-np.ones(half), np.ones(half)])
    col = lambda v: v.reshape(-1, P).T
    cols = np.concatenate([col(q_norm[0]), col(kv_norm[0]), col(v_norm[0]),
                           conv_w[0].reshape(3, 4, P).transpose(2, 1, 0).reshape(P, 12), rope], axis=1)
    wq = w_q_up[0].reshape(3, P, H, DQK).transpose(2, 1, 0, 3).reshape(H, P, 3 * DQK)
    w_kv = w_kv_up[0].reshape(2, P, H, NOPE + VD)
    wk = w_kv[..., :NOPE].transpose(2, 1, 0, 3).reshape(H, P, 2 * NOPE)
    wv = w_kv[..., NOPE:].transpose(1, 0, 2, 3).reshape(P, 2 * H * VD)
    router = np.concatenate([w_router_group, w_router_expert], axis=2)
    return {
        "x": x[0], "cols": cols, "positions": positions,
        "norm_mix": norm_mix, "norm_ffn": norm_ffn, "norm_ple": norm_ple, "final_norm": final_norm[None],
        "w_in_e": _panels(np.concatenate([conv, w_in[:, 3 * CONV:3 * CONV + QR]], axis=1), 3 * P),
        "w_in_kv": _panels(w_in[:, 3 * CONV + QR:], KVR + ROPE)[0],
        "w_heads": np.concatenate([wq, wk], axis=2), "w_v": wv,
        "w_out_e": _panels(w_out_e[0], 512), "w_in_o": _panels(w_in_o[0], 512), "w_out_o": _panels(w_out_o[0], 512),
        "w_s_t": w_s[0].transpose(2, 0, 1), "b_s": b_s[0].reshape(1, SGG * P),
        "w_router": router.reshape(DEPTH, KD, P, NG + E).transpose(0, 2, 1, 3),
        "w_gate": w_gate, "w_up": w_up, "w_down": w_down,
        "w_ple_gate": np.stack([_panels(w, 512) for w in w_ple_gate]),
        "w_ple_proj": np.stack([_panels(w, 512) for w in w_ple_proj]),
        "p_t": p[:, 0].reshape(DEPTH, T, 2, P).transpose(0, 3, 2, 1),
    }


def kernel(**inputs):
    import concourse.bacc as _bacc
    from concourse.bass_utils import run_bass_kernel_spmd as _run

    nc = _bacc.Bacc("TRN2", target_bir_lowering=False, num_devices=1)
    arrays = {n: np.ascontiguousarray(a) for n, a in _layout(**{k: np.asarray(v) for k, v in inputs.items()}).items()}
    aps = {n: nc.dram_tensor(n, a.shape, mybir.dt.from_np(a.dtype), kind="ExternalInput").ap()
           for n, a in arrays.items()}
    out = nc.dram_tensor("out_0", (T, D), F32, kind="ExternalOutput").ap()
    program(nc, aps, out)
    r = _run(nc, [arrays], core_ids=[0])
    return r.results[0]["out_0"].reshape(1, T, D)
```
